# Optimizing a Trainium2 kernel written in Bass

```python
import math
import jax, jax.numpy as jnp
from jax import lax
import numpy as np

D_MODEL = 1024
BATCH = 1
SEQ = 256
DEPTH = 2
DEC_BATCH = 8
DEC_SEQ = 8
PAST_LEN = 2048
PAGE_SIZE = 128

D_A = D_MODEL // 2
H_A = 4
HD_A = D_A // H_A
CHUNK = 128
D_B = D_MODEL // 2
H_B = 8
BH_B = D_B // H_B
CONV_W = 4
LRU_C = 8.0
D_C = D_MODEL // 2
HG_C = 16
G_C = D_C // HG_C
P_STATE = 64
N_BRANCH = 3
D_BR = D_MODEL // 2
IN_COLS = 2 * D_A + 2 * D_B + D_C + N_BRANCH * D_MODEL
D_FF = 11 * D_MODEL // 4
N_EXPERTS = 8
TOP_K = 2
D_EXP = D_FF // 2
N_DENSE = (DEPTH + 1) // 2
N_MOE = DEPTH // 2
EPS = 1e-6

kernel_name = 'hybrid_gmlp_rglru_s5_decoder_step'

F32 = jnp.float32

def _rmsnorm(x, g):
    x32 = x.astype(F32)
    y = x32 * lax.rsqrt(jnp.mean(x32 * x32, axis=-1, keepdims=True) + EPS)
    return (y * g.astype(F32)).astype(x.dtype)

def _layernorm(x, g, b):
    x32 = x.astype(F32)
    xc = x32 - jnp.mean(x32, axis=-1, keepdims=True)
    var = jnp.mean(xc * xc, axis=-1, keepdims=True)
    return (xc * lax.rsqrt(var + EPS) * g.astype(F32) + b.astype(F32)).astype(x.dtype)

def _linear_combine(left, right):
    a1, b1 = left
    a2, b2 = right
    return a1 * a2, a2 * b1 + b2

def _chunk_spatial_gate(v, ws, bs):
    n, t, _ = v.shape
    t_pad = -(-t // CHUNK) * CHUNK
    vp = jnp.pad(v, ((0, 0), (0, t_pad - t), (0, 0))).reshape(n, t_pad // CHUNK, CHUNK, H_A, HD_A)
    causal = jnp.tril(jnp.ones((CHUNK, CHUNK), dtype=bool))
    wm = jnp.where(causal[None], ws, jnp.zeros_like(ws))
    mixed = jnp.einsum('hts,ncshd->ncthd', wm, vp) + bs.T[:, :, None]
    return mixed.reshape(n, t_pad, D_A)[:, :t]

def _causal_dwconv(x, buf, w, b):
    t = x.shape[1]
    xp = jnp.concatenate([buf.astype(x.dtype), x], axis=1)
    y = b + xp[:, 0:t] * w[0]
    for k in range(1, CONV_W):
        y = y + xp[:, k:k + t] * w[k]
    return y, xp[:, t:]

def _rg_lru(xc, h0, wa, ba, wx, bx, lam):
    n, t, _ = xc.shape
    xh = xc.reshape(n, t, H_B, BH_B)
    r = jax.nn.sigmoid(jnp.einsum('nthi,hij->nthj', xh, wa).reshape(n, t, D_B) + ba).astype(F32)
    i = jax.nn.sigmoid(jnp.einsum('nthi,hij->nthj', xh, wx).reshape(n, t, D_B) + bx)
    log_a = -LRU_C * r * jax.nn.softplus(-lam.astype(F32))
    a = jnp.exp(log_a)
    drive = jnp.sqrt(-jnp.expm1(2.0 * log_a)) * (i * xc).astype(F32)
    drive = drive.at[:, 0].add(a[:, 0] * h0.astype(F32))
    _, hs = lax.associative_scan(_linear_combine, (a, drive), axis=1)
    return hs, hs[:, -1]

def _s5(u, h0_re, h0_im, lam_re, lam_im, log_dt, b_re, b_im, c_re, c_im, d):
    n, t, _ = u.shape
    lam = lax.complex(lam_re.astype(F32), lam_im.astype(F32))
    dt = jnp.exp(log_dt.astype(F32))[:, None]
    a_bar = jnp.exp(lam * dt)
    b_bar = ((a_bar - 1.0) / lam)[:, :, None] * lax.complex(b_re.astype(F32), b_im.astype(F32))
    c_mat = lax.complex(c_re.astype(F32), c_im.astype(F32))
    ug = u.astype(F32).reshape(n, t, G_C, HG_C).astype(jnp.complex64)
    bu = jnp.einsum('gph,ntgh->ntgp', b_bar, ug)
    bu = bu.at[:, 0].add(a_bar * lax.complex(h0_re.astype(F32), h0_im.astype(F32)))
    a_seq = jnp.broadcast_to(a_bar, bu.shape)
    _, xs = lax.associative_scan(_linear_combine, (a_seq, bu), axis=1)
    y = jnp.einsum('ghp,ntgp->ntgh', c_mat, xs).real.reshape(n, t, D_C)
    y = y + d.astype(F32) * u.astype(F32)
    last = xs[:, -1]
    return y.astype(u.dtype), jnp.real(last), jnp.imag(last)

def _mixer(h, conv_buf, lru_h, s5_re, s5_im, w_in, b_gate, a_ln_g, a_ln_b, a_ws, a_bs,
           b_conv_w, b_conv_b, b_wa, b_ba, b_wx, b_bx, b_lam, c_lam_re, c_lam_im, c_log_dt,
           c_b_re, c_b_im, c_c_re, c_c_im, c_d, c_glu_w, c_glu_b, w_branch, w_out):
    n, t, _ = h.shape
    proj = h @ w_in
    o1 = D_A
    o2 = o1 + D_A
    o3 = o2 + D_B
    o4 = o3 + D_B
    o5 = o4 + D_C
    ua, va, xb, gb, uc, gl = jnp.split(proj, [o1, o2, o3, o4, o5], axis=-1)
    va = _layernorm(jax.nn.gelu(va), a_ln_g, a_ln_b)
    ya = jax.nn.gelu(ua) * _chunk_spatial_gate(va, a_ws, a_bs)
    xc, conv_new = _causal_dwconv(xb, conv_buf, b_conv_w, b_conv_b)
    hs, h_last = _rg_lru(xc, lru_h, b_wa, b_ba, b_wx, b_bx, b_lam)
    yb = hs.astype(h.dtype) * jax.nn.gelu(gb)
    ys, s_re, s_im = _s5(uc, s5_re, s5_im, c_lam_re, c_lam_im, c_log_dt, c_b_re, c_b_im,
                         c_c_re, c_c_im, c_d)
    z = jax.nn.gelu(ys)
    yc = z * jax.nn.sigmoid(z @ c_glu_w + c_glu_b)
    br = jnp.stack([ya, yb, yc], axis=2)
    p = jnp.einsum('ntkc,kcd->ntkd', br, w_branch)
    g = jax.nn.sigmoid(gl + b_gate).reshape(n, t, N_BRANCH, D_MODEL)
    out = jnp.sum(g * p, axis=2) @ w_out
    return out, va, conv_new, h_last, s_re, s_im

def _swiglu(h, wg, wu, wd):
    return (jax.nn.silu(h @ wg) * (h @ wu)) @ wd

def _moe(h, rw, rb, wg, wu, wd):
    logits = (h @ rw + rb).astype(F32)
    top_v, top_i = lax.top_k(logits, TOP_K)
    probs = jax.nn.softmax(top_v, axis=-1)
    comb = jnp.sum(jax.nn.one_hot(top_i, N_EXPERTS, dtype=F32) * probs[..., None], axis=-2)
    comb = comb.astype(h.dtype)
    out = jnp.zeros_like(h)
    for e in range(N_EXPERTS):
        out = out + comb[..., e:e + 1] * _swiglu(h, wg[e], wu[e], wd[e])
    return out

def _trunk(x, conv_s, lru_s, s5re_s, s5im_s, mix_w, norm_mix_g, norm_ffn_g, ffn_w_gate,
           ffn_w_up, ffn_w_down, moe_router_w, moe_router_b, moe_w_gate, moe_w_up,
           moe_w_down, final_norm_g):
    vas, convs, lrus, sres, sims = [], [], [], [], []
    for l in range(DEPTH):
        hn = _rmsnorm(x, norm_mix_g[l])
        mix, va, cs, hl, sr, si = _mixer(hn, conv_s[l], lru_s[l], s5re_s[l], s5im_s[l],
                                         *[w[l] for w in mix_w])
        x = x + mix
        hn = _rmsnorm(x, norm_ffn_g[l])
        j = l // 2
        if l % 2 == 0:
            x = x + _swiglu(hn, ffn_w_gate[j], ffn_w_up[j], ffn_w_down[j])
        else:
            x = x + _moe(hn, moe_router_w[j], moe_router_b[j], moe_w_gate[j], moe_w_up[j],
                         moe_w_down[j])
        vas.append(va)
        convs.append(cs)
        lrus.append(hl)
        sres.append(sr)
        sims.append(si)
    return (_rmsnorm(x, final_norm_g), jnp.stack(vas), jnp.stack(convs), jnp.stack(lrus),
            jnp.stack(sres), jnp.stack(sims))

def setup_inputs(seed: int = 0) -> dict:
    key = jax.random.key(seed)
    ks = jax.random.split(key, 42)

    def nrm(i, shape, scale):
        return scale * jax.random.normal(ks[i], shape, F32)

    u_lam = jax.random.uniform(ks[19], (DEPTH, D_B), F32, 0.9, 0.999)
    base = u_lam ** (1.0 / LRU_C)
    lam_im = math.pi * jnp.arange(P_STATE, dtype=F32)
    return {
        'x_prompt': nrm(0, (BATCH, SEQ, D_MODEL), 1.0),
        'x_sample': nrm(1, (DEC_BATCH, DEC_SEQ, D_MODEL), 1.0),
        'state_conv_b': nrm(2, (DEPTH, DEC_BATCH, CONV_W - 1, D_B), 1.0),
        'state_lru_b': nrm(3, (DEPTH, DEC_BATCH, D_B), 0.5),
        'state_s5_re': nrm(4, (DEPTH, DEC_BATCH, G_C, P_STATE), 0.1),
        'state_s5_im': nrm(5, (DEPTH, DEC_BATCH, G_C, P_STATE), 0.1),
        'norm_mix_g': 1.0 + nrm(6, (DEPTH, D_MODEL), 0.02),
        'w_in': nrm(7, (DEPTH, D_MODEL, IN_COLS), D_MODEL ** -0.5),
        'b_gate': nrm(8, (DEPTH, N_BRANCH * D_MODEL), 0.02),
        'a_ln_g': 1.0 + nrm(9, (DEPTH, D_A), 0.02),
        'a_ln_b': nrm(10, (DEPTH, D_A), 0.02),
        'a_ws': nrm(11, (DEPTH, H_A, CHUNK, CHUNK), CHUNK ** -0.5),
        'a_bs': 1.0 + nrm(12, (DEPTH, H_A, CHUNK), 0.02),
        'b_conv_w': nrm(13, (DEPTH, CONV_W, D_B), CONV_W ** -0.5),
        'b_conv_b': nrm(14, (DEPTH, D_B), 0.01),
        'b_wa': nrm(15, (DEPTH, H_B, BH_B, BH_B), BH_B ** -0.5),
        'b_ba': nrm(16, (DEPTH, D_B), 0.1),
        'b_wx': nrm(17, (DEPTH, H_B, BH_B, BH_B), BH_B ** -0.5),
        'b_bx': nrm(18, (DEPTH, D_B), 0.1),
        'b_lam': jnp.log(base) - jnp.log1p(-base),
        'c_lam_re': -0.5 + nrm(20, (DEPTH, G_C, P_STATE), 0.01),
        'c_lam_im': lam_im + nrm(21, (DEPTH, G_C, P_STATE), 0.01),
        'c_log_dt': jax.random.uniform(ks[22], (DEPTH, G_C), F32, math.log(1e-3), math.log(1e-1)),
        'c_b_re': nrm(23, (DEPTH, G_C, P_STATE, HG_C), (2.0 * HG_C) ** -0.5),
        'c_b_im': nrm(24, (DEPTH, G_C, P_STATE, HG_C), (2.0 * HG_C) ** -0.5),
        'c_c_re': nrm(25, (DEPTH, G_C, HG_C, P_STATE), (2.0 * P_STATE) ** -0.5),
        'c_c_im': nrm(26, (DEPTH, G_C, HG_C, P_STATE), (2.0 * P_STATE) ** -0.5),
        'c_d': nrm(27, (DEPTH, D_C), 1.0),
        'c_glu_w': nrm(28, (DEPTH, D_C, D_C), D_C ** -0.5),
        'c_glu_b': nrm(29, (DEPTH, D_C), 0.02),
        'w_branch': nrm(30, (DEPTH, N_BRANCH, D_BR, D_MODEL), D_BR ** -0.5),
        'w_out': nrm(31, (DEPTH, D_MODEL, D_MODEL), D_MODEL ** -0.5),
        'norm_ffn_g': 1.0 + nrm(32, (DEPTH, D_MODEL), 0.02),
        'ffn_w_gate': nrm(33, (N_DENSE, D_MODEL, D_FF), D_MODEL ** -0.5),
        'ffn_w_up': nrm(34, (N_DENSE, D_MODEL, D_FF), D_MODEL ** -0.5),
        'ffn_w_down': nrm(35, (N_DENSE, D_FF, D_MODEL), D_FF ** -0.5),
        'moe_router_w': nrm(36, (N_MOE, D_MODEL, N_EXPERTS), D_MODEL ** -0.5),
        'moe_router_b': nrm(37, (N_MOE, N_EXPERTS), 0.01),
        'moe_w_gate': nrm(38, (N_MOE, N_EXPERTS, D_MODEL, D_EXP), D_MODEL ** -0.5),
        'moe_w_up': nrm(39, (N_MOE, N_EXPERTS, D_MODEL, D_EXP), D_MODEL ** -0.5),
        'moe_w_down': nrm(40, (N_MOE, N_EXPERTS, D_EXP, D_MODEL), D_EXP ** -0.5),
        'final_norm_g': 1.0 + nrm(41, (D_MODEL,), 0.02),
    }

def reference(x_prompt, x_sample, state_conv_b, state_lru_b, state_s5_re, state_s5_im,
              norm_mix_g, w_in, b_gate, a_ln_g, a_ln_b, a_ws, a_bs, b_conv_w, b_conv_b,
              b_wa, b_ba, b_wx, b_bx, b_lam, c_lam_re, c_lam_im, c_log_dt, c_b_re, c_b_im,
              c_c_re, c_c_im, c_d, c_glu_w, c_glu_b, w_branch, w_out, norm_ffn_g,
              ffn_w_gate, ffn_w_up, ffn_w_down, moe_router_w, moe_router_b, moe_w_gate,
              moe_w_up, moe_w_down, final_norm_g):
    mix_w = (w_in, b_gate, a_ln_g, a_ln_b, a_ws, a_bs, b_conv_w, b_conv_b, b_wa, b_ba, b_wx,
             b_bx, b_lam, c_lam_re, c_lam_im, c_log_dt, c_b_re, c_b_im, c_c_re, c_c_im, c_d,
             c_glu_w, c_glu_b, w_branch, w_out)
    nb = x_prompt.shape[0]
    conv0 = jnp.zeros((DEPTH, nb, CONV_W - 1, D_B), x_prompt.dtype)
    lru0 = jnp.zeros((DEPTH, nb, D_B), F32)
    s50 = jnp.zeros((DEPTH, nb, G_C, P_STATE), F32)
    y_prompt, _, conv_b_p, lru_b_p, s5_re_p, s5_im_p = _trunk(
        x_prompt, conv0, lru0, s50, s50, mix_w, norm_mix_g, norm_ffn_g, ffn_w_gate, ffn_w_up,
        ffn_w_down, moe_router_w, moe_router_b, moe_w_gate, moe_w_up, moe_w_down, final_norm_g)
    y_sample, v_a_s, conv_b_s, lru_b_s, s5_re_s, s5_im_s = _trunk(
        x_sample, state_conv_b, state_lru_b, state_s5_re, state_s5_im, mix_w, norm_mix_g,
        norm_ffn_g, ffn_w_gate, ffn_w_up, ffn_w_down, moe_router_w, moe_router_b, moe_w_gate,
        moe_w_up, moe_w_down, final_norm_g)
    return (y_prompt, y_sample, conv_b_p, lru_b_p, s5_re_p, s5_im_p,
            v_a_s, conv_b_s, lru_b_s, s5_re_s, s5_im_s)


_drawn_inputs = setup_inputs


def setup_inputs(seed=0):
    import zlib

    import numpy as np

    out = dict(_drawn_inputs(seed))
    spreads = {}
    factors = {'b_gate': 3.849,
     'a_ln_g': 2.832,
     'c_lam_re': 19.058,
     'c_glu_b': 12.671,
     'final_norm_g': 8.353,
     'a_ln_b': 4.387,
     'c_c_im': 3.033,
     'moe_router_b': 4.038}
    for name, (base, spread) in spreads.items():
        noise = np.random.default_rng([zlib.crc32(name.encode()), seed]).standard_normal(out[name].shape)
        drawn = base * np.exp(spread * noise) if base else spread * noise
        out[name] = __import__('jax').numpy.asarray(drawn.astype(out[name].dtype))
    for name, factor in factors.items():
        out[name] = (out[name] * factor).astype(out[name].dtype)
    return out
```

```python
from contextlib import ExitStack

import concourse.bass as bass
from concourse import mybir

ALU = mybir.AluOpType
ACT = mybir.ActivationFunctionType
F32 = mybir.dt.float32
AX_X = mybir.AxisListType.X

P = 128
D, DEPTH, SEQ, NSEQ, TS = 1024, 2, 256, 8, 8
T = SEQ + NSEQ * TS
KD = D // P
DB = D // 2
KB = DB // P
CONVW = 4
SEG = CONVW - 1 + TS
XB = CONVW - 1 + SEQ + NSEQ * SEG
H_A = 4
NST = 16
HG = 16
NEXP = 8
FT = 11
EPS = 1e-6
TOKS = [(0, 128), (128, 128), (256, 64)]
NLAST = 1 + NSEQ
SLOTS = 3
SLOT = 3072
N_UNITS = [2, NEXP]
UNIT_CHUNKS, UNIT_A, UNIT_V = FT + 4, FT, FT + 8

SM = {}
_n = 0
for _name, _w in (("g_mix", 8), ("g_ffn", 8), ("b_gate", 24), ("conv_w", 16), ("conv_b", 4), ("ba", 4), ("bx", 4),
                  ("lam", 4), ("c_d", 4), ("glu_b", 4), ("lam_re", 16), ("lam_im", 16), ("log_dt", 16), ("lru_h0", 32)):
    SM[_name] = _n
    _n += _w
NSM = _n
PL = {}
_n = 0
for _name, _w in (("b_re", 256), ("b_im", 256), ("c_re", 512), ("c_im", 512), ("ws", 512), ("ws_s", 256), ("wa", 512),
                  ("wx", 512), ("h0_re", 128), ("h0_im", 128), ("conv", 96)):
    PL[_name] = _n
    _n += _w
NPL = _n


class Ring:

    def __init__(self, banks):
        self.banks, self.n, self.drained, self.of = banks, 0, {}, {}

    def take(self, key):
        b = self.n % self.banks
        self.of[key] = (b, self.n, self.drained.get(b, 0))
        self.n += 1
        self.drained[b] = self.n

    def loop(self, key, per, times):
        self.of[key] = self.n
        self.n += per * times
        self.drained = {b: self.n for b in range(self.banks)}


class Plan:

    def __init__(self):
        self.a, self.v = Ring(3), Ring(2)
        self.chunks, self.order, self.freed = {}, [], {}
        for l in range(DEPTH):
            self.layer(l)
        self.a.take("norm_f")

    def chunk(self, key, ring, last):
        c = len(self.order)
        self.order.append(key)
        self.chunks[key] = (c % SLOTS, 16 * (c // SLOTS + 1), self.freed.get(c - SLOTS))
        self.freed[c] = (ring, last)

    def count(self, ring, key):
        return (self.a if ring == "a" else self.v).of[key][1] + 1

    def layer(self, l):
        a, v = self.a, self.v
        a.take(("norm1", l))
        todo = []
        for m in range(KB):
            a.take(("uc", l, m))
        todo += [(("uc", l, j), "a", ("uc", l, 2 * j + 1)) for j in range(2)]
        for c in range(2):
            a.take(("bt", l, c))
        for j in range(2):
            for b in range(3):
                a.take(("va", l, j, b))
            todo.append((("va", l, j), "a", ("va", l, j, 2)))
        for m in range(KB):
            a.take(("xb", l, m))
        todo += [(("xb", l, j), "a", ("xb", l, 2 * j + 1)) for j in range(2)]
        for s in range(NST):
            if s < 8:
                name, m = ("ua", "gb")[s // 4], s % 4
                a.take((name, l, m))
                if m % 2:
                    todo.append(((name, l, m // 2), "a", (name, l, m)))
            else:
                self.step(l, 0, s - 8, todo)
            if s == 3:
                for g in range(8):
                    a.take(("ri", l, g))
            if s == 4:
                for h in range(H_A):
                    v.take(("mixed", l, h))
        for m in range(KD):
            self.step(l, 1, m, todo)
        for m in range(KB):
            a.take(("glu", l, m))
        todo.append((("glu", l), "a", ("glu", l, 3)))
        for m in range(KD):
            self.step(l, 2, m, todo)
        for m in range(KD):
            v.take(("wo", l, m))
            if m % 2:
                todo.append((("wo", l, m // 2), "v", ("wo", l, m)))
        for key, ring, last in todo:
            self.chunk(key, ring, self.count(ring, last))
        a.take(("norm2", l))
        if l == 1:
            for b in range(3):
                a.take(("logits", b))
            for e in range(NEXP):
                a.take(("comb", e))
        c0 = len(self.order)
        assert c0 % SLOTS == 0 and UNIT_CHUNKS % SLOTS == 0
        self.chunks[("unit", l)] = c0
        a.loop(("unit", l), UNIT_A, N_UNITS[l])
        v.loop(("unit", l), UNIT_V, N_UNITS[l])
        for u in range(N_UNITS[l]):
            self.order += [("unit", l)] * UNIT_CHUNKS
        for k in range(SLOTS):
            self.freed[len(self.order) - SLOTS + k] = ("v", v.n - 2 * (SLOTS - 1 - k))

    def step(self, l, k, m, todo):
        self.a.take(("gate", l, k, m))
        self.v.take(("branch", l, k, m))
        if m % 2:
            todo.append((("step", l, k, m // 2), "v", ("branch", l, k, m)))


def build(nc, x_in, small_in, final_in, router_in, rb_in, pl_in, rows_in, w_proj, w_step, w_glu, w_wo, w_gu, w_dn,
          y_out, va_out, conv_out, lru_out, s5_out):
    plan = Plan()
    A, V = plan.a, plan.v

    with ExitStack() as ctx:
        def sb(name, shape):
            return ctx.enter_context(nc.sbuf_tensor(name, shape, F32))

        def sem(name):
            return ctx.enter_context(nc.semaphore(name))

        ring = [sb(f"ring{i}", [P, SLOT]) for i in range(SLOTS)]
        x = sb("x", [P, KD, T])
        hn = sb("hn", [P, KD, T])
        acc = sb("acc", [P, KD, T])
        mix = sb("mix", [P, 7936])
        xbuf = sb("xbuf", [P, KB, XB])
        E = sb("E", [P, 2, NST, T])
        drive = sb("drive", [P, 2, T])
        rot_v = sb("rot_v", [P, T])
        decay = sb("decay", [P, T])
        z = sb("z", [P, 2, 2, T])
        rot_p = sb("rot_p", [P, 2, T])
        xs = sb("xs", [P, 2, 2, T])
        tmp = sb("tmp", [P, T])
        th = sb("th", [P, 2, T])
        bt = sb("bt", [P, 2, 4, P])
        bbar = sb("bbar", [P, 2, NST, 2 * HG])
        pl = sb("pl", [P, NPL])
        rows = sb("rows", [P, 3, DB])
        small = sb("small", [P, DEPTH, NSM])
        half = sb("half", [P, DEPTH, NSM])
        final = sb("final", [P, KD])
        router = sb("router", [P, KD, NEXP])
        rb = sb("rb", [P, NEXP])
        ones = sb("ones", [P, P])
        ident = sb("ident", [P, P])
        mask = sb("mask", [P, T])
        eps = sb("eps", [P, 1])
        rs = sb("rs", [P, T])
        sp = sb("sp", [P, 24, DEPTH * NST])
        ah0 = sb("ah0", [P, 2, NST, NSEQ])
        ah_t = sb("ah_t", [P, NST, NSEQ])
        bnst = sb("bnst", [P, 3, 6])
        mv = sb("mv", [P, 3, 2])
        lnr = sb("lnr", [P, 3])
        s5_last = sb("s5_last", [P, 2, NST, NLAST])
        lru_last = sb("lru_last", [P, KB, NLAST])
        conv_last = sb("conv_last", [P, KB, NLAST * (CONVW - 1)])
        lg = sb("lg", [P, 3, NEXP])
        rt = sb("rt", [P, 6, 3, NEXP])
        rm = sb("rm", [P, 8, 3])
        revidx = sb("revidx", [P, NEXP])

        bank = [ctx.enter_context(nc.psum_tensor(f"bank{i}", [P, 512], F32)) for i in range(8)]
        a_bank, v_bank, s5_bank, y_bank = bank[0:3], bank[3:5], bank[5:7], bank[7]

        def tiles(t, off, n=KB):
            return t[:, off:off + n * T].rearrange("p (k t) -> p k t", k=n)

        uc, xc, ug, gbg = (tiles(mix[:, :], i * KB * T) for i in range(4))
        v_tok = mix[:, 5120:6656].rearrange("p (b c) -> p b c", b=3)
        zc = tiles(mix[:, :], 5120)
        lru_i = tiles(mix[:, :], 6656)
        hid = tiles(mix[:, :], 0, FT)
        silu = tiles(mix[:, :], 3840, 3)
        accf = acc[:, :, :].rearrange("p k t -> p (k t)")
        lru_a, lru_d = tiles(accf, 0), tiles(accf, KB * T)
        comb_bc = acc

        def sm(name, l, i=0, n=1, t=None):
            return (small if t is None else t)[:, l, SM[name] + i:SM[name] + i + n]

        def mat(name, n, **kw):
            return pl[:, PL[name]:PL[name] + n]

        def cst(row, l, i=0, n=NST):
            return sp[:, row, l * NST + i:l * NST + i + n]

        (R_DT, R_X, R_TH, R_M, R_Y, R_R, R_N, R_SH, R_SN, R_C1, R_CS, R_AR, R_AI, R_NR, R_CR, R_CI, R_T, R_T2,
         R_Q, R_E, R_L1, R_L2, R_L3, R_L4) = range(24)

        landed = [sem(f"landed{i}") for i in range(SLOTS)]
        x_loaded = sem("x_loaded")
        small_loaded = sem("small_loaded")
        layer_loaded = sem("layer_loaded")
        const_ready = sem("const_ready")
        layer_prepared = sem("layer_prepared")
        a_full, a_free = sem("a_full"), sem("a_free")
        v_full, v_free = sem("v_full"), sem("v_free")
        dve_done = sem("dve_done")
        act_done = sem("act_done")
        pool_done = sem("pool_done")
        consts_in = sem("consts_in")
        consts_act = sem("consts_act")
        consts_done = sem("consts_done")
        x_ready = sem("x_ready")
        sq_ready = sem("sq_ready")
        hn_ready = sem("hn_ready")
        bbar_ready = sem("bbar_ready")
        var_ready, std_ready, v_ready = sem("var_ready"), sem("std_ready"), sem("v_ready")
        pads_ready = sem("pads_ready")
        xc_ready = sem("xc_ready")
        tanh_ready = sem("tanh_ready")
        dec_ready, dec_root = sem("dec_ready"), sem("dec_root")
        lru_ready = sem("lru_ready")
        ya_ready, yb_ready, yc_ready = sem("ya_ready"), sem("yb_ready"), sem("yc_ready")
        s5_full, s5_free = sem("s5_full"), sem("s5_free")
        scan_ready, rot_ready = sem("scan_ready"), sem("rot_ready")
        y_full, ys_ready, z_ready = sem("y_full"), sem("ys_ready"), sem("z_ready")
        acc_ready = sem("acc_ready")
        diff_ready, ediff_ready, comb_ready = sem("diff_ready"), sem("ediff_ready"), sem("comb_ready")
        stored, va_stored, y_stored = sem("stored"), sem("va_stored"), sem("y_stored")

        block = ctx.enter_context(nc.Block())

        @block.sync
        def _(sync):
            def load(key, dst, src):
                slot, _, freed = plan.chunks[key]
                if freed:
                    sync.wait_ge(a_full if freed[0] == "a" else v_full, freed[1])
                sync.dma_start(ring[slot][:, 0:dst], src).then_inc(landed[slot], 16)

            for l in range(DEPTH):
                for key in plan.order[plan.order.index(("uc", l, 0)):plan.chunks[("unit", l)]]:
                    name = key[0]
                    if name in ("uc", "va", "xb", "ua", "gb"):
                        i = ("uc", "va", "xb", "ua", "gb").index(name)
                        load(key, 2048, w_proj[l, 2 * i + key[2]])
                    elif name == "step":
                        load(key, 3072, w_step[l, 4 * key[2] + key[3]])
                    elif name == "glu":
                        load(key, 2048, w_glu[l])
                    else:
                        load(key, 2048, w_wo[l, key[2]])
                vb = V.of[("unit", l)]
                u0 = 2 * l
                with sync.Fori(0, N_UNITS[l]) as u:
                    for c in range(UNIT_CHUNKS):
                        if c < SLOTS:
                            freed = 2 * (c + 1 - SLOTS)
                        elif c - SLOTS < FT:
                            freed = c - SLOTS + 1
                        else:
                            freed = FT + 2 * (c - SLOTS - FT + 1)
                        sync.wait_ge(v_full, vb + freed + UNIT_V * u)
                        if c < FT:
                            dst, src = ring[c % SLOTS][:, 0:2048], w_gu[c, bass.ds(u + u0, 1)]
                        else:
                            dst, src = ring[c % SLOTS][:, 0:2816], w_dn[c - FT, bass.ds(u + u0, 1)]
                        sync.dma_start(dst, src.rearrange("u p n -> p (u n)")).then_inc(landed[c % SLOTS], 16)
            sync.wait_ge(hn_ready, 8 * (2 * DEPTH + 1))
            sync.dma_start(y_out, hn[:, :, :].rearrange("p k t -> p (k t)")).then_inc(y_stored, 16)
            sync.wait_ge(y_stored, 16)
            sync.wait_ge(stored, 48 * DEPTH)
            sync.wait_ge(va_stored, 16 * DEPTH)

        @block.gpsimd
        def _(pool):
            n = [0]

            def chain(ins):
                n[0] += 1
                ins.then_inc(pool_done, 1)
                pool.wait_ge(pool_done, n[0])

            def load_layer(l):
                pool.dma_start(pl[:, :], pl_in[l]).then_inc(layer_loaded, 16)
                for r in range(3):
                    pool.dma_start(rows[:, r, :], rows_in[l, r:r + 1].to_broadcast([P, DB])).then_inc(layer_loaded, 16)

            pool.dma_start(small[:, :, :], small_in).then_inc(small_loaded, 16)
            load_layer(0)
            pool.dma_start(final[:, :], final_in).then_inc(small_loaded, 16)
            pool.dma_start(router[:, :, :], router_in).then_inc(small_loaded, 16)
            pool.dma_start(rb[:, :], rb_in.to_broadcast([P, NEXP])).then_inc(small_loaded, 16)
            pool.memset(ones[:, :], 1.0).then_inc(const_ready, 1)
            pool.memset(eps[:, :], EPS).then_inc(const_ready, 1)
            chain(pool.memset(ident[:, :], 0.0))
            pool.affine_select(out=ident[:, :], in_=ident[:, :], compare_op=ALU.not_equal, fill=1.0, base=0,
                               pattern=[[-1, P]], channel_multiplier=1).then_inc(const_ready, 1)
            chain(pool.memset(mask[:, :], 1.0))
            pool.memset(mask[:, SEQ::TS], 0.0).then_inc(const_ready, 1)
            pool.memset(bbar[:, :, :, :], 0.0).then_inc(const_ready, 1)
            pool.memset(xbuf[:, :, 0:CONVW - 1], 0.0).then_inc(const_ready, 1)
            pool.memset(mv[:, :, :], 1.0).then_inc(const_ready, 1)
            pool.memset(lg[:, :, :], 0.0).then_inc(const_ready, 1)
            for e in range(NEXP):
                pool.memset(revidx[:, e:e + 1], float(NEXP - e)).then_inc(const_ready, 1)

            for l in range(DEPTH):
                if l:
                    pool.wait_ge(x_ready, 16 * (l - 1) + 8)
                    load_layer(l)
                pool.wait_ge(layer_loaded, 64 * (l + 1))
                ws = mat("ws", 512).rearrange("p (h t) -> p h t", h=H_A)
                pool.affine_select(out=ws, in_=ws, compare_op=ALU.is_ge, fill=0.0, base=0,
                                   pattern=[[0, H_A], [1, P]], channel_multiplier=-1).then_inc(layer_prepared, 1)
                wss = mat("ws_s", 256).rearrange("p (h t) -> p h t", h=H_A)
                pool.affine_select(out=wss, in_=wss, compare_op=ALU.is_ge, fill=0.0, base=0,
                                   pattern=[[0, H_A], [1, 64]], channel_multiplier=-1).then_inc(layer_prepared, 1)
                ci = mat("c_im", 512)
                pool.tensor_scalar(ci, ci, -1.0, 0.0, ALU.mult, ALU.add).then_inc(layer_prepared, 1)

                pool.wait_ge(v_ready, l + 1)
                pool.dma_start(va_out[l], v_tok[0:64, 2, :]).then_inc(va_stored, 16)

                pool.wait_ge(a_free, A.of[("xb", l, KB - 1)][1] + 1)
                pool.wait_ge(pads_ready, l + 1)
                if l:
                    pool.wait_ge(stored, 48 * l)
                chain(pool.tensor_copy(conv_last[:, :, 0:3], xbuf[:, :, SEQ:SEQ + 3]))
                seg = xbuf[:, :, 3 + SEQ:].rearrange("p k (b s) -> p k b s", s=SEG)
                for k in range(KB):
                    chain(pool.tensor_copy(conv_last[:, k, 3:].rearrange("p (b s) -> p b s", s=3), seg[:, k, :, TS:SEG]))
                pool.dma_start(conv_out[l], conv_last[:, :, :].rearrange("p k n -> p (k n)")).then_inc(stored, 16)

                for s in range(NST):
                    q = l * NST + s
                    zr, zi = z[:, q % 2, 0], z[:, q % 2, 1]
                    er, ei = E[:, 0, s], E[:, 1, s]
                    xr, xi = xs[:, q % 2, 0], xs[:, q % 2, 1]
                    pool.wait_ge(scan_ready, q + 1)
                    if q >= 2:
                        pool.wait_ge(y_full, q - 1)
                    pool.tensor_tensor(xr, zr, er, ALU.mult).then_inc(pool_done, 1)
                    pool.tensor_tensor(rot_p[:, 0], zi, ei, ALU.mult).then_inc(pool_done, 1)
                    pool.tensor_tensor(xi, zr, ei, ALU.mult).then_inc(pool_done, 1)
                    pool.tensor_tensor(rot_p[:, 1], zi, er, ALU.mult).then_inc(pool_done, 1)
                    n[0] += 4
                    pool.wait_ge(pool_done, n[0])
                    chain(pool.tensor_tensor(xr, xr, rot_p[:, 0], ALU.subtract))
                    chain(pool.tensor_tensor(xi, xi, rot_p[:, 1], ALU.add))
                    pool.tensor_copy(s5_last[:, 0, s, :], xr[:, SEQ - 1::TS]).then_inc(pool_done, 1)
                    n[0] += 1
                    pool.tensor_copy(s5_last[:, 1, s, :], xi[:, SEQ - 1::TS]).then_inc(rot_ready, 1)
                pool.wait_ge(pool_done, n[0])
                pool.wait_ge(rot_ready, NST * (l + 1))
                pool.dma_start(s5_out[l], s5_last[:, :, :, :].rearrange("p c s n -> p (c s n)")).then_inc(stored, 16)
                pool.wait_ge(lru_ready, l + 1)
                pool.dma_start(lru_out[l], lru_last[:, :, :].rearrange("p k n -> p (k n)")).then_inc(stored, 16)
                pool.wait_ge(stored, 48 * (l + 1))

        @block.scalar
        def _(act):
            n = [0]

            def chain(ins):
                n[0] += 1
                ins.then_inc(act_done, 1)
                act.wait_ge(act_done, n[0])

            def evac(key, rows_, cols):
                b, q, _ = A.of[key]
                act.wait_ge(a_full, q + 1)
                return a_bank[b][0:rows_, 0:cols]

            def norm(key, r):
                for k in range(KD):
                    if r:
                        act.wait_ge(x_ready, 8 * (r - 1) + k + 1)
                    act.activation(hn[:, k], x[:, k], ACT.Square).then_inc(sq_ready, 1)
                act.wait_ge(const_ready, 2)
                if r:
                    act.wait_ge(hn_ready, 8 * r)
                act.activation(rs[:, :], evac(key, P, T), ACT.Sqrt, bias=eps[:, :], scale=1.0 / D).then_inc(a_free, 1)

            act.dma_start(x[:, :, :], x_in).then_inc(x_loaded, 16)
            act.wait_ge(small_loaded, 64)
            act.activation(sp[:, R_DT].rearrange("p (l n) -> p l n", l=DEPTH), small[:, :, SM["log_dt"]:SM["log_dt"] + NST],
                           ACT.Exp).then_inc(consts_act, 1)
            act.wait_ge(consts_in, 1)
            act.activation(sp[:, R_E, 0:8], sp[:, R_L1, 0:8], ACT.Exp, scale=-1.0).then_inc(consts_act, 1)
            act.wait_ge(consts_in, 2)
            act.activation(sp[:, R_SH], sp[:, R_N], ACT.Sin, scale=0.5).then_inc(consts_act, 1)
            act.activation(sp[:, R_SN], sp[:, R_N], ACT.Sin).then_inc(consts_act, 1)
            act.wait_ge(x_loaded, 16)
            for l in range(DEPTH):
                norm(("norm1", l), 2 * l)
                for m in range(KB):
                    act.activation(uc[:, m], evac(("uc", l, m), P, T), ACT.Copy).then_inc(a_free, 1)
                for c in range(2):
                    act.activation(bt[:, c].rearrange("p k n -> p (k n)"), evac(("bt", l, c), P, 512), ACT.Copy)\
                        .then_inc(a_free, 1)
                for j in range(2):
                    for b, (_, w) in enumerate(TOKS):
                        act.activation(v_tok[0:w, b, 256 * j:256 * j + 256], evac(("va", l, j, b), w, 256),
                                       ACT.Gelu_apprx_tanh).then_inc(a_free, 1)
                for m in range(KB):
                    src = evac(("xb", l, m), P, T)
                    chain(act.activation(xbuf[:, m, 3:3 + SEQ], src[:, 0:SEQ], ACT.Copy))
                    act.activation(xbuf[:, m, 3 + SEQ:].rearrange("p (b s) -> p b s", s=SEG)[:, :, 3:SEG],
                                   src[:, SEQ:T].rearrange("p (b s) -> p b s", s=TS), ACT.Copy).then_inc(a_free, 1)
                act.wait_ge(var_ready, l + 1)
                act.activation(lnr[:, :], mv[:, :, 1], ACT.Sqrt, bias=eps[:, :]).then_inc(std_ready, 1)

                def gate(k, m):
                    b, vq, _ = V.of[("branch", l, k, m)]
                    src = evac(("gate", l, k, m), P, T)
                    q = (l * 3 + k) * 8 + m
                    if q >= 2:
                        prev = (l * 3 + k) * 8 + m - 2
                        pk = ("branch", prev // 24, prev // 8 % 3, prev % 8)
                        act.wait_ge(v_free, V.of[pk][1] + 1)
                    act.activation(th[:, q % 2], src, ACT.Tanh, scale=0.5, bias=sm("b_gate", l, 8 * k + m, t=half))\
                        .then_inc(a_free, 1)

                def z_gelu(ct):
                    act.wait_ge(ys_ready, KB * l + ct + 1)
                    act.activation(zc[:, ct], zc[:, ct], ACT.Gelu_apprx_tanh).then_inc(z_ready, 1)

                for s in range(NST):
                    if s < 8:
                        name, dst = (("ua", ug), ("gb", gbg))[s // 4]
                        act.activation(dst[:, s % 4], evac((name, l, s % 4), P, T), ACT.Gelu_apprx_tanh).then_inc(a_free, 1)
                    else:
                        gate(0, s - 8)
                    if s == 3:
                        for g in range(8):
                            dst, bias = ((lru_a, "ba"), (lru_i, "bx"))[g // 4]
                            act.activation(dst[:, g % 4], evac(("ri", l, g), P, T), ACT.Tanh, scale=0.5,
                                           bias=sm(bias, l, g % 4, t=half)).then_inc(a_free, 1)
                        act.wait_ge(a_free, A.of[("ri", l, 7)][1] + 1)
                        for g in range(4):
                            q = sp[:, R_Q, 4 * l + g:4 * l + g + 1]
                            act.activation(lru_a[:, g], lru_a[:, g], ACT.Tanh, scale=q, bias=q).then_inc(tanh_ready, 1)
                    if s == 5:
                        act.wait_ge(dec_ready, l + 1)
                        act.activation(lru_d, lru_d, ACT.Sqrt).then_inc(dec_root, 1)
                    if s >= 6 and (s - 6) % 4 == 0:
                        z_gelu((s - 6) // 4)
                z_gelu(3)
                for m in range(KD):
                    gate(1, m)
                for m in range(KB):
                    act.activation(lru_i[:, m], evac(("glu", l, m), P, T), ACT.Tanh, scale=0.5,
                                   bias=sm("glu_b", l, m, t=half)).then_inc(a_free, 1)
                for m in range(KD):
                    gate(2, m)
                norm(("norm2", l), 2 * l + 1)
                if l == 1:
                    for b, (_, w) in enumerate(TOKS):
                        act.activation(lg[0:w, b, :], evac(("logits", b), w, NEXP), ACT.Copy).then_inc(a_free, 1)
                    act.wait_ge(diff_ready, 1)
                    act.activation(rm[:, 4, :], rm[:, 3, :], ACT.Exp).then_inc(ediff_ready, 1)
                    for e in range(NEXP):
                        act.activation(comb_bc[:, e], evac(("comb", e), P, T), ACT.Copy).then_inc(a_free, 1)
                ab, vb = A.of[("unit", l)], V.of[("unit", l)]
                with act.Fori(0, N_UNITS[l]) as u:
                    for f in range(FT):
                        act.wait_ge(a_full, ab + f + 1 + UNIT_A * u)
                        act.wait_ge(v_free, vb + (f - 2 if f >= 3 else 0) + UNIT_V * u)
                        act.activation(silu[:, f % 3], a_bank[f % 3][:, 0:T], ACT.Silu).then_inc(a_free, 1)
            norm("norm_f", 2 * DEPTH)

        @block.vector
        def _(dve):
            n = [0]

            def chain(ins):
                n[0] += 1
                ins.then_inc(dve_done, 1)
                dve.wait_ge(dve_done, n[0])

            def norm(key, r, gain):
                b, q, _ = A.of[key]
                dve.wait_ge(a_free, q + 1)
                chain(dve.reciprocal(rs[:, :], rs[:, :]))
                for k in range(KD):
                    dve.scalar_tensor_tensor(hn[:, k], x[:, k], gain(k), rs[:, :], ALU.mult, ALU.mult).then_inc(hn_ready, 1)

            def bc(ap, shape):
                return ap.unsqueeze(len(shape) - 1).to_broadcast(shape)

            row = lambda r: sp[:, r]

            dve.wait_ge(small_loaded, 64)
            chain(dve.tensor_scalar(half[:, :, :], small[:, :, :], 0.5, None, ALU.mult))
            two = lambda r, w: sp[:, r, 0:DEPTH * w].rearrange("p (l n) -> p l n", l=DEPTH)
            lam = small[:, :, SM["lam"]:SM["lam"] + 4]
            l1, l2, l3, l4 = (sp[:, r, 0:8] for r in (R_L1, R_L2, R_L3, R_L4))
            ee = sp[:, R_E, 0:8]
            chain(dve.tensor_scalar(two(R_L2, 4), lam, -1.0, None, ALU.mult))
            dve.tensor_tensor(two(R_L1, 4), two(R_L2, 4), lam, ALU.max).then_inc(consts_in, 1)
            dve.wait_ge(consts_act, 2)
            chain(dve.tensor_scalar(l3, ee, 2.0, None, ALU.add))
            chain(dve.reciprocal(l3, l3))
            chain(dve.tensor_tensor(l3, l3, ee, ALU.mult))
            chain(dve.tensor_tensor(l4, l3, l3, ALU.mult))
            chain(dve.tensor_scalar(ee, l4, 1.0 / 15, None, ALU.mult))
            for d in (13, 11, 9, 7, 5, 3):
                chain(dve.scalar_tensor_tensor(ee, ee, 1.0 / d, l4, ALU.add, ALU.mult))
            chain(dve.scalar_tensor_tensor(ee, ee, 1.0, l3, ALU.add, ALU.mult))
            chain(dve.tensor_scalar(l2, l2, 0.0, None, ALU.max))
            chain(dve.scalar_tensor_tensor(l1, ee, 2.0, l2, ALU.mult, ALU.add))
            dve.tensor_scalar(sp[:, R_Q, 0:8], l1, 2.0, None, ALU.mult).then_inc(consts_done, 1)

            lre, lim = (small[:, :, SM[k]:SM[k] + NST] for k in ("lam_re", "lam_im"))
            chain(dve.tensor_tensor(two(R_X, NST), lre, two(R_DT, NST), ALU.mult))
            chain(dve.tensor_tensor(two(R_TH, NST), lim, two(R_DT, NST), ALU.mult))
            chain(dve.tensor_scalar(row(R_N), row(R_TH), 0.15915494309189535, 12582912.0, ALU.mult, ALU.add))
            chain(dve.tensor_scalar(row(R_N), row(R_N), -12582912.0, None, ALU.add))
            chain(dve.scalar_tensor_tensor(row(R_TH), row(R_N), -6.28125, row(R_TH), ALU.mult, ALU.add))
            chain(dve.scalar_tensor_tensor(row(R_TH), row(R_N), -0.0019353071795864769, row(R_TH), ALU.mult, ALU.add))
            dve.tensor_scalar(row(R_N), row(R_TH), 3.1415925, -3.1415925, ALU.min, ALU.max).then_inc(consts_in, 1)
            chain(dve.tensor_scalar(row(R_Y), row(R_X), 1.0 / 64, None, ALU.mult))
            chain(dve.tensor_scalar(row(R_M), row(R_Y), 1.0 / 5040, None, ALU.mult))
            for c in (720, 120, 24, 6, 2, 1):
                chain(dve.scalar_tensor_tensor(row(R_M), row(R_M), 1.0 / c, row(R_Y), ALU.add, ALU.mult))
            for _ in range(6):
                chain(dve.scalar_tensor_tensor(row(R_M), row(R_M), 2.0, row(R_M), ALU.add, ALU.mult))
            chain(dve.tensor_scalar(row(R_R), row(R_M), 1.0, None, ALU.add))
            dve.wait_ge(consts_act, 4)
            chain(dve.tensor_tensor(row(R_C1), row(R_SH), row(R_SH), ALU.mult))
            chain(dve.tensor_scalar(row(R_C1), row(R_C1), -2.0, None, ALU.mult))
            chain(dve.tensor_scalar(row(R_CS), row(R_C1), 1.0, None, ALU.add))
            chain(dve.tensor_tensor(row(R_AR), row(R_R), row(R_CS), ALU.mult))
            chain(dve.tensor_tensor(row(R_AI), row(R_R), row(R_SN), ALU.mult))
            chain(dve.tensor_tensor(row(R_NR), row(R_M), row(R_CS), ALU.mult))
            chain(dve.tensor_tensor(row(R_NR), row(R_NR), row(R_C1), ALU.add))
            chain(dve.tensor_tensor(two(R_T, NST), lre, lre, ALU.mult))
            chain(dve.tensor_tensor(two(R_T2, NST), lim, lim, ALU.mult))
            chain(dve.tensor_tensor(row(R_T), row(R_T), row(R_T2), ALU.add))
            chain(dve.reciprocal(row(R_T), row(R_T)))
            chain(dve.tensor_tensor(two(R_CR, NST), two(R_NR, NST), lre, ALU.mult))
            chain(dve.tensor_tensor(two(R_T2, NST), two(R_AI, NST), lim, ALU.mult))
            chain(dve.tensor_tensor(row(R_CR), row(R_CR), row(R_T2), ALU.add))
            chain(dve.tensor_tensor(row(R_CR), row(R_CR), row(R_T), ALU.mult))
            chain(dve.tensor_tensor(two(R_CI, NST), two(R_AI, NST), lre, ALU.mult))
            chain(dve.tensor_tensor(two(R_T2, NST), two(R_NR, NST), lim, ALU.mult))
            chain(dve.tensor_tensor(row(R_CI), row(R_CI), row(R_T2), ALU.subtract))
            chain(dve.tensor_tensor(row(R_CI), row(R_CI), row(R_T), ALU.mult))
            dve.wait_ge(const_ready, 16)
            dve.wait_ge(x_loaded, 16)

            for l in range(DEPTH):
                norm(("norm1", l), 2 * l, lambda k: sm("g_mix", l, k))

                dve.wait_ge(layer_loaded, 64 * (l + 1))
                br, bi = (mat(k, 256).rearrange("p (s h) -> p s h", h=HG) for k in ("b_re", "b_im"))
                cr, ci = (bc(cst(r, l), [P, NST, HG]) for r in (R_CR, R_CI))
                t = [accf[:, 256 * i:256 * i + 256].rearrange("p (s h) -> p s h", h=HG) for i in range(4)]
                chain(dve.tensor_tensor(t[0], br, cr, ALU.mult))
                chain(dve.tensor_tensor(t[1], bi, ci, ALU.mult))
                chain(dve.tensor_tensor(t[2], br, ci, ALU.mult))
                chain(dve.tensor_tensor(t[3], bi, cr, ALU.mult))
                for c, op in ((0, ALU.subtract), (1, ALU.add)):
                    for g in range(2):
                        rng = slice(64 * g, 64 * g + 64)
                        dve.tensor_tensor(bbar[rng, c, :, HG * g:HG * g + HG], t[2 * c][rng], t[2 * c + 1][rng], op)\
                            .then_inc(bbar_ready, 1)
                dve.wait_ge(bbar_ready, 4 * (l + 1))

                h0r, h0i = (mat(k, 128).rearrange("p (s b) -> p s b", b=NSEQ) for k in ("h0_re", "h0_im"))
                ar, ai = (bc(cst(r, l), [P, NST, NSEQ]) for r in (R_AR, R_AI))
                chain(dve.tensor_tensor(ah0[:, 0], h0r, ar, ALU.mult))
                chain(dve.tensor_tensor(ah_t[:, :, :], h0i, ai, ALU.mult))
                chain(dve.tensor_tensor(ah0[:, 0], ah0[:, 0], ah_t[:, :, :], ALU.subtract))
                chain(dve.tensor_tensor(ah0[:, 1], h0r, ai, ALU.mult))
                chain(dve.tensor_tensor(ah_t[:, :, :], h0i, ar, ALU.mult))
                chain(dve.tensor_tensor(ah0[:, 1], ah0[:, 1], ah_t[:, :, :], ALU.add))

                chain(dve.memset(E[:, 0, :, 0:1], 1.0))
                chain(dve.memset(E[:, 1, :, 0:1], 0.0))
                chain(dve.tensor_copy(E[:, 0, :, 1:2], cst(R_CS, l).unsqueeze(2)))
                chain(dve.tensor_copy(E[:, 1, :, 1:2], cst(R_SN, l).unsqueeze(2)))
                pr, pi, pt = row(R_X)[:, 0:NST], row(R_TH)[:, 0:NST], row(R_T)[:, 0:NST]
                w = 2
                while w < SEQ:
                    er, ei = E[:, 0, :, w // 2], E[:, 1, :, w // 2]
                    chain(dve.tensor_tensor(pr, er, er, ALU.mult))
                    chain(dve.tensor_tensor(pt, ei, ei, ALU.mult))
                    chain(dve.tensor_tensor(pr, pr, pt, ALU.subtract))
                    chain(dve.scalar_tensor_tensor(pi, er, 2.0, ei, ALU.mult, ALU.mult))
                    prb, pib = bc(pr, [P, NST, w]), bc(pi, [P, NST, w])
                    tt = accf[:, 0:NST * w].rearrange("p (s w) -> p s w", w=w)
                    lo_r, lo_i, hi_r, hi_i = E[:, 0, :, 0:w], E[:, 1, :, 0:w], E[:, 0, :, w:2 * w], E[:, 1, :, w:2 * w]
                    chain(dve.tensor_tensor(hi_r, lo_r, prb, ALU.mult))
                    chain(dve.tensor_tensor(tt, lo_i, pib, ALU.mult))
                    chain(dve.tensor_tensor(hi_r, hi_r, tt, ALU.subtract))
                    chain(dve.tensor_tensor(hi_i, lo_r, pib, ALU.mult))
                    chain(dve.tensor_tensor(tt, lo_i, prb, ALU.mult))
                    chain(dve.tensor_tensor(hi_i, hi_i, tt, ALU.add))
                    w *= 2
                for c in range(2):
                    chain(dve.tensor_copy(E[:, c, :, SEQ:T].rearrange("p s (b t) -> p s b t", t=TS),
                                          E[:, c, :, 0:TS].unsqueeze(2).to_broadcast([P, NST, NSEQ, TS])))

                seg = xbuf[:, :, 3 + SEQ:].rearrange("p k (b s) -> p k b s", s=SEG)
                cv = mat("conv", 96).rearrange("p (k b w) -> p k b w", k=KB, w=3)
                if l:
                    dve.wait_ge(stored, 48 * l)
                for k in range(KB):
                    chain(dve.tensor_copy(seg[:, k, :, 0:3], cv[:, k]))
                dve.sem_inc(pads_ready, 1)

                dve.wait_ge(a_free, A.of[("va", l, 1, 2)][1] + 1)
                for b, (_, w) in enumerate(TOKS):
                    chain(dve.bn_stats(bnst[0:w, b], v_tok[0:w, b]))
                    if b < 2:
                        chain(dve.bn_aggr(mv[0:w, b], bnst[0:w, b]))
                    else:
                        dve.bn_aggr(mv[0:w, b], bnst[0:w, b]).then_inc(var_ready, 1)
                dve.wait_ge(std_ready, l + 1)
                chain(dve.reciprocal(lnr[:, :], lnr[:, :]))
                for b, (_, w) in enumerate(TOKS):
                    vt = v_tok[0:w, b]
                    chain(dve.tensor_scalar(vt, vt, mv[0:w, b, 0:1], lnr[0:w, b:b + 1], ALU.subtract, ALU.mult))
                    chain(dve.tensor_tensor(vt, vt, rows[0:w, 0], ALU.mult))
                    if b < 2:
                        chain(dve.tensor_tensor(vt, vt, rows[0:w, 1], ALU.add))
                    else:
                        dve.tensor_tensor(vt, vt, rows[0:w, 1], ALU.add).then_inc(v_ready, 1)
                dve.wait_ge(v_ready, l + 1)

                def s5(s):
                    q = l * NST + s
                    vr, vi = s5_bank[0][:, 0:T], s5_bank[1][:, 0:T]
                    er, ei = E[:, 0, s], E[:, 1, s]
                    dr, di = drive[:, 0], drive[:, 1]
                    dve.wait_ge(s5_full, q + 1)
                    chain(dve.tensor_scalar(decay[:, :], mask[:, :], cst(R_R, l, s, 1), None, ALU.mult))
                    chain(dve.tensor_tensor(dr, vr, er, ALU.mult))
                    chain(dve.tensor_tensor(rot_v[:, :], vi, ei, ALU.mult))
                    chain(dve.tensor_tensor(dr, dr, rot_v[:, :], ALU.add))
                    chain(dve.tensor_tensor(di, vi, er, ALU.mult))
                    dve.tensor_tensor(rot_v[:, :], vr, ei, ALU.mult).then_inc(s5_free, 1)
                    dve.wait_ge(s5_free, q + 1)
                    chain(dve.tensor_tensor(di, di, rot_v[:, :], ALU.subtract))
                    chain(dve.tensor_tensor(dr[:, SEQ::TS], dr[:, SEQ::TS], ah0[:, 0, s], ALU.add))
                    chain(dve.tensor_tensor(di[:, SEQ::TS], di[:, SEQ::TS], ah0[:, 1, s], ALU.add))
                    if q >= 2:
                        dve.wait_ge(rot_ready, q - 1)
                    chain(dve.tensor_tensor_scan(z[:, q % 2, 0], decay[:, :], dr, 0.0, ALU.mult, ALU.add))
                    dve.tensor_tensor_scan(z[:, q % 2, 1], decay[:, :], di, 0.0, ALU.mult, ALU.add).then_inc(scan_ready, 1)
                    dve.wait_ge(scan_ready, q + 1)

                def conv():
                    for k in range(KB):
                        w = lambda i: sm("conv_w", l, 4 * i + k)
                        p_out = xc[:, k, 0:SEQ]
                        s_out = xc[:, k, SEQ:T].rearrange("p (b s) -> p b s", s=TS)
                        chain(dve.tensor_scalar(p_out, xbuf[:, k, 0:SEQ], w(0), sm("conv_b", l, k), ALU.mult, ALU.add))
                        chain(dve.tensor_scalar(s_out, seg[:, k, :, 0:TS], w(0), sm("conv_b", l, k), ALU.mult, ALU.add))
                        for i in range(1, CONVW):
                            chain(dve.scalar_tensor_tensor(p_out, xbuf[:, k, i:i + SEQ], w(i), p_out, ALU.mult, ALU.add))
                            chain(dve.scalar_tensor_tensor(s_out, seg[:, k, :, i:i + TS], w(i), s_out, ALU.mult, ALU.add))
                    dve.sem_inc(xc_ready, 1)

                def mixed():
                    for h in range(H_A):
                        b, q, _ = V.of[("mixed", l, h)]
                        src = v_bank[b]
                        dve.wait_ge(v_full, q + 1)
                        bs = rows[:, 2, P * h:P * h + P]
                        chain(dve.tensor_tensor(tmp[:, 0:SEQ].rearrange("p (c t) -> p c t", c=2),
                                                src[:, 0:SEQ].rearrange("p (c t) -> p c t", c=2),
                                                bs.unsqueeze(1).to_broadcast([P, 2, P]), ALU.add))
                        dve.tensor_tensor(tmp[:, SEQ:T].rearrange("p (b t) -> p b t", t=TS),
                                          src[:, SEQ:T].rearrange("p (b t) -> p b t", t=TS),
                                          bs[:, 0:TS].unsqueeze(1).to_broadcast([P, NSEQ, TS]), ALU.add).then_inc(v_free, 1)
                        dve.wait_ge(v_free, q + 1)
                        dve.wait_ge(a_free, A.of[("ua", l, h)][1] + 1)
                        chain(dve.tensor_tensor(ug[:, h], tmp[:, :], ug[:, h], ALU.mult))
                    dve.sem_inc(ya_ready, 1)

                def decays():
                    dve.wait_ge(tanh_ready, 4 * (l + 1))
                    chain(dve.tensor_scalar(lru_d, lru_a, 1.0, None, ALU.add))
                    chain(dve.reciprocal(lru_d, lru_d))
                    chain(dve.scalar_tensor_tensor(lru_d, lru_a, 2.0, lru_d, ALU.mult, ALU.mult))
                    chain(dve.tensor_scalar(lru_a, lru_d, -1.0, 1.0, ALU.mult, ALU.add))
                    dve.scalar_tensor_tensor(lru_d, lru_a, 1.0, lru_d, ALU.add, ALU.mult).then_inc(dec_ready, 1)

                def lru():
                    chain(dve.scalar_tensor_tensor(lru_i, lru_i, 1.0, xc, ALU.add, ALU.mult))
                    dve.wait_ge(dec_root, l + 1)
                    chain(dve.scalar_tensor_tensor(lru_i, lru_i, 0.5, lru_d, ALU.mult, ALU.mult))
                    a0, d0 = lru_a[:, :, SEQ::TS], lru_i[:, :, SEQ::TS]
                    t = ah_t[:, 0:KB, :]
                    chain(dve.tensor_tensor(t, a0, sm("lru_h0", l, 0, 32).rearrange("p (k b) -> p k b", b=NSEQ), ALU.mult))
                    chain(dve.tensor_tensor(d0, d0, t, ALU.add))
                    chain(dve.memset(a0, 0.0))
                    for k in range(KB):
                        chain(dve.tensor_tensor_scan(lru_d[:, k], lru_a[:, k], lru_i[:, k], 0.0, ALU.mult, ALU.add))
                    dve.tensor_copy(lru_last[:, :, :], lru_d[:, :, SEQ - 1::TS]).then_inc(lru_ready, 1)

                def branch(k, m):
                    b, q, _ = V.of[("branch", l, k, m)]
                    src = v_bank[b][:, 0:T]
                    g = th[:, ((l * 3 + k) * 8 + m) % 2]
                    dve.wait_ge(v_full, q + 1)
                    dve.wait_ge(a_free, A.of[("gate", l, k, m)][1] + 1)
                    dst = acc[:, m] if k == 0 else tmp[:, :]
                    dve.scalar_tensor_tensor(dst, g, 1.0, src, ALU.add, ALU.mult).then_inc(v_free, 1)
                    dve.wait_ge(v_free, q + 1)
                    if k == 1:
                        chain(dve.tensor_tensor(acc[:, m], acc[:, m], tmp[:, :], ALU.add))
                    if k == 2:
                        dve.scalar_tensor_tensor(acc[:, m], tmp[:, :], 0.5, acc[:, m], ALU.mult, ALU.add).then_inc(acc_ready, 1)
                        dve.wait_ge(acc_ready, KD * l + m + 1)

                def ys(ct):
                    dve.wait_ge(y_full, l * NST + 4 * ct + 4)
                    dve.scalar_tensor_tensor(zc[:, ct], uc[:, ct], sm("c_d", l, ct), y_bank[:, 0:T], ALU.mult, ALU.add)\
                        .then_inc(ys_ready, 1)

                for s in range(NST + 3):
                    if s == 4:
                        mixed()
                    if s == 8:
                        dve.wait_ge(lru_ready, l + 1)
                        dve.wait_ge(a_free, A.of[("gb", l, 3)][1] + 1)
                        dve.tensor_tensor(gbg, gbg, lru_d, ALU.mult).then_inc(yb_ready, 1)
                        dve.wait_ge(yb_ready, l + 1)
                    if 8 <= s < NST:
                        branch(0, s - 8)
                    if s < NST:
                        s5(s)
                    if s == 0:
                        dve.wait_ge(a_free, A.of[("xb", l, 3)][1] + 1)
                        conv()
                    if s == 4:
                        decays()
                    if s == 6:
                        lru()
                    if s >= 6 and (s - 6) % 4 == 0:
                        if s == 6:
                            dve.wait_ge(va_stored, 16 * (l + 1))
                        ys((s - 6) // 4)
                for m in range(KD):
                    branch(1, m)
                dve.wait_ge(a_free, A.of[("glu", l, 3)][1] + 1)
                for m in range(KB):
                    dve.scalar_tensor_tensor(zc[:, m], lru_i[:, m], 1.0, zc[:, m], ALU.add, ALU.mult).then_inc(yc_ready, 1)
                for m in range(KD):
                    branch(2, m)
                for m in range(KD):
                    b, q, _ = V.of[("wo", l, m)]
                    dve.wait_ge(v_full, q + 1)
                    dve.scalar_tensor_tensor(x[:, m], v_bank[b][:, 0:T], 0.5, x[:, m], ALU.mult, ALU.add).then_inc(v_free, 1)
                    dve.wait_ge(v_free, q + 1)
                    dve.sem_inc(x_ready, 1)
                norm(("norm2", l), 2 * l + 1, lambda k: sm("g_ffn", l, k))
                if l == 1:
                    dve.wait_ge(a_free, A.of[("logits", 2)][1] + 1)
                    full = [P, 3, NEXP]
                    rix = revidx[:, :].unsqueeze(1).to_broadcast(full)
                    for b in range(3):
                        chain(dve.tensor_tensor(lg[:, b], lg[:, b], rb[:, :], ALU.add))
                    k1, k2, t0, lg2 = rt[:, 0], rt[:, 1], rt[:, 2], rt[:, 3]
                    m1, m2, mx, df, ex, p1, p2 = (rm[:, i] for i in range(7))

                    def best(src, top, pick):
                        chain(dve.tensor_reduce(top, src, AX_X, ALU.max))
                        chain(dve.tensor_tensor(t0, src, bc(top, full), ALU.is_equal))
                        chain(dve.tensor_tensor(t0, t0, rix, ALU.mult))
                        chain(dve.tensor_reduce(mx, t0, AX_X, ALU.max))
                        chain(dve.tensor_tensor(pick, t0, bc(mx, full), ALU.is_equal))

                    best(lg[:, :, :], m1, k1)
                    chain(dve.scalar_tensor_tensor(lg2, k1, -3.0e38, lg[:, :, :], ALU.mult, ALU.add))
                    best(lg2, m2, k2)
                    dve.tensor_tensor(df, m2, m1, ALU.subtract).then_inc(diff_ready, 1)
                    dve.wait_ge(ediff_ready, 1)
                    chain(dve.tensor_scalar(p1, ex, 1.0, None, ALU.add))
                    chain(dve.reciprocal(p1, p1))
                    chain(dve.tensor_tensor(p2, ex, p1, ALU.mult))
                    chain(dve.tensor_tensor(k1, k1, bc(p1, full), ALU.mult))
                    chain(dve.tensor_tensor(k2, k2, bc(p2, full), ALU.mult))
                    dve.tensor_tensor(k1, k1, k2, ALU.add).then_inc(comb_ready, 1)
                ab, vb = A.of[("unit", l)], V.of[("unit", l)]
                xb0 = 16 * l + 8
                d0 = n[0]
                with dve.Fori(0, N_UNITS[l]) as u:
                    for f in range(FT):
                        dve.wait_ge(a_free, ab + f + 1 + UNIT_A * u)
                        dve.wait_ge(v_full, vb + f + 1 + UNIT_V * u)
                        dve.tensor_tensor(hid[:, f], silu[:, f % 3], v_bank[f % 2][:, 0:T], ALU.mult).then_inc(v_free, 1)
                    for m in range(KD):
                        g = FT + m
                        dve.wait_ge(v_full, vb + g + 1 + UNIT_V * u)
                        if l == 0:
                            dve.tensor_tensor(x[:, m], v_bank[g % 2][:, 0:T], x[:, m], ALU.add).then_inc(v_free, 1)
                            dve.wait_ge(v_free, vb + g + 1 + UNIT_V * u)
                        else:
                            cb = comb_bc[:, bass.ds(u, 1)].rearrange("p u t -> p (u t)")
                            dve.tensor_tensor(tmp[:, :], v_bank[g % 2][:, 0:T], cb, ALU.mult).then_inc(v_free, 1)
                            dve.wait_ge(v_free, vb + g + 1 + UNIT_V * u)
                            dve.tensor_tensor(x[:, m], x[:, m], tmp[:, :], ALU.add).then_inc(dve_done, 1)
                            dve.wait_ge(dve_done, d0 + m + 1 + KD * u)
                if l == 1:
                    n[0] += KD * N_UNITS[l]
                for m in range(KD):
                    dve.sem_inc(x_ready, 1)
            norm("norm_f", 2 * DEPTH, lambda k: final[:, k:k + 1])

        @block.tensor
        def _(pe):
            def chunk(key):
                slot, n, _ = plan.chunks[key]
                pe.wait_ge(landed[slot], n)
                return ring[slot]

            def a_take(key):
                b, _, need = A.of[key]
                if need:
                    pe.wait_ge(a_free, need)
                return a_bank[b]

            def v_take(key):
                b, _, need = V.of[key]
                if need:
                    pe.wait_ge(v_free, need)
                return v_bank[b]

            def product(out, w, rhs, full):
                for k, (a, b) in enumerate(zip(w, rhs)):
                    mm = pe.matmul(out, a, b, start=(k == 0), stop=(k == len(w) - 1))
                mm.then_inc(full, 1)

            hk = [hn[:, k] for k in range(KD)]

            def norm(key, r):
                out = a_take(key)[:, 0:T]
                for k in range(KD):
                    pe.wait_ge(sq_ready, 8 * r + k + 1)
                    mm = pe.matmul(out, ones[:, :], hn[:, k], start=(k == 0), stop=(k == KD - 1))
                mm.then_inc(a_full, 1)

            def project(name, l, m):
                w = chunk((name, l, m // 2))[:, 0:2048].rearrange("p (k n) -> p k n", k=KD)
                c = P * (m % 2)
                product(a_take((name, l, m))[:, 0:T], [w[:, k, c:c + P] for k in range(KD)], hk, a_full)

            def step(l, k, m, src, ready):
                w = chunk(("step", l, k, m // 2))[:, :].rearrange("p (k n) -> p k n", k=KD + KB)
                c = P * (m % 2)
                product(a_take(("gate", l, k, m))[:, 0:T], [w[:, i, c:c + P] for i in range(KD)], hk, a_full)
                out = v_take(("branch", l, k, m))[:, 0:T]
                if m == 0:
                    ready()
                product(out, [w[:, KD + i, c:c + P] for i in range(KB)], [src[:, i] for i in range(KB)], v_full)

            pe.wait_ge(const_ready, 3)
            for l in range(DEPTH):
                norm(("norm1", l), 2 * l)
                pe.wait_ge(hn_ready, 8 * (2 * l + 1))
                for m in range(KB):
                    project("uc", l, m)
                pe.wait_ge(bbar_ready, 4 * (l + 1))
                for c in range(2):
                    out = a_take(("bt", l, c))
                    for ct in range(4):
                        mm = pe.transpose(out[:, P * ct:P * ct + P],
                                          bbar[:, c, 4 * ct:4 * ct + 4, :].rearrange("p s h -> p (s h)"), ident[:, :])
                    mm.then_inc(a_full, 1)
                for j in range(2):
                    w = chunk(("va", l, j))[:, 0:2048].rearrange("p (k n) -> p k n", k=KD)
                    for b, (t0, tw) in enumerate(TOKS):
                        product(a_take(("va", l, j, b))[0:tw, 0:256], [hn[:, k, t0:t0 + tw] for k in range(KD)],
                                [w[:, k, :] for k in range(KD)], a_full)
                for m in range(KB):
                    project("xb", l, m)

                def s5_in(s):
                    q = l * NST + s
                    if q:
                        pe.wait_ge(s5_free, q)
                    if s == 0:
                        pe.wait_ge(a_free, A.of[("bt", l, 1)][1] + 1)
                    j, ct = 32 * (s % 4), s // 4
                    pe.matmul(s5_bank[0][:, 0:T], bt[j:j + 32, 0, ct], uc[j:j + 32, ct], start=True, stop=True)
                    pe.matmul(s5_bank[1][:, 0:T], bt[j:j + 32, 1, ct], uc[j:j + 32, ct], start=True, stop=True)\
                        .then_inc(s5_full, 1)

                def s5_out_(s):
                    q = l * NST + s
                    pe.wait_ge(rot_ready, q + 1)
                    j = 32 * (s % 4)
                    if s % 4 == 0 and q:
                        pe.wait_ge(ys_ready, q // 4)
                    if s == 0:
                        pe.wait_ge(layer_prepared, 3 * (l + 1))
                    out = y_bank[j:j + 32, 0:T]
                    pe.matmul(out, mat("c_re", 512)[:, 32 * s:32 * s + 32], xs[:, q % 2, 0], start=True, stop=False)
                    pe.matmul(out, mat("c_im", 512)[:, 32 * s:32 * s + 32], xs[:, q % 2, 1], start=False, stop=True)\
                        .then_inc(y_full, 1)

                for s in range(NST + 2):
                    if s < 8:
                        project(("ua", "gb")[s // 4], l, s % 4)
                    elif s < NST:
                        step(l, 0, s - 8, ug, lambda: pe.wait_ge(ya_ready, l + 1))
                    if s == 3:
                        pe.wait_ge(xc_ready, l + 1)
                        for g in range(8):
                            w = mat(("wa", "wx")[g // 4], 512)[:, P * (g % 4):P * (g % 4) + P]
                            product(a_take(("ri", l, g))[:, 0:T], [w], [xc[:, g % 4]], a_full)
                    if s == 4:
                        pe.wait_ge(v_ready, l + 1)
                        pe.wait_ge(layer_prepared, 3 * (l + 1))
                        for h in range(H_A):
                            out = v_take(("mixed", l, h))
                            c = slice(P * h, P * h + P)
                            pe.matmul(out[:, 0:P], v_tok[:, 0, c], mat("ws", 512)[:, c], start=True, stop=True)
                            pe.matmul(out[:, P:SEQ], v_tok[:, 1, c], mat("ws", 512)[:, c], start=True, stop=True)
                            pe.matmul(out[:, SEQ:T], v_tok[0:64, 2, c], mat("ws_s", 256)[0:64, 64 * h:64 * h + 64],
                                      start=True, stop=True).then_inc(v_full, 1)
                    if s < NST:
                        s5_in(s)
                    if s >= 2:
                        s5_out_(s - 2)
                for m in range(KD):
                    step(l, 1, m, gbg, lambda: pe.wait_ge(yb_ready, l + 1))
                w = chunk(("glu", l))[:, 0:2048].rearrange("p (k n) -> p k n", k=KB)
                pe.wait_ge(z_ready, KB * (l + 1))
                for m in range(KB):
                    product(a_take(("glu", l, m))[:, 0:T], [w[:, k, P * m:P * m + P] for k in range(KB)],
                            [zc[:, k] for k in range(KB)], a_full)
                for m in range(KD):
                    step(l, 2, m, zc, lambda: pe.wait_ge(yc_ready, KB * (l + 1)))
                pe.wait_ge(acc_ready, KD * (l + 1))
                for m in range(KD):
                    w = chunk(("wo", l, m // 2))[:, 0:2048].rearrange("p (k n) -> p k n", k=KD)
                    c = P * (m % 2)
                    product(v_take(("wo", l, m))[:, 0:T], [w[:, k, c:c + P] for k in range(KD)],
                            [acc[:, k] for k in range(KD)], v_full)
                norm(("norm2", l), 2 * l + 1)
                pe.wait_ge(hn_ready, 8 * (2 * l + 2))
                if l == 1:
                    for b, (t0, tw) in enumerate(TOKS):
                        product(a_take(("logits", b))[0:tw, 0:NEXP], [hn[:, k, t0:t0 + tw] for k in range(KD)],
                                [router[:, k] for k in range(KD)], a_full)
                    pe.wait_ge(comb_ready, 1)
                    for e in range(NEXP):
                        out = a_take(("comb", e))
                        for b, (t0, tw) in enumerate(TOKS):
                            mm = pe.matmul(out[:, t0:t0 + tw], rt[0:tw, 0, b, e:e + 1].to_broadcast([tw, P]),
                                           ident[0:tw, 0:tw], start=True, stop=True)
                        mm.then_inc(a_full, 1)
                ab, vb, c0 = A.of[("unit", l)], V.of[("unit", l)], plan.chunks[("unit", l)]
                per_slot = 16 * UNIT_CHUNKS // SLOTS
                with pe.Fori(0, N_UNITS[l]) as u:
                    for f in range(FT):
                        w = ring[f % SLOTS][:, 0:2048].rearrange("p (k c n) -> p k c n", k=KD, c=2)
                        pe.wait_ge(landed[f % SLOTS], 16 * ((c0 + f) // SLOTS + 1) + per_slot * u)
                        pe.wait_ge(a_free, ab + (f - 2 if f >= 3 else 0) + UNIT_A * u)
                        product(a_bank[f % 3][:, 0:T], [w[:, k, 0] for k in range(KD)], hk, a_full)
                        pe.wait_ge(v_free, vb + (f - 1 if f >= 2 else 0) + UNIT_V * u)
                        product(v_bank[f % 2][:, 0:T], [w[:, k, 1] for k in range(KD)], hk, v_full)
                    for m in range(KD):
                        g, c = FT + m, FT + m // 2
                        w = ring[c % SLOTS][:, 0:2816].rearrange("p (k n) -> p k n", k=FT)
                        if m % 2 == 0:
                            pe.wait_ge(landed[c % SLOTS], 16 * ((c0 + c) // SLOTS + 1) + per_slot * u)
                        pe.wait_ge(v_free, vb + max(g - 1, FT) + UNIT_V * u)
                        o = P * (m % 2)
                        product(v_bank[g % 2][:, 0:T], [w[:, k, o:o + P] for k in range(FT)],
                                [hid[:, k] for k in range(FT)], v_full)
            norm("norm_f", 2 * DEPTH)


def kernel(x_prompt, x_sample, state_conv_b, state_lru_b, state_s5_re, state_s5_im, norm_mix_g, w_in, b_gate,
           a_ln_g, a_ln_b, a_ws, a_bs, b_conv_w, b_conv_b, b_wa, b_ba, b_wx, b_bx, b_lam, c_lam_re, c_lam_im,
           c_log_dt, c_b_re, c_b_im, c_c_re, c_c_im, c_d, c_glu_w, c_glu_b, w_branch, w_out, norm_ffn_g,
           ffn_w_gate, ffn_w_up, ffn_w_down, moe_router_w, moe_router_b, moe_w_gate, moe_w_up, moe_w_down,
           final_norm_g):
    import numpy as np
    import concourse.bacc as bacc
    from concourse.bass_utils import run_bass_kernel_spmd

    def host(a):
        return np.ascontiguousarray(a)

    L = DEPTH

    def vec(a):
        return host(a).reshape(L, -1, P).transpose(2, 0, 1)

    def state(a):
        a = host(a)
        a = a.reshape((L, NST, P) + a.shape[3:])
        return a.transpose((2, 0, 1) + tuple(range(3, a.ndim)))

    x = np.concatenate([host(x_prompt)[0], host(x_sample).reshape(-1, D)])
    arrays = {"x": x.T.reshape(KD, P, T).transpose(1, 0, 2)}
    log_dt = np.broadcast_to(host(c_log_dt)[:, :, None], (L, 32, 64))
    parts = {
        "g_mix": vec(norm_mix_g), "g_ffn": vec(norm_ffn_g), "b_gate": vec(b_gate),
        "conv_w": vec(host(b_conv_w).reshape(L, -1)), "conv_b": vec(b_conv_b), "ba": vec(b_ba), "bx": vec(b_bx),
        "lam": vec(b_lam), "c_d": vec(c_d), "glu_b": vec(c_glu_b), "lam_re": state(c_lam_re),
        "lam_im": state(c_lam_im), "log_dt": state(log_dt),
        "lru_h0": host(state_lru_b).reshape(L, NSEQ, KB, P).transpose(3, 0, 2, 1).reshape(P, L, -1)}
    arrays["small"] = np.concatenate([parts[k] for k in SM], axis=2)
    arrays["final"] = host(final_norm_g).reshape(KD, P).T
    arrays["router"] = host(moe_router_w)[0].reshape(KD, P, NEXP).transpose(1, 0, 2)
    arrays["rb"] = host(moe_router_b)

    f = np.float32
    cblk = {k: np.zeros((P, L, NST, 2, HG), f) for k in ("c_re", "c_im")}
    for k, a in (("c_re", c_c_re), ("c_im", c_c_im)):
        a = host(a).reshape(L, NST, 2, HG, 64)
        for g in range(2):
            cblk[k][64 * g:64 * g + 64, :, :, g] = a[:, :, g].transpose(3, 0, 1, 2)
    wblk = {k: np.zeros((P, L, KB, P), f) for k in ("wa", "wx")}
    for k, a in (("wa", b_wa), ("wx", b_wx)):
        a = host(a).reshape(L, KB, 2, 64, 64)
        for g in range(2):
            wblk[k][64 * g:64 * g + 64, :, :, 64 * g:64 * g + 64] = a[:, :, g].transpose(2, 0, 1, 3)
    wst = host(a_ws).transpose(3, 0, 1, 2)
    wss = np.zeros((P, L, H_A, NSEQ, TS), f)
    for b in range(NSEQ):
        wss[TS * b:TS * b + TS, :, :, b] = wst[0:TS, :, :, 0:TS]
    mats = {
        "b_re": state(c_b_re), "b_im": state(c_b_im), **cblk, "ws": wst, "ws_s": wss, **wblk,
        "h0_re": state(host(state_s5_re).transpose(0, 2, 3, 1)), "h0_im": state(host(state_s5_im).transpose(0, 2, 3, 1)),
        "conv": host(state_conv_b).reshape(L, NSEQ, 3, KB, P).transpose(4, 0, 3, 1, 2)}
    arrays["pl"] = np.concatenate([host(mats[k]).reshape(P, L, -1) for k in PL], axis=2).transpose(1, 0, 2)
    arrays["rows"] = np.stack([host(a_ln_g), host(a_ln_b), host(a_bs).reshape(L, -1)], axis=1)

    def chunks(w, width):
        w = host(w)
        return w.reshape(w.shape[0], -1, P, w.shape[2] // width, width).transpose(0, 3, 2, 1, 4)

    win = chunks(w_in, 256)
    order = [8, 9, 2, 3, 4, 5, 0, 1, 6, 7]
    arrays["w_proj"] = win[:, order]
    br = host(w_branch)
    br = br.reshape(L, 3, KB, P, 4, 256).transpose(0, 1, 4, 3, 2, 5).reshape(L, 12, P, KB, 256)
    arrays["w_step"] = np.concatenate([win[:, 10:22], br], axis=3)
    arrays["w_glu"] = chunks(c_glu_w, DB)[:, 0]
    arrays["w_wo"] = chunks(w_out, 256)

    def cols(w):
        return w.reshape(-1, KD, P, FT, P).transpose(3, 0, 2, 1, 4)[:, :, :, :, None]

    def dense(w):
        return host(w)[0].reshape(D, 2, FT * P).transpose(1, 0, 2)

    gate = np.concatenate([dense(ffn_w_gate), host(moe_w_gate)[0]])
    up = np.concatenate([dense(ffn_w_up), host(moe_w_up)[0]])
    down = np.concatenate([host(ffn_w_down)[0].reshape(2, FT * P, D), host(moe_w_down)[0]])
    arrays["w_gu"] = np.concatenate([cols(gate), cols(up)], axis=4)
    arrays["w_dn"] = down.reshape(-1, FT, P, 4, 256).transpose(3, 0, 2, 1, 4)

    shapes = {"x": (P, KD, T), "small": (P, L, NSM), "final": (P, KD), "router": (P, KD, NEXP), "rb": (1, NEXP),
              "pl": (L, P, NPL), "rows": (L, 3, DB), "w_proj": (L, 10, P, 2048), "w_step": (L, 12, P, 3072),
              "w_glu": (L, P, 2048), "w_wo": (L, 4, P, 2048), "w_gu": (FT, 2 + NEXP, P, 2048),
              "w_dn": (4, 2 + NEXP, P, 2816)}
    outs = {"y": (P, KD * T), "va": (L, 64, DB), "conv": (L, P, KB * NLAST * 3), "lru": (L, P, KB * NLAST),
            "s5": (L, P, 2 * NST * NLAST)}
    nc = bacc.Bacc("TRN2", target_bir_lowering=False, num_devices=1)
    feed, args = {}, []
    for name, shape in shapes.items():
        feed[f"{name}_in"] = host(arrays[name]).reshape(shape)
        args.append(nc.dram_tensor(f"{name}_in", shape, F32, kind="ExternalInput").ap())
    for name, shape in outs.items():
        args.append(nc.dram_tensor(f"{name}_out", shape, F32, kind="ExternalOutput").ap())
    build(nc, *args)
    got = run_bass_kernel_spmd(nc, [feed], core_ids=[0]).results[0]

    y = got["y_out"].reshape(P, KD, T).transpose(2, 1, 0).reshape(T, D)
    va = got["va_out"].reshape(L, NSEQ, TS, DB)
    conv = got["conv_out"].reshape(L, P, KB, NLAST, 3).transpose(0, 3, 4, 2, 1).reshape(L, NLAST, 3, DB)
    lru = got["lru_out"].reshape(L, P, KB, NLAST).transpose(0, 3, 2, 1).reshape(L, NLAST, DB)
    s5 = got["s5_out"].reshape(L, P, 2, NST, NLAST).transpose(2, 0, 4, 3, 1).reshape(2, L, NLAST, 32, 64)
    return (host(y[None, 0:SEQ]), host(y[SEQ:].reshape(NSEQ, TS, D)), host(conv[:, 0:1]), host(lru[:, 0:1]),
            host(s5[0][:, 0:1]), host(s5[1][:, 0:1]), host(va), host(conv[:, 1:]), host(lru[:, 1:]),
            host(s5[0][:, 1:]), host(s5[1][:, 1:]))
```

```python
from contextlib import ExitStack

import concourse.bass as bass
from concourse import mybir

ALU = mybir.AluOpType
ACT = mybir.ActivationFunctionType
F32 = mybir.dt.float32
F32R = mybir.dt.float32r
AX_X = mybir.AxisListType.X

P = 128
D, DEPTH, SEQ, NSEQ, TS = 1024, 2, 256, 8, 8
T = SEQ + NSEQ * TS
KD = D // P
DB = D // 2
KB = DB // P
CONVW = 4
SEG = CONVW - 1 + TS
XB = CONVW - 1 + SEQ + NSEQ * SEG
H_A = 4
NST = 16
HG = 16
NEXP = 8
FT = 11
EPS = 1e-6
TOKS = (0, 128, 192)
NLAST = 1 + NSEQ
RAW, WHOLE, CHUNK = 3, 2, 1024
SPLIT = 3
URAW, UCHUNK = 5, FT * P
N_UNITS = 2
UNIT_G, UNIT_A, UNIT_V = 2 * FT + KD, FT, FT + KD

SLOTS = 128
BLK = FT * P // 4
QTR = D // 4
MCHUNK = KD * BLK
assert MCHUNK == FT * QTR
N_CHUNK = 12
MRAW, MSPLIT = 4, 3
BLK_TILES = [[k for k in range(FT) if b * BLK < P * (k + 1) <= (b + 1) * BLK] for b in range(4)]
SMALLS = ["PS", "S", "T0", "T1", "T2", "G0", "T3", "Sc0", "Sc1", "Sc2", "Sc3", "G1", "Sc4", "Sc5", "Sc6", "Sc7"]
SMALLS_LAST = [k for k in SMALLS if k[0] != "G"]
ITEM_S = len(SMALLS)
ROUND_S = 2 + ITEM_S * (NEXP - 1) + len(SMALLS_LAST)
ROUNDS = -(-T // SLOTS)

SM = {}
_n = 0
for _name, _w in (("g_mix", 8), ("g_ffn", 8), ("b_gate", 24), ("conv_w", 16), ("conv_b", 4), ("ba", 4), ("bx", 4),
                  ("lam", 4), ("c_d", 4), ("glu_b", 4), ("lam_re", 16), ("lam_im", 16), ("log_dt", 16), ("lru_h0", 32)):
    SM[_name] = _n
    _n += _w
NSM = _n
N_HALF = SM["lam_re"]
PL = {}
_n = 0
for _name, _w in (("b_re", 256), ("b_im", 256), ("c_re", 512), ("c_im", 512), ("ws", 512), ("ws_s", 256), ("wa", 512),
                  ("wx", 512), ("h0_re", 128), ("h0_im", 128), ("conv", 96)):
    PL[_name] = _n
    _n += _w
NPL = _n


class Ring:

    def __init__(self, banks):
        self.banks, self.n, self.drained, self.of = banks, 0, {}, {}

    def take(self, key):
        b = self.n % self.banks
        self.of[key] = (b, self.n, self.drained.get(b, 0))
        self.n += 1
        self.drained[b] = self.n

    def loop(self, key, per, times):
        self.of[key] = self.n
        self.n += per * times
        self.drained = {b: self.n for b in range(self.banks)}


class Plan:

    def __init__(self):
        self.a, self.v = Ring(3), Ring(2)
        self.chunks, self.order = {}, []
        self.loads = {"split": [], "whole": []}
        self.split, self.reader = {}, {}
        self.n_split = self.n_half = 0
        for l in range(DEPTH):
            self.layer(l)
        self.a.take("norm_f")
        for c, key in enumerate(self.loads["split"]):
            self.chunks[key] = (c % RAW, 16 * (c // RAW + 1), ("lo", self.split[self.loads["split"][c - RAW]] + 1) if c >= RAW else None)
        whole = self.loads["whole"]
        for c, (key, last) in enumerate(whole):
            freed = None
            if c >= WHOLE:
                last = whole[c - WHOLE][1]
                freed = ("a" if last[0] == "glu" else "v", self.count(last))
            self.chunks[key] = (RAW + c % WHOLE, 16 * (c // WHOLE + 1), freed)
        for l in range(DEPTH):
            self.merge(l)

    def merge(self, l):
        split = [k for k in self.loads["split"] if k[1] == l]
        whole = [k for k, _ in self.loads["whole"] if k[1] == l]
        freed = [-5, -5] + [{"branch": lambda k: 8 * k[2] + 2 * k[3] + 1, "glu": lambda k: 15,
                             "wo": lambda k: 24}[k[0]](k) for k in whole]
        gates = [k for k in split if k[0] == "gate"]
        todo = list(zip(whole, freed))
        for k in split:
            while k in gates and todo and todo[0][1] + 5 <= gates.index(k):
                self.order.append(todo.pop(0)[0])
            self.order.append(k)
        self.order += [k for k, _ in todo]

    def count(self, key):
        return (self.a if key in self.a.of else self.v).of[key][1] + 1

    def split_chunk(self, key, reader):
        self.loads["split"].append(key)
        self.split[key] = self.n_split
        self.reader[self.n_split] = reader
        self.n_split += 1

    def layer(self, l):
        a, v = self.a, self.v
        self.first = self.n_split
        a.take(("norm1", l))
        for m in range(KB):
            a.take(("uc", l, m))
            self.split_chunk(("uc", l, m), ("a", a.n))
        for c in range(2):
            a.take(("bt", l, c))
        for j in range(2):
            for b in range(3):
                a.take(("va", l, j, b))
            self.n_half += 1
            self.split_chunk(("va", l, j, 0), ("half", self.n_half))
            self.split_chunk(("va", l, j, 1), ("a", a.n))
        for m in range(KB):
            a.take(("xb", l, m))
            self.split_chunk(("xb", l, m), ("a", a.n))
        for s in range(NST):
            if s < 8:
                key = (("ua", "gb")[s // 4], l, s % 4)
                a.take(key)
                self.split_chunk(key, ("a", a.n))
            else:
                self.step(l, 0, s - 8)
            if s == 3:
                for g in range(8):
                    a.take(("ri", l, g))
            if s == 4:
                for h in range(H_A):
                    v.take(("mixed", l, h))
        for m in range(KD):
            self.step(l, 1, m)
        for m in range(KB):
            a.take(("glu", l, m))
            if m % 2:
                self.loads["whole"].append((("glu", l, m // 2), ("glu", l, m)))
        for m in range(KD):
            self.step(l, 2, m)
        for m in range(KD):
            v.take(("wo", l, m))
            self.loads["whole"].append((("wo", l, m), ("wo", l, m)))
        a.take(("norm2", l))
        if l == 1:
            a.take(("logits_t",))
            a.take(("logits",))
            for i in range(12):
                a.take(("tok", i))
            self.moe_v, self.moe_split = v.n, self.n_split
            return
        a.loop(("unit", l), UNIT_A, N_UNITS)
        v.loop(("unit", l), UNIT_V, N_UNITS)
        self.split[("unit", l)] = self.n_split
        self.n_split += UNIT_G * N_UNITS
        for k in range(SPLIT):
            self.reader[self.n_split - SPLIT + k] = ("v", v.n - (SPLIT - 1 - k))

    def step(self, l, k, m):
        self.a.take(("gate", l, k, m))
        self.split_chunk(("gate", l, k, m), ("a", self.a.n))
        self.v.take(("branch", l, k, m))
        if m % 2 == 0:
            self.loads["whole"].append((("branch", l, k, m // 2), ("branch", l, k, m + 1)))


def build(nc, x_in, small_in, final_in, router_in, rb_in, pl_in, rows_in, w_in, w_br, w_glu, w_wo, w_gu, w_dn, w_moe,
          y_out, va_out, conv_out, lru_out, s5_out):
    plan = Plan()
    A, V = plan.a, plan.v

    with ExitStack() as ctx:
        at = [-(-nc.sbuf_base // 32) * 32]

        def sb(name, shape, dt=F32, where=None):
            size = 4
            for w in shape[1:]:
                size *= w
            t = nc.alloc_sbuf_tensor_at(name, shape, dt, offset=at[0] if where is None else where)
            if where is None:
                at[0] += -(-size // 32) * 32
            return t

        def sem(name):
            return ctx.enter_context(nc.semaphore(name))

        x = sb("x", [P, KD, T])
        hn_at = at[0]
        hn_hi, hn_lo = sb("hn_hi", [P, KD, T], F32R), sb("hn_lo", [P, KD, T], F32R)
        small = sb("small", [P, DEPTH, NSM])
        half = sb("half", [P, DEPTH, N_HALF])
        final = sb("final", [P, KD])
        router = sb("router", [P, KD, NEXP])
        router_w = sb("router_w", [P, 2 * KD * NEXP + P - NEXP], F32R)
        router_hi, router_lo = (router_w[:, i * KD * NEXP:(i + 1) * KD * NEXP].rearrange("p (k e) -> p k e", e=NEXP)
                                for i in range(2))
        rb = sb("rb", [P, NEXP])
        ones = sb("ones", [P, P])
        ident = sb("ident", [P, P])
        mask = sb("mask", [P, T])
        eps = sb("eps", [P, 1])
        rs = sb("rs", [P, T])
        tmp = sb("tmp", [P, T])
        sp = sb("sp", [P, 21, DEPTH * NST])
        lg = sb("lg", [P, 3, NEXP])
        rt = sb("rt", [P, 6, 3, NEXP])
        rm = sb("rm", [P, 8, 3])
        revidx = sb("revidx", [P, NEXP])
        pl_at = at[0]
        pl = sb("pl", [P, NPL])
        bs_row = sb("bs_row", [P, DB])
        raw = [sb(f"raw{i}", [P, CHUNK]) for i in range(RAW + WHOLE)]
        w_hi = [sb(f"w_hi{i}", [P, CHUNK], F32R) for i in range(SPLIT)]
        w_lo = [sb(f"w_lo{i}", [P, CHUNK], F32R) for i in range(SPLIT)]
        th_at = at[0]
        th = sb("th", [P, 2, T])
        ah0 = sb("ah0", [P, 2, NST, NSEQ])
        ah_t = sb("ah_t", [P, NST, NSEQ])
        bnst = sb("bnst", [P, 3, 6])
        mv = sb("mv", [P, 3, 2])
        lnr = sb("lnr", [P, 3])
        s5_last = sb("s5_last", [P, 2, NST, NLAST])
        lru_last = sb("lru_last", [P, KB, NLAST])
        conv_last = sb("conv_last", [P, KB, NLAST * (CONVW - 1)])
        e_at = at[0]
        E = sb("E", [P, 2, NST, SEQ])
        mix_at = at[0]
        mix = sb("mix", [P, 7936])
        bbar = sb("bbar", [P, 2, NST, 2 * HG], where=mix_at + 4 * 2560)
        ln_rows = sb("ln_rows", [P, 2, DB], where=mix_at + 4 * 3840)
        squares = sb("squares", [P, KD, T], where=mix_at)
        y_fin = sb("y_fin", [P, KD, T], where=mix_at + 4 * 2560)
        acc_at = at[0]
        acc = sb("acc", [P, KD, T])
        xbuf = sb("xbuf", [P, KB, XB])
        z = sb("z", [P, 2, 2, T])
        xs = sb("xs", [P, 2, 2, T])
        rot_v = sb("rot_v", [P, 2, T])
        rot_p = sb("rot_p", [P, 2, T])
        decay = sb("decay", [P, 2, T])
        bt = sb("bt", [P, 2, 4, P])
        def over(name, shape, dt, where):
            size = 4 * shape[1] * (shape[2] if len(shape) > 2 else 1)
            return sb(name, shape, dt, where), where + -(-size // 32) * 32

        uraw, cur = [], e_at
        for i in range(URAW):
            t, cur = over(f"uraw{i}", [P, UCHUNK], F32, cur)
            uraw.append(t)
        silu, cur = over("silu", [P, 3, T], F32, cur)
        assert cur <= mix_at
        hid_hi, cur = over("hid_hi", [P, FT, T], F32R, mix_at)
        hid_lo, cur = over("hid_lo", [P, FT, T], F32R, cur)
        assert cur <= acc_at
        cur, uw_hi, uw_lo = acc_at, [], []
        for i in range(SPLIT):
            t, cur = over(f"uw_hi{i}", [P, UCHUNK], F32R, cur)
            uw_hi.append(t)
            t, cur = over(f"uw_lo{i}", [P, UCHUNK], F32R, cur)
            uw_lo.append(t)
        assert cur <= at[0] <= nc.sbuf_usable_end, (cur, at[0], nc.sbuf_usable_end)
        cur, mraw, mw_hi, mw_lo = e_at, [None] * MRAW, [None] * MSPLIT, [None] * MSPLIT
        mraw[0], cur = over("mraw0", [P, MCHUNK], F32, cur)
        mraw[1], cur = over("mraw1", [P, MCHUNK], F32, cur)
        x_hi, cur = over("x_hi", [P, KD, SLOTS], F32R, cur)
        x_lo, cur = over("x_lo", [P, KD, SLOTS], F32R, cur)
        scat, cur = over("scat", [P, T], F32R, cur)
        assert cur <= mix_at
        disp, cur = over("disp", [P, 3, SLOTS], F32R, mix_at)
        hid, cur = over("hid", [P, FT * P], F32, cur)
        ht_hi, cur = over("ht_hi", [P, FT, SLOTS], F32R, cur)
        ht_lo, cur = over("ht_lo", [P, FT, SLOTS], F32R, cur)
        mraw[3], cur = over("mraw3", [P, MCHUNK], F32, cur)
        assert cur <= acc_at
        mraw[2], cur = over("mraw2", [P, MCHUNK], F32, acc_at)
        mw_hi[0], cur = over("mw_hi0", [P, MCHUNK], F32R, cur)
        mw_hi[1], cur = over("mw_hi1", [P, MCHUNK], F32R, cur)
        assert cur <= at[0]
        mw_hi[2], cur = over("mw_hi2", [P, MCHUNK], F32R, hn_at)
        ym_hi, cur = over("ym_hi", [P, D], F32R, cur)
        ym_lo, cur = over("ym_lo", [P, D], F32R, cur)
        assert cur <= hn_at + 8 * KD * T
        cur = pl_at
        for i in range(MSPLIT):
            mw_lo[i], cur = over(f"mw_lo{i}", [P, MCHUNK], F32R, cur)
        tok_hi, cur = over("tok_hi", [P, 3, D], F32R, cur)
        tok_lo, cur = over("tok_lo", [P, 3, D], F32R, cur)
        tok_hi, tok_lo = (t[:, :, :] for t in (tok_hi, tok_lo))
        before, cur = over("before", [P, P], F32, cur)
        slot_no, cur = over("slot_no", [P, SLOTS], F32, cur)
        ident_r, cur = over("ident_r", [P, P], F32R, cur)
        comb_hi, cur = over("comb_hi", [P, 3, NEXP], F32R, cur)
        comb_lo, cur = over("comb_lo", [P, 3, NEXP], F32R, cur)
        slot_w, cur = over("slot_w", [P, 1], F32, cur)
        busiest, cur = over("busiest", [P, 1], mybir.dt.int32, cur)
        assert cur <= th_at

        bank = [ctx.enter_context(nc.psum_tensor(f"bank{i}", [P, 512], F32)) for i in range(5)]
        s5_bank = ctx.enter_context(nc.psum_tensor("s5_bank", [P, 2, 512], F32))
        bank += [s5_bank[:, 0], s5_bank[:, 1], ctx.enter_context(nc.psum_tensor("bank7", [P, 512], F32))]
        a_bank, v_bank, y_bank = bank[0:3], bank[3:5], bank[7]

        def tiles(t, off, n=KB):
            return t[:, off:off + n * T].rearrange("p (k t) -> p k t", k=n)

        uc, xc, ug, gbg = (tiles(mix[:, :], i * KB * T) for i in range(4))
        v_tok = mix[:, 5120:6656].rearrange("p (b c) -> p b c", b=3)
        zc = tiles(mix[:, :], 5120)
        lru_i = tiles(mix[:, :], 6656)
        accf = acc[:, :, :].rearrange("p k t -> p (k t)")
        lru_a, lru_d = tiles(accf, 0), tiles(accf, KB * T)

        def sm(name, l, i=0, n=1, t=None):
            return (small if t is None else t)[:, l, SM[name] + i:SM[name] + i + n]

        def mat(name, n, **kw):
            return pl[:, PL[name]:PL[name] + n]

        def cst(row, l, i=0, n=NST):
            return sp[:, row, l * NST + i:l * NST + i + n]

        def with_e(t, c, s):
            e = E[:, c, s]
            return ((t[:, :, 0:SEQ], e.unsqueeze(1).to_broadcast([P, 2, SEQ])),
                    (t[:, :, SEQ:T].rearrange("p c (b t) -> p c b t", t=TS),
                     e[:, 0:TS].unsqueeze(1).unsqueeze(1).to_broadcast([P, 2, NSEQ, TS])))

        (R_DT, R_X, R_TH, R_M, R_Y, R_R, R_N, R_SH, R_SN, R_C1, R_CS, R_AR, R_AI, R_NR, R_CR, R_CI, R_T, R_T2,
         R_Q, R_E, R_L) = range(21)

        landed = [sem(f"landed{i}") for i in range(RAW + WHOLE)]
        ulanded = [sem(f"ulanded{i}") for i in range(URAW)]
        hi_ready, lo_ready = sem("hi_ready"), sem("lo_ready")
        half_read = sem("half_read")
        hid_hi_ready, hid_lo_ready = sem("hid_hi_ready"), sem("hid_lo_ready")
        xn_ready, hnh_ready = sem("xn_ready"), sem("hnh_ready")
        router_hi_ready = sem("router_hi_ready")
        x_loaded = sem("x_loaded")
        small_loaded = sem("small_loaded")
        layer_loaded, ln_loaded = sem("layer_loaded"), sem("ln_loaded")
        const_ready = sem("const_ready")
        layer_prepared = sem("layer_prepared")
        a_full, a_free = sem("a_full"), sem("a_free")
        v_full, v_free = sem("v_full"), sem("v_free")
        dve_done = sem("dve_done")
        act_done = sem("act_done")
        pool_done = sem("pool_done")
        consts_in = sem("consts_in")
        consts_act = sem("consts_act")
        decays_done = sem("decays_done")
        consts_done = sem("consts_done")
        x_ready = sem("x_ready")
        sq_ready = sem("sq_ready")
        hn_ready = sem("hn_ready")
        bbar_ready = sem("bbar_ready")
        var_ready, std_ready, v_ready = sem("var_ready"), sem("std_ready"), sem("v_ready")
        pads_ready = sem("pads_ready")
        xc_ready = sem("xc_ready")
        tanh_ready = sem("tanh_ready")
        dec_root = sem("dec_root")
        lru_ready = sem("lru_ready")
        ya_ready, yb_ready, yc_ready = sem("ya_ready"), sem("yb_ready"), sem("yc_ready")
        s5_full, s5_free = sem("s5_full"), sem("s5_free")
        decay_ready = sem("decay_ready")
        scan_ready, rot_ready = sem("scan_ready"), sem("rot_ready")
        y_full, ys_ready, z_ready = sem("y_full"), sem("ys_ready"), sem("z_ready")
        acc_ready = sem("acc_ready")
        diff_ready, ediff_ready, comb_ready = sem("diff_ready"), sem("ediff_ready"), sem("comb_ready")
        mlanded = [sem(f"mlanded{i}") for i in range(MRAW)]
        before_ready, ident_r_ready = sem("before_ready"), sem("ident_r_ready")
        chosen_ready, comb_hi_ready = sem("chosen_ready"), sem("comb_hi_ready")
        small_full, small_free = sem("small_full"), sem("small_free")
        key_ready, disp_ready, busiest_ready = sem("key_ready"), sem("disp_ready"), sem("busiest_ready")
        silu_ready = sem("silu_ready")
        round_begun = sem("round_begun")
        x_hi_ready, ht_hi_ready, ym_hi_ready = sem("x_hi_ready"), sem("ht_hi_ready"), sem("ym_hi_ready")
        stored, va_stored, y_stored = sem("stored"), sem("va_stored"), sem("y_stored")

        block = ctx.enter_context(nc.Block())

        first = [min(plan.split[k] for k in plan.chunks if k in plan.split and k[1] == l) for l in range(DEPTH)]
        count_of = {"a": a_full, "v": v_full, "lo": lo_ready, "half": half_read}

        def uloads(g):
            return 16 * (g // URAW + 1)

        def u_reader(l, g, u):
            ab, vb = A.of[("unit", l)], V.of[("unit", l)]
            if g < 0:
                return v_full, vb + g + 1 + UNIT_V * u
            if g >= 2 * FT:
                return v_full, vb + g - FT + 1 + UNIT_V * u
            return (v_full, vb + g // 2 + 1 + UNIT_V * u) if g % 2 else (a_full, ab + g // 2 + 1 + UNIT_A * u)

        wide_bank, small_bank = bank[0:4], bank[4:8]

        def of_round(r, c):
            return 1 + c + ROUND_S * r

        def small_no(r, u, name, last=False):
            i = (SMALLS_LAST if last else SMALLS).index(name)
            return of_round(r, 2 + i + ITEM_S * u), small_bank[(3 + i) % 4]

        def parted(it, c):
            return plan.moe_split + c + 1 + N_CHUNK * it

        def wide(it, c):
            return plan.moe_v + c + 1 + N_CHUNK * it

        def up_done(it, b):
            return plan.moe_v + b + 1 + 8 * it

        def down_done(it, q):
            return plan.moe_v + 4 + q + 1 + 8 * it

        def items(engine, r, item):
            with engine.Fori(0, NEXP - 1) as u:
                item(u, u if isinstance(r, int) and r == 0 else u + NEXP * r, False)
            item(NEXP - 1, (NEXP - 1) + NEXP * r, True)

        def rounds(engine, round_):
            round_(0)
            engine.wait_ge(busiest_ready, 1)
            most = engine.value_load(busiest[0:1, 0:1], min_val=0, max_val=T)
            with engine.If(most > SLOTS):
                with engine.Fori(1, ROUNDS) as r:
                    round_(r)

        @block.sync
        def _(sync):
            for l in range(DEPTH):
                for key in plan.order:
                    if key[1] != l:
                        continue
                    slot, _, freed = plan.chunks[key]
                    if freed:
                        sync.wait_ge(count_of[freed[0]], freed[1])
                    name, m = key[0], key[2]
                    tile = {"uc": 0, "xb": 8, "ua": 12, "gb": 16}
                    if name in tile:
                        src = w_in[l, tile[name] + m]
                    elif name == "va":
                        src = w_in[l, 4 + 2 * m + key[3]]
                    elif name == "gate":
                        src = w_in[l, 20 + 8 * m + key[3]]
                    elif name == "branch":
                        src = w_br[l, 4 * m + key[3]]
                    else:
                        src = (w_glu if name == "glu" else w_wo)[l, m]
                    sync.dma_start(raw[slot][:, :], src).then_inc(landed[slot], 16)
                sync.wait_ge(rot_ready, NST * (l + 1))
                if l == 0:
                    s0 = plan.split[("unit", l)]
                    with sync.Fori(0, N_UNITS) as u:
                        for g in range(UNIT_G):
                            sync.wait_ge(lo_ready, s0 + g + 1 - URAW + UNIT_G * u)
                            if g < 2 * FT:
                                dst, src = uraw[g % URAW][:, 0:KD * P], w_gu[g, bass.ds(u, 1)]
                            else:
                                dst, src = uraw[g % URAW][:, :], w_dn[g - 2 * FT, bass.ds(u, 1)]
                            sync.dma_start(dst, src.rearrange("u p n -> p (u n)")).then_inc(ulanded[g % URAW], 16)

            def item(u, it, last):
                for c in range(N_CHUNK):
                    sync.wait_ge(lo_ready, parted(it, c - MRAW))
                    if c in (2, 3):
                        sync.wait_ge(v_full, V.of[("wo", 1, KD - 1)][1] + 1)
                    src = w_moe[c, u] if isinstance(u, int) else w_moe[c, bass.ds(u, 1)].rearrange("u p n -> p (u n)")
                    sync.dma_start(mraw[c % MRAW][:, :], src).then_inc(mlanded[c % MRAW], 16)

            rounds(sync, lambda r: items(sync, r, item))
            sync.wait_ge(hn_ready, 8 * (2 * DEPTH + 1))
            sync.dma_start(y_out, y_fin[:, :, :].rearrange("p k t -> p (k t)")).then_inc(y_stored, 16)
            sync.wait_ge(y_stored, 16)
            sync.wait_ge(stored, 48 * DEPTH)
            sync.wait_ge(va_stored, 16 * DEPTH)

        @block.gpsimd
        def _(pool):
            n = [0]

            def chain(ins):
                n[0] += 1
                ins.then_inc(pool_done, 1)
                pool.wait_ge(pool_done, n[0])

            def load_layer(l):
                pool.dma_start(pl[:, :], pl_in[l]).then_inc(layer_loaded, 16)
                pool.dma_start(bs_row[:, :], rows_in[l, 2:3].to_broadcast([P, DB])).then_inc(layer_loaded, 16)

            def load_ln(l):
                for r in range(2):
                    pool.dma_start(ln_rows[:, r, :], rows_in[l, r:r + 1].to_broadcast([P, DB])).then_inc(ln_loaded, 16)

            pool.dma_start(small[:, :, :], small_in).then_inc(small_loaded, 16)
            load_layer(0)
            load_ln(0)
            pool.dma_start(final[:, :], final_in).then_inc(small_loaded, 16)
            pool.dma_start(router[:, :, :], router_in).then_inc(small_loaded, 16)
            pool.dma_start(rb[:, :], rb_in.to_broadcast([P, NEXP])).then_inc(small_loaded, 16)
            pool.memset(ones[:, :], 1.0).then_inc(const_ready, 1)
            pool.memset(eps[:, :], EPS).then_inc(const_ready, 1)
            chain(pool.memset(ident[:, :], 0.0))
            pool.affine_select(out=ident[:, :], in_=ident[:, :], compare_op=ALU.not_equal, fill=1.0, base=0,
                               pattern=[[-1, P]], channel_multiplier=1).then_inc(const_ready, 1)
            chain(pool.memset(mask[:, :], 1.0))
            pool.memset(mask[:, SEQ::TS], 0.0).then_inc(const_ready, 1)
            pool.memset(mv[:, :, :], 1.0).then_inc(const_ready, 1)
            pool.memset(lg[:, :, :], 0.0).then_inc(const_ready, 1)
            for e in range(NEXP):
                pool.memset(revidx[:, e:e + 1], float(NEXP - e)).then_inc(const_ready, 1)

            for l in range(DEPTH):
                if l:
                    pool.wait_ge(x_ready, 16 * (l - 1) + 8)
                    load_layer(l)
                pool.wait_ge(layer_loaded, 32 * (l + 1))
                ws = mat("ws", 512).rearrange("p (h t) -> p h t", h=H_A)
                pool.affine_select(out=ws, in_=ws, compare_op=ALU.is_ge, fill=0.0, base=0,
                                   pattern=[[0, H_A], [1, P]], channel_multiplier=-1).then_inc(layer_prepared, 1)
                wss = mat("ws_s", 256).rearrange("p (h t) -> p h t", h=H_A)
                pool.affine_select(out=wss, in_=wss, compare_op=ALU.is_ge, fill=0.0, base=64,
                                   pattern=[[0, H_A], [1, 64]], channel_multiplier=-1).then_inc(layer_prepared, 1)
                ci = mat("c_im", 512)
                pool.tensor_scalar(ci, ci, -1.0, 0.0, ALU.mult, ALU.add).then_inc(layer_prepared, 1)

                if l:
                    pool.wait_ge(x_ready, 16 * l)
                    load_ln(l)
                pool.wait_ge(v_ready, l + 1)
                pool.dma_start(va_out[l], v_tok[64:128, 2, :]).then_inc(va_stored, 16)

                pool.wait_ge(a_free, A.of[("xb", l, KB - 1)][1] + 1)
                pool.wait_ge(pads_ready, l + 1)
                if l:
                    pool.wait_ge(stored, 48 * l)
                chain(pool.tensor_copy(conv_last[:, :, 0:3], xbuf[:, :, SEQ:SEQ + 3]))
                seg = xbuf[:, :, 3 + SEQ:].rearrange("p k (b s) -> p k b s", s=SEG)
                for k in range(KB):
                    chain(pool.tensor_copy(conv_last[:, k, 3:].rearrange("p (b s) -> p b s", s=3), seg[:, k, :, TS:SEG]))
                pool.dma_start(conv_out[l], conv_last[:, :, :].rearrange("p k n -> p (k n)")).then_inc(stored, 16)

                for s in range(NST):
                    q = l * NST + s
                    zq, xq = z[:, q % 2], xs[:, q % 2]
                    pool.wait_ge(scan_ready, 2 * q + 2)
                    if q >= 2:
                        pool.wait_ge(y_full, q - 1)
                    for out, c in ((xq, 0), (rot_p[:, :, :], 1)):
                        for (o, e), (i, _) in zip(with_e(out, c, s), with_e(zq, c, s)):
                            pool.tensor_tensor(o, i, e, ALU.mult).then_inc(pool_done, 1)
                            n[0] += 1
                    pool.wait_ge(pool_done, n[0])
                    pool.tensor_tensor(xq[:, 0], xq[:, 0], rot_p[:, 1], ALU.subtract).then_inc(pool_done, 1)
                    n[0] += 1
                    chain(pool.tensor_tensor(xq[:, 1], xq[:, 1], rot_p[:, 0], ALU.add))
                    pool.tensor_copy(s5_last[:, :, s, :], xq[:, :, SEQ - 1::TS]).then_inc(rot_ready, 1)
                pool.wait_ge(pool_done, n[0])
                pool.wait_ge(rot_ready, NST * (l + 1))
                pool.dma_start(s5_out[l], s5_last[:, :, :, :].rearrange("p c s n -> p (c s n)")).then_inc(stored, 16)
                pool.wait_ge(lru_ready, l + 1)
                pool.dma_start(lru_out[l], lru_last[:, :, :].rearrange("p k n -> p (k n)")).then_inc(stored, 16)
                pool.wait_ge(stored, 48 * (l + 1))
            pool.wait_ge(x_ready, 24)
            chain(pool.memset(before[:, :], 1.0))
            pool.affine_select(out=before[:, :], in_=before[:, :], compare_op=ALU.is_ge, fill=0.0, base=-1,
                               pattern=[[1, P]], channel_multiplier=-1).then_inc(before_ready, 1)

        @block.scalar
        def _(act):
            n = [0]

            def chain(ins):
                n[0] += 1
                ins.then_inc(act_done, 1)
                act.wait_ge(act_done, n[0])

            def evac(key, rows_, cols):
                b, q, _ = A.of[key]
                act.wait_ge(a_full, q + 1)
                return a_bank[b][0:rows_, 0:cols]

            def split(l, upto):
                while todo and plan.split[todo[0]] <= first[l] + upto and todo[0][1] == l:
                    key = todo.pop(0)
                    g = plan.split[key]
                    slot, loads, _ = plan.chunks[key]
                    act.wait_ge(landed[slot], loads)
                    reader = plan.reader.get(g - SPLIT)
                    if reader:
                        act.wait_ge(count_of[reader[0]], reader[1])
                    act.activation(w_hi[g % SPLIT][:, :], raw[slot][:, :], ACT.Copy).then_inc(hi_ready, 1)

            def norm(key, r):
                for k in range(KD):
                    if r:
                        act.wait_ge(x_ready, 8 * (r - 1) + k + 1)
                    act.activation(squares[:, k], x[:, k], ACT.Square).then_inc(sq_ready, 1)
                act.wait_ge(const_ready, 2)
                if r:
                    act.wait_ge(hn_ready, 8 * r)
                act.activation(rs[:, :], evac(key, P, T), ACT.Sqrt, bias=eps[:, :], scale=1.0 / D).then_inc(a_free, 1)
                if r < 2 * DEPTH:
                    for k in range(KD):
                        act.wait_ge(xn_ready, 8 * r + k + 1)
                        act.activation(hn_hi[:, k], squares[:, k], ACT.Copy).then_inc(hnh_ready, 1)

            todo = [k for k in plan.chunks if k in plan.split]
            todo.sort(key=plan.split.get)
            act.dma_start(x[:, :, :], x_in).then_inc(x_loaded, 16)
            act.wait_ge(small_loaded, 64)
            act.activation(sp[:, R_DT].rearrange("p (l n) -> p l n", l=DEPTH), small[:, :, SM["log_dt"]:SM["log_dt"] + NST],
                           ACT.Exp).then_inc(consts_act, 1)
            act.wait_ge(consts_in, 1)
            act.activation(sp[:, R_E, 0:8], sp[:, R_L, 0:8], ACT.Exp, scale=-1.0).then_inc(consts_act, 1)
            act.wait_ge(consts_in, 2)
            act.activation(sp[:, R_SH], sp[:, R_N], ACT.Sin, scale=0.5).then_inc(consts_act, 1)
            act.activation(sp[:, R_SN], sp[:, R_N], ACT.Sin).then_inc(consts_act, 1)
            act.wait_ge(x_loaded, 16)
            for l in range(DEPTH):
                if l == 0:
                    act.wait_ge(const_ready, 3)
                    act.activation(router_hi, router[:, :, :], ACT.Copy).then_inc(router_hi_ready, 1)
                    act.activation(router_w[:, 2 * KD * NEXP:], ident[:, 0:P - NEXP], ACT.Copy).then_inc(router_hi_ready, 1)
                split(l, 2)
                norm(("norm1", l), 2 * l)
                for m in range(KB):
                    split(l, m + 2)
                    act.activation(uc[:, m], evac(("uc", l, m), P, T), ACT.Copy).then_inc(a_free, 1)
                for c in range(2):
                    act.activation(bt[:, c].rearrange("p k n -> p (k n)"), evac(("bt", l, c), P, 512), ACT.Copy)\
                        .then_inc(a_free, 1)
                for j in range(2):
                    split(l, 7 + 2 * j)
                    for b in range(3):
                        act.activation(v_tok[:, b, 256 * j:256 * j + 256], evac(("va", l, j, b), P, 256),
                                       ACT.Gelu_apprx_tanh).then_inc(a_free, 1)
                for m in range(KB):
                    split(l, 10 + m)
                    src = evac(("xb", l, m), P, T)
                    chain(act.activation(xbuf[:, m, 3:3 + SEQ], src[:, 0:SEQ], ACT.Copy))
                    act.activation(xbuf[:, m, 3 + SEQ:].rearrange("p (b s) -> p b s", s=SEG)[:, :, 3:SEG],
                                   src[:, SEQ:T].rearrange("p (b s) -> p b s", s=TS), ACT.Copy).then_inc(a_free, 1)
                act.wait_ge(var_ready, l + 1)
                act.activation(lnr[:, :], mv[:, :, 1], ACT.Sqrt, bias=eps[:, :]).then_inc(std_ready, 1)

                def gate(k, m):
                    b, vq, _ = V.of[("branch", l, k, m)]
                    src = evac(("gate", l, k, m), P, T)
                    q = (l * 3 + k) * 8 + m
                    if q >= 2:
                        prev = (l * 3 + k) * 8 + m - 2
                        pk = ("branch", prev // 24, prev // 8 % 3, prev % 8)
                        act.wait_ge(v_free, V.of[pk][1] + 1)
                    act.activation(th[:, q % 2], src, ACT.Tanh, scale=0.5, bias=sm("b_gate", l, 8 * k + m, t=half))\
                        .then_inc(a_free, 1)

                def z_gelu(ct):
                    act.wait_ge(ys_ready, KB * l + ct + 1)
                    act.activation(zc[:, ct], zc[:, ct], ACT.Gelu_apprx_tanh).then_inc(z_ready, 1)

                def decay_of(s):
                    q = l * NST + s
                    if q >= 2:
                        act.wait_ge(scan_ready, 2 * q - 2)
                    act.activation(decay[:, q % 2], mask[:, :], ACT.Copy, scale=cst(R_R, l, s, 1)).then_inc(decay_ready, 1)

                if l == 0:
                    act.wait_ge(decays_done, 1)
                decay_of(0)
                decay_of(1)
                for s in range(NST):
                    split(l, 14 + s)
                    if s < 8:
                        name, dst = (("ua", ug), ("gb", gbg))[s // 4]
                        act.activation(dst[:, s % 4], evac((name, l, s % 4), P, T), ACT.Gelu_apprx_tanh).then_inc(a_free, 1)
                    else:
                        gate(0, s - 8)
                    if s == 3:
                        for g in range(8):
                            dst, bias = ((lru_a, "ba"), (lru_i, "bx"))[g // 4]
                            act.activation(dst[:, g % 4], evac(("ri", l, g), P, T), ACT.Tanh, scale=0.5,
                                           bias=sm(bias, l, g % 4, t=half)).then_inc(a_free, 1)
                        act.wait_ge(a_free, A.of[("ri", l, 7)][1] + 1)
                        if l == 0:
                            act.wait_ge(consts_done, 1)
                        for g in range(4):
                            q = sp[:, R_Q, 4 * l + g:4 * l + g + 1]
                            act.activation(lru_d[:, g], lru_a[:, g], ACT.Tanh, scale=q, bias=q).then_inc(act_done, 1)
                            n[0] += 1
                        for g in range(4):
                            q = sp[:, R_Q, 8 + 4 * l + g:8 + 4 * l + g + 1]
                            act.activation(lru_a[:, g], lru_a[:, g], ACT.Exp, scale=q, bias=q).then_inc(tanh_ready, 1)
                        act.wait_ge(act_done, n[0])
                        act.activation(lru_d, lru_d, ACT.Sqrt).then_inc(dec_root, 1)
                    if 1 <= s < NST - 1:
                        decay_of(s + 1)
                    if s >= 6 and (s - 6) % 4 == 0:
                        z_gelu((s - 6) // 4)
                z_gelu(3)
                for m in range(KD):
                    split(l, 30 + m)
                    gate(1, m)
                for m in range(KB):
                    act.activation(lru_i[:, m], evac(("glu", l, m), P, T), ACT.Tanh, scale=0.5,
                                   bias=sm("glu_b", l, m, t=half)).then_inc(a_free, 1)
                for m in range(KD):
                    split(l, 38 + m)
                    gate(2, m)
                norm(("norm2", l), 2 * l + 1)
                if l == 1:
                    act.activation(ident_r[:, :], ident[:, :], ACT.Copy).then_inc(ident_r_ready, 1)
                    act.activation(tmp[:, :], evac(("logits_t",), P, T), ACT.Copy).then_inc(a_free, 1)
                    act.activation(lg[:, :, :].rearrange("p b e -> p (b e)"), evac(("logits",), P, 3 * NEXP), ACT.Copy)\
                        .then_inc(a_free, 1)
                    act.wait_ge(diff_ready, 1)
                    act.activation(rm[:, 4, :], rm[:, 3, :], ACT.Exp).then_inc(ediff_ready, 1)
                    for i in range(12):
                        b, h = i % 6 // 2, i % 2
                        act.activation((tok_hi, tok_lo)[i // 6][:, b, 512 * h:512 * h + 512], evac(("tok", i), P, 512),
                                       ACT.Copy).then_inc(a_free, 1)
                    act.wait_ge(comb_ready, 1)
                    act.activation(comb_hi[:, :, :], rt[:, 0], ACT.Copy).then_inc(comb_hi_ready, 1)
                    continue
                ab, vb, s0 = A.of[("unit", l)], V.of[("unit", l)], plan.split[("unit", l)]
                hb = 0
                with act.Fori(0, N_UNITS) as u:
                    def usplit(g):
                        if g >= UNIT_G:
                            return
                        w = KD * P if g < 2 * FT else UCHUNK
                        act.wait_ge(ulanded[g % URAW], uloads(g) + 16 * (UNIT_G // URAW) * u)
                        act.wait_ge(*u_reader(l, g - SPLIT, u))
                        act.activation(uw_hi[g % SPLIT][:, 0:w], uraw[g % URAW][:, 0:w], ACT.Copy).then_inc(hi_ready, 1)

                    def hid_high(f):
                        act.wait_ge(v_free, vb + f + 1 + UNIT_V * u)
                        act.activation(hid_hi[:, f], silu[:, f % 3], ACT.Copy).then_inc(hid_hi_ready, 1)

                    usplit(0)
                    usplit(1)
                    for g in range(UNIT_G):
                        usplit(g + 2)
                        if g < 2 * FT and g % 2 == 0:
                            f = g // 2
                            act.wait_ge(a_full, ab + f + 1 + UNIT_A * u)
                            if f >= 3:
                                act.wait_ge(hid_lo_ready, hb + f - 2 + FT * u)
                            act.activation(silu[:, f % 3], a_bank[f % 3][:, 0:T], ACT.Silu).then_inc(a_free, 1)
                            if f:
                                hid_high(f - 1)
                        if g == 2 * FT - 1:
                            hid_high(FT - 1)

            def high(it, c):
                slot, loads = c % MRAW, 16 * (c // MRAW + 1) + 16 * (N_CHUNK // MRAW) * it
                act.wait_ge(mlanded[slot], loads)
                act.wait_ge(v_full, wide(it, c - MSPLIT))
                act.activation(mw_hi[c % MSPLIT][:, :], mraw[slot][:, :], ACT.Copy).then_inc(hi_ready, 1)

            def tokens_high(no, src, h):
                act.wait_ge(small_full, no + 1)
                act.activation(x_hi[:, 4 * h:4 * h + 4].rearrange("p k n -> p (k n)"), src[:, 0:4 * SLOTS], ACT.Copy)\
                    .then_inc(x_hi_ready, 1)

            def round_(r):
                if not isinstance(r, int):
                    high(NEXP * r, 0)
                    high(NEXP * r, 1)
                for h in range(2):
                    tokens_high(of_round(r, h), small_bank[1 + h], h)

                def item(u, it, last):
                    def silu_(b):
                        act.wait_ge(v_full, wide(it, 2 * b))
                        act.activation(hid[:, BLK * b:BLK * b + BLK], wide_bank[2 * b % 4][:, 0:BLK], ACT.Silu)\
                            .then_inc(silu_ready, 1)

                    def hidden_high(b):
                        no, src = small_no(r, u, f"T{b}", last)
                        act.wait_ge(small_full, no + 1)
                        k0, n = BLK_TILES[b][0], len(BLK_TILES[b])
                        act.activation(ht_hi[:, k0:k0 + n].rearrange("p k n -> p (k n)"), src[:, 0:n * SLOTS], ACT.Copy)\
                            .then_inc(ht_hi_ready, 1)

                    def result_high(q):
                        if q == 0:
                            act.wait_ge(small_free, small_no(r, u, "PS", last)[0] + 1)
                        act.wait_ge(v_full, wide(it, 8 + q))
                        act.activation(ym_hi[:, QTR * q:QTR * q + QTR], wide_bank[q][:, 0:QTR], ACT.Copy,
                                       scale=slot_w[:, 0:1]).then_inc(ym_hi_ready, 1)

                    for c in range(N_CHUNK):
                        if c in (1, 3, 5, 7):
                            silu_(c // 2)
                        if c in (4, 6, 8):
                            hidden_high(c // 2 - 2)
                        if c > 8:
                            result_high(c - 9)
                        if c + 2 < N_CHUNK:
                            high(it, c + 2)
                        elif not last:
                            high(it + 1, c + 2 - N_CHUNK)
                        if c == 8:
                            if not last:
                                tokens_high(*small_no(r, u, "G0"), 0)
                            hidden_high(3)
                    if not last:
                        tokens_high(*small_no(r, u, "G1"), 1)
                    result_high(3)

                items(act, r, item)

            for c in range(2):
                high(0, c)
            rounds(act, round_)
            norm("norm_f", 2 * DEPTH)

        @block.vector
        def _(dve):
            n = [0]

            def chain(ins):
                n[0] += 1
                ins.then_inc(dve_done, 1)
                dve.wait_ge(dve_done, n[0])

            todo = [k for k in plan.chunks if k in plan.split]
            todo.sort(key=plan.split.get)

            def split(l, upto):
                while todo and plan.split[todo[0]] <= first[l] + upto and todo[0][1] == l:
                    key = todo.pop(0)
                    g = plan.split[key]
                    slot = plan.chunks[key][0]
                    dve.wait_ge(hi_ready, g + 1)
                    dve.tensor_tensor(w_lo[g % SPLIT][:, :], raw[slot][:, :], w_hi[g % SPLIT][:, :].bitcast(F32),
                                      ALU.subtract).then_inc(lo_ready, 1)

            def norm(key, r, gain):
                b, q, _ = A.of[key]
                dve.wait_ge(a_free, q + 1)
                chain(dve.reciprocal(rs[:, :], rs[:, :]))
                def low(k):
                    dve.wait_ge(xn_ready, 8 * r + k + 1)
                    dve.wait_ge(hnh_ready, 8 * r + k + 1)
                    dve.tensor_tensor(hn_lo[:, k], squares[:, k], hn_hi[:, k].bitcast(F32), ALU.subtract).then_inc(hn_ready, 1)

                for k in range(KD):
                    if r == 2 * DEPTH:
                        dve.scalar_tensor_tensor(y_fin[:, k], x[:, k], gain(k), rs[:, :], ALU.mult, ALU.mult).then_inc(hn_ready, 1)
                        continue
                    dve.scalar_tensor_tensor(squares[:, k], x[:, k], gain(k), rs[:, :], ALU.mult, ALU.mult).then_inc(xn_ready, 1)
                    if k > 1:
                        low(k - 2)
                if r < 2 * DEPTH:
                    low(KD - 2)
                    low(KD - 1)

            def bc(ap, shape):
                return ap.unsqueeze(len(shape) - 1).to_broadcast(shape)

            row = lambda r: sp[:, r]

            dve.wait_ge(small_loaded, 64)
            chain(dve.tensor_scalar(half[:, :, :], small[:, :, 0:N_HALF], 0.5, None, ALU.mult))
            two = lambda r, w: sp[:, r, 0:DEPTH * w].rearrange("p (l n) -> p l n", l=DEPTH)
            lam = small[:, :, SM["lam"]:SM["lam"] + 4]
            l1, l2, l3, l4 = (sp[:, R_L, 8 * i:8 * i + 8] for i in range(4))
            ee = sp[:, R_E, 0:8]
            two4 = lambda v: v.rearrange("p (l n) -> p l n", l=DEPTH)
            chain(dve.tensor_scalar(two4(l2), lam, -1.0, None, ALU.mult))
            dve.tensor_tensor(two4(l1), two4(l2), lam, ALU.max).then_inc(consts_in, 1)
            dve.wait_ge(consts_act, 2)
            chain(dve.tensor_scalar(l3, ee, 2.0, None, ALU.add))
            chain(dve.reciprocal(l3, l3))
            chain(dve.tensor_tensor(l3, l3, ee, ALU.mult))
            chain(dve.tensor_tensor(l4, l3, l3, ALU.mult))
            chain(dve.tensor_scalar(ee, l4, 1.0 / 15, None, ALU.mult))
            for d in (13, 11, 9, 7, 5, 3):
                chain(dve.scalar_tensor_tensor(ee, ee, 1.0 / d, l4, ALU.add, ALU.mult))
            chain(dve.scalar_tensor_tensor(ee, ee, 1.0, l3, ALU.add, ALU.mult))
            chain(dve.tensor_scalar(l2, l2, 0.0, None, ALU.max))
            chain(dve.scalar_tensor_tensor(l1, ee, 2.0, l2, ALU.mult, ALU.add))
            chain(dve.tensor_scalar(sp[:, R_Q, 8:16], l1, -4.0, None, ALU.mult))
            dve.tensor_scalar(sp[:, R_Q, 0:8], l1, 2.0, None, ALU.mult).then_inc(consts_done, 1)

            lre, lim = (small[:, :, SM[k]:SM[k] + NST] for k in ("lam_re", "lam_im"))
            chain(dve.tensor_tensor(two(R_X, NST), lre, two(R_DT, NST), ALU.mult))
            chain(dve.tensor_tensor(two(R_TH, NST), lim, two(R_DT, NST), ALU.mult))
            chain(dve.tensor_scalar(row(R_N), row(R_TH), 0.15915494309189535, 12582912.0, ALU.mult, ALU.add))
            chain(dve.tensor_scalar(row(R_N), row(R_N), -12582912.0, None, ALU.add))
            chain(dve.scalar_tensor_tensor(row(R_TH), row(R_N), -6.28125, row(R_TH), ALU.mult, ALU.add))
            chain(dve.scalar_tensor_tensor(row(R_TH), row(R_N), -0.0019353071795864769, row(R_TH), ALU.mult, ALU.add))
            dve.tensor_scalar(row(R_N), row(R_TH), 3.1415925, -3.1415925, ALU.min, ALU.max).then_inc(consts_in, 1)
            chain(dve.tensor_scalar(row(R_Y), row(R_X), 1.0 / 64, None, ALU.mult))
            chain(dve.tensor_scalar(row(R_M), row(R_Y), 1.0 / 5040, None, ALU.mult))
            for c in (720, 120, 24, 6, 2, 1):
                chain(dve.scalar_tensor_tensor(row(R_M), row(R_M), 1.0 / c, row(R_Y), ALU.add, ALU.mult))
            for _ in range(6):
                chain(dve.scalar_tensor_tensor(row(R_M), row(R_M), 2.0, row(R_M), ALU.add, ALU.mult))
            dve.tensor_scalar(row(R_R), row(R_M), 1.0, None, ALU.add).then_inc(decays_done, 1)
            dve.wait_ge(decays_done, 1)
            dve.wait_ge(consts_act, 4)
            chain(dve.tensor_tensor(row(R_C1), row(R_SH), row(R_SH), ALU.mult))
            chain(dve.tensor_scalar(row(R_C1), row(R_C1), -2.0, None, ALU.mult))
            chain(dve.tensor_scalar(row(R_CS), row(R_C1), 1.0, None, ALU.add))
            chain(dve.tensor_tensor(row(R_AR), row(R_R), row(R_CS), ALU.mult))
            chain(dve.tensor_tensor(row(R_AI), row(R_R), row(R_SN), ALU.mult))
            chain(dve.tensor_tensor(row(R_NR), row(R_M), row(R_CS), ALU.mult))
            chain(dve.tensor_tensor(row(R_NR), row(R_NR), row(R_C1), ALU.add))
            chain(dve.tensor_tensor(two(R_T, NST), lre, lre, ALU.mult))
            chain(dve.tensor_tensor(two(R_T2, NST), lim, lim, ALU.mult))
            chain(dve.tensor_tensor(row(R_T), row(R_T), row(R_T2), ALU.add))
            chain(dve.reciprocal(row(R_T), row(R_T)))
            chain(dve.tensor_tensor(two(R_CR, NST), two(R_NR, NST), lre, ALU.mult))
            chain(dve.tensor_tensor(two(R_T2, NST), two(R_AI, NST), lim, ALU.mult))
            chain(dve.tensor_tensor(row(R_CR), row(R_CR), row(R_T2), ALU.add))
            chain(dve.tensor_tensor(row(R_CR), row(R_CR), row(R_T), ALU.mult))
            chain(dve.tensor_tensor(two(R_CI, NST), two(R_AI, NST), lre, ALU.mult))
            chain(dve.tensor_tensor(two(R_T2, NST), two(R_NR, NST), lim, ALU.mult))
            chain(dve.tensor_tensor(row(R_CI), row(R_CI), row(R_T2), ALU.subtract))
            chain(dve.tensor_tensor(row(R_CI), row(R_CI), row(R_T), ALU.mult))
            dve.wait_ge(const_ready, 14)
            dve.wait_ge(x_loaded, 16)
            dve.wait_ge(router_hi_ready, 1)
            chain(dve.tensor_tensor(router_lo, router[:, :, :], router_hi.bitcast(F32), ALU.subtract))

            for l in range(DEPTH):
                split(l, 2)
                norm(("norm1", l), 2 * l, lambda k: sm("g_mix", l, k))

                dve.wait_ge(layer_loaded, 32 * (l + 1))
                br, bi = (mat(k, 256).rearrange("p (s h) -> p s h", h=HG) for k in ("b_re", "b_im"))
                cr, ci = (bc(cst(r, l), [P, NST, HG]) for r in (R_CR, R_CI))
                chain(dve.memset(bbar[:, :, :, :], 0.0))
                t = [accf[:, 256 * i:256 * i + 256].rearrange("p (s h) -> p s h", h=HG) for i in range(4)]
                chain(dve.tensor_tensor(t[0], br, cr, ALU.mult))
                chain(dve.tensor_tensor(t[1], bi, ci, ALU.mult))
                chain(dve.tensor_tensor(t[2], br, ci, ALU.mult))
                chain(dve.tensor_tensor(t[3], bi, cr, ALU.mult))
                for c, op in ((0, ALU.subtract), (1, ALU.add)):
                    for g in range(2):
                        rng = slice(64 * g, 64 * g + 64)
                        dve.tensor_tensor(bbar[rng, c, :, HG * g:HG * g + HG], t[2 * c][rng], t[2 * c + 1][rng], op)\
                            .then_inc(bbar_ready, 1)
                dve.wait_ge(bbar_ready, 4 * (l + 1))

                split(l, 4)
                h0r, h0i = (mat(k, 128).rearrange("p (s b) -> p s b", b=NSEQ) for k in ("h0_re", "h0_im"))
                ar, ai = (bc(cst(r, l), [P, NST, NSEQ]) for r in (R_AR, R_AI))
                chain(dve.tensor_tensor(ah0[:, 0], h0r, ar, ALU.mult))
                chain(dve.tensor_tensor(ah_t[:, :, :], h0i, ai, ALU.mult))
                chain(dve.tensor_tensor(ah0[:, 0], ah0[:, 0], ah_t[:, :, :], ALU.subtract))
                chain(dve.tensor_tensor(ah0[:, 1], h0r, ai, ALU.mult))
                chain(dve.tensor_tensor(ah_t[:, :, :], h0i, ar, ALU.mult))
                chain(dve.tensor_tensor(ah0[:, 1], ah0[:, 1], ah_t[:, :, :], ALU.add))

                chain(dve.memset(E[:, 0, :, 0:1], 1.0))
                chain(dve.memset(E[:, 1, :, 0:1], 0.0))
                chain(dve.tensor_copy(E[:, 0, :, 1:2], cst(R_CS, l).unsqueeze(2)))
                chain(dve.tensor_copy(E[:, 1, :, 1:2], cst(R_SN, l).unsqueeze(2)))
                pr, pi, pt = row(R_X)[:, 0:NST], row(R_TH)[:, 0:NST], row(R_T)[:, 0:NST]
                w = 2
                while w < SEQ:
                    er, ei = E[:, 0, :, w // 2], E[:, 1, :, w // 2]
                    chain(dve.tensor_tensor(pr, er, er, ALU.mult))
                    chain(dve.tensor_tensor(pt, ei, ei, ALU.mult))
                    chain(dve.tensor_tensor(pr, pr, pt, ALU.subtract))
                    chain(dve.scalar_tensor_tensor(pi, er, 2.0, ei, ALU.mult, ALU.mult))
                    prb, pib = bc(pr, [P, NST, w]), bc(pi, [P, NST, w])
                    tt = accf[:, 0:NST * w].rearrange("p (s w) -> p s w", w=w)
                    lo_r, lo_i, hi_r, hi_i = E[:, 0, :, 0:w], E[:, 1, :, 0:w], E[:, 0, :, w:2 * w], E[:, 1, :, w:2 * w]
                    chain(dve.tensor_tensor(hi_r, lo_r, prb, ALU.mult))
                    chain(dve.tensor_tensor(tt, lo_i, pib, ALU.mult))
                    chain(dve.tensor_tensor(hi_r, hi_r, tt, ALU.subtract))
                    chain(dve.tensor_tensor(hi_i, lo_r, pib, ALU.mult))
                    chain(dve.tensor_tensor(tt, lo_i, prb, ALU.mult))
                    chain(dve.tensor_tensor(hi_i, hi_i, tt, ALU.add))
                    w *= 2
                    split(l, {4: 5, 8: 5, 16: 6, 32: 6, 64: 7, 128: 8, 256: 9}[w])

                seg = xbuf[:, :, 3 + SEQ:].rearrange("p k (b s) -> p k b s", s=SEG)
                cv = mat("conv", 96).rearrange("p (k b w) -> p k b w", k=KB, w=3)
                if l:
                    dve.wait_ge(stored, 48 * l)
                chain(dve.memset(xbuf[:, :, 0:CONVW - 1], 0.0))
                for k in range(KB):
                    chain(dve.tensor_copy(seg[:, k, :, 0:3], cv[:, k]))
                dve.sem_inc(pads_ready, 1)

                split(l, 10)
                dve.wait_ge(a_free, A.of[("va", l, 1, 2)][1] + 1)
                for b, w in enumerate((P, P, P)):
                    chain(dve.bn_stats(bnst[0:w, b], v_tok[0:w, b]))
                    if b < 2:
                        chain(dve.bn_aggr(mv[0:w, b], bnst[0:w, b]))
                    else:
                        dve.bn_aggr(mv[0:w, b], bnst[0:w, b]).then_inc(var_ready, 1)
                split(l, 12)
                dve.wait_ge(std_ready, l + 1)
                dve.wait_ge(ln_loaded, 32 * (l + 1))
                chain(dve.reciprocal(lnr[:, :], lnr[:, :]))
                for b, w in enumerate((P, P, P)):
                    vt = v_tok[0:w, b]
                    chain(dve.tensor_scalar(vt, vt, mv[0:w, b, 0:1], lnr[0:w, b:b + 1], ALU.subtract, ALU.mult))
                    chain(dve.tensor_tensor(vt, vt, ln_rows[0:w, 0], ALU.mult))
                    if b < 2:
                        chain(dve.tensor_tensor(vt, vt, ln_rows[0:w, 1], ALU.add))
                    else:
                        dve.tensor_tensor(vt, vt, ln_rows[0:w, 1], ALU.add).then_inc(v_ready, 1)
                dve.wait_ge(v_ready, l + 1)

                def s5(s):
                    q = l * NST + s
                    v, d = s5_bank[:, :, 0:T], z[:, q % 2]

                    if q >= 2:
                        dve.wait_ge(rot_ready, q - 1)
                    dve.wait_ge(s5_full, q + 1)
                    for c, out in enumerate((d, rot_v[:, :, :])):
                        for i, ((o, e), (a, _)) in enumerate(zip(with_e(out, c, s), with_e(v, c, s))):
                            mult = dve.tensor_tensor(o, a, e, ALU.mult)
                            if c and i:
                                mult.then_inc(s5_free, 1)
                            else:
                                mult.then_inc(dve_done, 1)
                                n[0] += 1
                    dve.wait_ge(dve_done, n[0])
                    dve.wait_ge(s5_free, q + 1)
                    dve.tensor_tensor(d[:, 0], d[:, 0], rot_v[:, 1], ALU.add).then_inc(dve_done, 1)
                    n[0] += 1
                    chain(dve.tensor_tensor(d[:, 1], d[:, 1], rot_v[:, 0], ALU.subtract))
                    chain(dve.tensor_tensor(d[:, :, SEQ::TS], d[:, :, SEQ::TS], ah0[:, :, s], ALU.add))
                    dve.wait_ge(decay_ready, q + 1)
                    for c in range(2):
                        dve.tensor_tensor_scan(d[:, c], decay[:, q % 2], d[:, c], 0.0, ALU.mult, ALU.add)\
                            .then_inc(scan_ready, 1)

                def conv():
                    for k in range(KB):
                        w = lambda i: sm("conv_w", l, 4 * i + k)
                        p_out = xc[:, k, 0:SEQ]
                        s_out = xc[:, k, SEQ:T].rearrange("p (b s) -> p b s", s=TS)
                        chain(dve.tensor_scalar(p_out, xbuf[:, k, 0:SEQ], w(0), sm("conv_b", l, k), ALU.mult, ALU.add))
                        chain(dve.tensor_scalar(s_out, seg[:, k, :, 0:TS], w(0), sm("conv_b", l, k), ALU.mult, ALU.add))
                        for i in range(1, CONVW):
                            chain(dve.scalar_tensor_tensor(p_out, xbuf[:, k, i:i + SEQ], w(i), p_out, ALU.mult, ALU.add))
                            chain(dve.scalar_tensor_tensor(s_out, seg[:, k, :, i:i + TS], w(i), s_out, ALU.mult, ALU.add))
                    dve.sem_inc(xc_ready, 1)

                def mixed():
                    for h in range(H_A):
                        b, q, _ = V.of[("mixed", l, h)]
                        src = v_bank[b]
                        dve.wait_ge(v_full, q + 1)
                        bs = bs_row[:, P * h:P * h + P]
                        chain(dve.tensor_tensor(tmp[:, 0:SEQ].rearrange("p (c t) -> p c t", c=2),
                                                src[:, 0:SEQ].rearrange("p (c t) -> p c t", c=2),
                                                bs.unsqueeze(1).to_broadcast([P, 2, P]), ALU.add))
                        dve.tensor_tensor(tmp[:, SEQ:T].rearrange("p (b t) -> p b t", t=TS),
                                          src[:, SEQ:T].rearrange("p (b t) -> p b t", t=TS),
                                          bs[:, 0:TS].unsqueeze(1).to_broadcast([P, NSEQ, TS]), ALU.add).then_inc(v_free, 1)
                        dve.wait_ge(v_free, q + 1)
                        dve.wait_ge(a_free, A.of[("ua", l, h)][1] + 1)
                        chain(dve.tensor_tensor(ug[:, h], tmp[:, :], ug[:, h], ALU.mult))
                    dve.sem_inc(ya_ready, 1)

                def lru():
                    chain(dve.scalar_tensor_tensor(lru_i, lru_i, 1.0, xc, ALU.add, ALU.mult))
                    dve.wait_ge(tanh_ready, 4 * (l + 1))
                    dve.wait_ge(dec_root, l + 1)
                    chain(dve.scalar_tensor_tensor(lru_d, lru_a, 1.0, lru_d, ALU.add, ALU.mult))
                    chain(dve.scalar_tensor_tensor(lru_i, lru_i, 0.5, lru_d, ALU.mult, ALU.mult))
                    a0, d0 = lru_a[:, :, SEQ::TS], lru_i[:, :, SEQ::TS]
                    t = ah_t[:, 0:KB, :]
                    chain(dve.tensor_tensor(t, a0, sm("lru_h0", l, 0, 32).rearrange("p (k b) -> p k b", b=NSEQ), ALU.mult))
                    chain(dve.tensor_tensor(d0, d0, t, ALU.add))
                    chain(dve.memset(a0, 0.0))
                    for k in range(KB):
                        chain(dve.tensor_tensor_scan(lru_d[:, k], lru_a[:, k], lru_i[:, k], 0.0, ALU.mult, ALU.add))
                    dve.tensor_copy(lru_last[:, :, :], lru_d[:, :, SEQ - 1::TS]).then_inc(lru_ready, 1)

                def branch(k, m):
                    b, q, _ = V.of[("branch", l, k, m)]
                    src = v_bank[b][:, 0:T]
                    g = th[:, ((l * 3 + k) * 8 + m) % 2]
                    dve.wait_ge(v_full, q + 1)
                    dve.wait_ge(a_free, A.of[("gate", l, k, m)][1] + 1)
                    dst = acc[:, m] if k == 0 else tmp[:, :]
                    dve.scalar_tensor_tensor(dst, g, 1.0, src, ALU.add, ALU.mult).then_inc(v_free, 1)
                    dve.wait_ge(v_free, q + 1)
                    if k == 1:
                        chain(dve.tensor_tensor(acc[:, m], acc[:, m], tmp[:, :], ALU.add))
                    if k == 2:
                        dve.scalar_tensor_tensor(acc[:, m], tmp[:, :], 0.5, acc[:, m], ALU.mult, ALU.add).then_inc(acc_ready, 1)
                        dve.wait_ge(acc_ready, KD * l + m + 1)

                def ys(ct):
                    dve.wait_ge(y_full, l * NST + 4 * ct + 4)
                    dve.scalar_tensor_tensor(zc[:, ct], uc[:, ct], sm("c_d", l, ct), y_bank[:, 0:T], ALU.mult, ALU.add)\
                        .then_inc(ys_ready, 1)

                for s in range(NST + 3):
                    split(l, 14 + min(s, NST - 1))
                    if s == 4:
                        mixed()
                    if s == 8:
                        dve.wait_ge(lru_ready, l + 1)
                        dve.wait_ge(a_free, A.of[("gb", l, 3)][1] + 1)
                        dve.tensor_tensor(gbg, gbg, lru_d, ALU.mult).then_inc(yb_ready, 1)
                        dve.wait_ge(yb_ready, l + 1)
                    if 8 <= s < NST:
                        branch(0, s - 8)
                    if s < NST:
                        s5(s)
                    if s == 0:
                        dve.wait_ge(a_free, A.of[("xb", l, 3)][1] + 1)
                        conv()
                    if s == 6:
                        lru()
                    if s >= 6 and (s - 6) % 4 == 0:
                        if s == 6:
                            dve.wait_ge(va_stored, 16 * (l + 1))
                        ys((s - 6) // 4)
                for m in range(KD):
                    split(l, 30 + m)
                    branch(1, m)
                dve.wait_ge(a_free, A.of[("glu", l, 3)][1] + 1)
                for m in range(KB):
                    dve.scalar_tensor_tensor(zc[:, m], lru_i[:, m], 1.0, zc[:, m], ALU.add, ALU.mult).then_inc(yc_ready, 1)
                for m in range(KD):
                    split(l, 38 + m)
                    branch(2, m)
                for m in range(KD):
                    b, q, _ = V.of[("wo", l, m)]
                    dve.wait_ge(v_full, q + 1)
                    dve.scalar_tensor_tensor(x[:, m], v_bank[b][:, 0:T], 0.5, x[:, m], ALU.mult, ALU.add).then_inc(v_free, 1)
                    dve.wait_ge(v_free, q + 1)
                    dve.sem_inc(x_ready, 1)
                norm(("norm2", l), 2 * l + 1, lambda k: sm("g_ffn", l, k))
                if l == 1:
                    dve.wait_ge(a_free, A.of[("logits",)][1] + 1)
                    full = [P, 3, NEXP]
                    rix = revidx[:, :].unsqueeze(1).to_broadcast(full)
                    for b in range(3):
                        chain(dve.tensor_tensor(lg[:, b], lg[:, b], rb[:, :], ALU.add))
                    k1, k2, t0, lg2 = rt[:, 0], rt[:, 1], rt[:, 2], rt[:, 3]
                    m1, m2, mx, df, ex, p1, p2 = (rm[:, i] for i in range(7))

                    def best(src, top, pick):
                        chain(dve.tensor_reduce(top, src, AX_X, ALU.max))
                        chain(dve.tensor_tensor(t0, src, bc(top, full), ALU.is_equal))
                        chain(dve.tensor_tensor(t0, t0, rix, ALU.mult))
                        chain(dve.tensor_reduce(mx, t0, AX_X, ALU.max))
                        chain(dve.tensor_tensor(pick, t0, bc(mx, full), ALU.is_equal))

                    best(lg[:, :, :], m1, k1)
                    chain(dve.scalar_tensor_tensor(lg2, k1, -3.0e38, lg[:, :, :], ALU.mult, ALU.add))
                    best(lg2, m2, k2)
                    chosen, key = rt[:, 4], rt[:, 5]
                    chain(dve.tensor_tensor(chosen, k1, k2, ALU.add))
                    dve.memset(chosen[0:64, 2], 0.0).then_inc(chosen_ready, 1)
                    dve.tensor_tensor(df, m2, m1, ALU.subtract).then_inc(diff_ready, 1)
                    dve.wait_ge(ediff_ready, 1)
                    chain(dve.tensor_scalar(p1, ex, 1.0, None, ALU.add))
                    chain(dve.reciprocal(p1, p1))
                    chain(dve.tensor_tensor(p2, ex, p1, ALU.mult))
                    chain(dve.tensor_tensor(k1, k1, bc(p1, full), ALU.mult))
                    chain(dve.tensor_tensor(k2, k2, bc(p2, full), ALU.mult))
                    dve.tensor_tensor(k1, k1, k2, ALU.add).then_inc(comb_ready, 1)
                    dve.wait_ge(small_full, 1)
                    places = small_bank[0][:, 0:3 * NEXP].rearrange("p (b e) -> p b e", e=NEXP)
                    dve.wait_ge(chosen_ready, 1)
                    chain(dve.scalar_tensor_tensor(key, places, 1.0, chosen, ALU.add, ALU.mult))
                    chain(dve.tensor_scalar(key, key, -1.0, None, ALU.add))
                    chain(dve.tensor_reduce(rm[:, 7, 0:1], small_bank[0][:, 3 * NEXP:4 * NEXP], AX_X, ALU.max))
                    dve.tensor_copy(busiest[:, :], rm[:, 7, 0:1]).then_inc(busiest_ready, 1)
                    dve.tensor_copy(slot_no[:, :], small_bank[0][:, 4 * NEXP:4 * NEXP + SLOTS]).then_inc(small_free, 1)
                    dve.wait_ge(small_free, 1)
                    dve.wait_ge(comb_hi_ready, 1)
                    chain(dve.tensor_tensor(comb_lo[:, :, :], k1, comb_hi[:, :, :].bitcast(F32), ALU.subtract))
                    continue
                ab, vb, s0 = A.of[("unit", l)], V.of[("unit", l)], plan.split[("unit", l)]
                hb = 0
                with dve.Fori(0, N_UNITS) as u:
                    def usplit(g):
                        if g >= UNIT_G:
                            return
                        w = KD * P if g < 2 * FT else UCHUNK
                        dve.wait_ge(hi_ready, s0 + g + 1 + UNIT_G * u)
                        dve.tensor_tensor(uw_lo[g % SPLIT][:, 0:w], uraw[g % URAW][:, 0:w],
                                          uw_hi[g % SPLIT][:, 0:w].bitcast(F32), ALU.subtract).then_inc(lo_ready, 1)

                    def hid_low(f):
                        dve.wait_ge(hid_hi_ready, hb + f + 1 + FT * u)
                        dve.wait_ge(v_free, vb + f + 1 + UNIT_V * u)
                        dve.tensor_tensor(hid_lo[:, f], silu[:, f % 3], hid_hi[:, f].bitcast(F32), ALU.subtract)\
                            .then_inc(hid_lo_ready, 1)

                    usplit(0)
                    usplit(1)
                    for g in range(UNIT_G):
                        usplit(g + 2)
                        if g < 2 * FT and g % 2:
                            f = g // 2
                            dve.wait_ge(a_free, ab + f + 1 + UNIT_A * u)
                            dve.wait_ge(v_full, vb + f + 1 + UNIT_V * u)
                            dve.tensor_tensor(silu[:, f % 3], silu[:, f % 3], v_bank[f % 2][:, 0:T], ALU.mult).then_inc(v_free, 1)
                            if f:
                                hid_low(f - 1)
                            if f == FT - 1:
                                hid_low(f)
                        if g >= 2 * FT:
                            m = g - 2 * FT
                            q = FT + m
                            dve.wait_ge(v_full, vb + q + 1 + UNIT_V * u)
                            dve.tensor_tensor(x[:, m], v_bank[q % 2][:, 0:T], x[:, m], ALU.add).then_inc(v_free, 1)
                            dve.wait_ge(v_free, vb + q + 1 + UNIT_V * u)
                for m in range(KD):
                    dve.sem_inc(x_ready, 1)

            def low(it, c):
                dve.wait_ge(hi_ready, parted(it, c))
                dve.tensor_tensor(mw_lo[c % MSPLIT][:, :], mraw[c % MRAW][:, :], mw_hi[c % MSPLIT][:, :].bitcast(F32),
                                  ALU.subtract).then_inc(lo_ready, 1)

            def tokens_low(no, src, r, i, h):
                dve.wait_ge(x_hi_ready, 1 + i + 2 * NEXP * r)
                dve.wait_ge(small_full, no + 1)
                k = slice(4 * h, 4 * h + 4)
                dve.tensor_tensor(x_lo[:, k].rearrange("p k n -> p (k n)"), src[:, 0:4 * SLOTS],
                                  x_hi[:, k].rearrange("p k n -> p (k n)").bitcast(F32), ALU.subtract)\
                    .then_inc(small_free, 1)

            def dispatch(key):
                full = [P, 3, SLOTS]
                dve.tensor_tensor(disp[:, :, :], slot_no[:, :].unsqueeze(1).to_broadcast(full), key.to_broadcast(full),
                                  ALU.is_equal).then_inc(disp_ready, 1)

            def round_(r):
                if not isinstance(r, int):
                    dve.tensor_scalar(rt[:, 5], rt[:, 5], float(-SLOTS), None, ALU.add).then_inc(key_ready, 1)
                    dve.wait_ge(key_ready, r)
                dispatch(rt[:, 5, :, 0:1])
                if not isinstance(r, int):
                    low(NEXP * r, 0)
                for h in range(2):
                    tokens_low(of_round(r, h), small_bank[1 + h], r, h, h)
                low(0 if isinstance(r, int) else NEXP * r, 1)

                def item(u, it, last):
                    def product(b):
                        dve.wait_ge(silu_ready, b + 1 + 4 * it)
                        dve.wait_ge(v_full, wide(it, 2 * b + 1))
                        h = hid[:, BLK * b:BLK * b + BLK]
                        dve.tensor_tensor(h, wide_bank[(2 * b + 1) % 4][:, 0:BLK], h, ALU.mult).then_inc(v_free, 1)

                    def small(name):
                        no, src = small_no(r, u, name, last)
                        dve.wait_ge(small_full, no + 1)
                        return no, src

                    def hidden_low(b):
                        _, src = small(f"T{b}")
                        dve.wait_ge(ht_hi_ready, b + 1 + 4 * it)
                        k = slice(BLK_TILES[b][0], BLK_TILES[b][-1] + 1)
                        dve.tensor_tensor(ht_lo[:, k].rearrange("p k n -> p (k n)"), src[:, 0:len(BLK_TILES[b]) * SLOTS],
                                          ht_hi[:, k].rearrange("p k n -> p (k n)").bitcast(F32), ALU.subtract)\
                            .then_inc(small_free, 1)

                    def result_low(q):
                        dve.wait_ge(ym_hi_ready, q + 1 + 4 * it)
                        c = slice(QTR * q, QTR * q + QTR)
                        dve.scalar_tensor_tensor(ym_lo[:, c], wide_bank[q][:, 0:QTR], slot_w[:, 0:1],
                                                 ym_hi[:, c].bitcast(F32), ALU.mult, ALU.subtract).then_inc(v_free, 1)

                    def scattered(m):
                        no, src = small(f"Sc{m}")
                        dve.wait_ge(small_free, no)
                        dve.tensor_tensor(x[:, m], x[:, m], src[:, 0:T], ALU.add).then_inc(small_free, 1)

                    for c in range(N_CHUNK):
                        if c in (2, 4, 6, 8):
                            product(c // 2 - 1)
                        if c == 2:
                            no, src = small("PS")
                            w = src[:, u:u + 1] if last else src[:, bass.ds(u, 1)]
                            dve.tensor_copy(slot_w[:, 0:1], w).then_inc(small_free, 1)
                            dve.wait_ge(small_free, no + 1)
                            _, src = small("S")
                            dve.tensor_copy(scat[:, :], src[:, 0:T]).then_inc(small_free, 1)
                            if not last:
                                dispatch(rt[:, 5, :, bass.ds(u + 1, 1)])
                        if c in (4, 6, 8):
                            hidden_low(c // 2 - 2)
                        if c > 8:
                            result_low(c - 9)
                        if c > 9:
                            scattered(2 * (c - 10))
                            scattered(2 * (c - 10) + 1)
                        if c + 2 < N_CHUNK:
                            low(it, c + 2)
                        elif not last:
                            low(it + 1, c + 2 - N_CHUNK)
                        if c == 8:
                            if not last:
                                tokens_low(*small_no(r, u, "G0"), r, 2 + 2 * u, 0)
                            hidden_low(3)
                    if not last:
                        tokens_low(*small_no(r, u, "G1"), r, 3 + 2 * u, 1)
                    result_low(3)
                    scattered(4)
                    scattered(5)
                    scattered(6)
                    scattered(7)

                items(dve, r, item)
                dve.wait_ge(small_free, of_round(r, ROUND_S))

            low(0, 0)
            rounds(dve, round_)
            for m in range(KD):
                dve.sem_inc(x_ready, 1)
            norm("norm_f", 2 * DEPTH, lambda k: final[:, k:k + 1])

        @block.tensor
        def _(pe):
            def whole(key):
                slot, n, _ = plan.chunks[key]
                pe.wait_ge(landed[slot], n)
                return raw[slot]

            def parts(key):
                g = plan.split[key]
                pe.wait_ge(lo_ready, g + 1)
                return w_hi[g % SPLIT], w_lo[g % SPLIT]

            def a_take(key):
                b, _, need = A.of[key]
                if need:
                    pe.wait_ge(a_free, need)
                return a_bank[b]

            def v_take(key):
                b, _, need = V.of[key]
                if need:
                    pe.wait_ge(v_free, need)
                return v_bank[b]

            def product(out, w, rhs, full):
                for k, (a, b) in enumerate(zip(w, rhs)):
                    mm = pe.matmul(out, a, b, start=(k == 0), stop=(k == len(w) - 1))
                mm.then_inc(full, 1)

            def product3(out, w_h, w_l, x_h, x_l, full=None, start=True, stop=True, ready=None):
                n = len(w_h)
                for k in range(n):
                    if ready:
                        ready(k)
                    pe.matmul(out, w_h[k], x_h[k], start=start and k == 0, stop=False)
                    pe.matmul(out, w_h[k], x_l[k], start=False, stop=False)
                    mm = pe.matmul(out, w_l[k], x_h[k], start=False, stop=stop and k == n - 1)
                if full is not None:
                    mm.then_inc(full, 1)

            hh, hl = [hn_hi[:, k] for k in range(KD)], [hn_lo[:, k] for k in range(KD)]

            def norm(key, r):
                out = a_take(key)[:, 0:T]
                for k in range(KD):
                    pe.wait_ge(sq_ready, 8 * r + k + 1)
                    mm = pe.matmul(out, ones[:, :], squares[:, k], start=(k == 0), stop=(k == KD - 1))
                mm.then_inc(a_full, 1)

            def cols(t, k=KD):
                t = t[:, 0:k * P].rearrange("p (k n) -> p k n", k=k)
                return [t[:, i] for i in range(k)]

            def project(key, ready=None):
                w_h, w_l = parts(key)
                product3(a_take(key)[:, 0:T], cols(w_h), cols(w_l), hh, hl, a_full, ready=ready)

            def step(l, k, m, src, ready):
                project(("gate", l, k, m))
                w = whole(("branch", l, k, m // 2))[:, :].rearrange("p (k n) -> p k n", k=KB)
                c = P * (m % 2)
                out = v_take(("branch", l, k, m))[:, 0:T]
                if m == 0:
                    ready()
                product(out, [w[:, i, c:c + P] for i in range(KB)], [src[:, i] for i in range(KB)], v_full)

            pe.wait_ge(const_ready, 3)
            for l in range(DEPTH):
                norm(("norm1", l), 2 * l)
                for m in range(KB):
                    project(("uc", l, m), None if m else lambda k: pe.wait_ge(hn_ready, 8 * 2 * l + k + 1))
                pe.wait_ge(bbar_ready, 4 * (l + 1))
                for c in range(2):
                    out = a_take(("bt", l, c))
                    for ct in range(4):
                        mm = pe.transpose(out[:, P * ct:P * ct + P],
                                          bbar[:, c, 4 * ct:4 * ct + 4, :].rearrange("p s h -> p (s h)"), ident[:, :])
                    mm.then_inc(a_full, 1)
                for j in range(2):
                    for i in range(2):
                        w_h, w_l = (w[:, :].rearrange("p (k n) -> p k n", k=4) for w in parts(("va", l, j, i)))
                        for b, t0 in enumerate(TOKS):
                            if i == 0:
                                a_take(("va", l, j, b))
                            out = a_bank[A.of[("va", l, j, b)][0]][:, 0:256]
                            product3(out, [hn_hi[:, 4 * i + k, t0:t0 + P] for k in range(4)],
                                     [hn_lo[:, 4 * i + k, t0:t0 + P] for k in range(4)],
                                     [w_h[:, k] for k in range(4)], [w_l[:, k] for k in range(4)],
                                     a_full if i else half_read if b == 2 else None, start=i == 0, stop=i == 1)
                for m in range(KB):
                    project(("xb", l, m))

                def s5_in(s):
                    q = l * NST + s
                    if q:
                        pe.wait_ge(s5_free, q)
                    if s == 0:
                        pe.wait_ge(a_free, A.of[("bt", l, 1)][1] + 1)
                    j, ct = 32 * (s % 4), s // 4
                    pe.matmul(s5_bank[:, 0, 0:T], bt[j:j + 32, 0, ct], uc[j:j + 32, ct], start=True, stop=True)
                    pe.matmul(s5_bank[:, 1, 0:T], bt[j:j + 32, 1, ct], uc[j:j + 32, ct], start=True, stop=True)\
                        .then_inc(s5_full, 1)

                def s5_out_(s):
                    q = l * NST + s
                    pe.wait_ge(rot_ready, q + 1)
                    j = 32 * (s % 4)
                    if s % 4 == 0 and q:
                        pe.wait_ge(ys_ready, q // 4)
                    if s == 0:
                        pe.wait_ge(layer_prepared, 3 * (l + 1))
                    out = y_bank[j:j + 32, 0:T]
                    pe.matmul(out, mat("c_re", 512)[:, 32 * s:32 * s + 32], xs[:, q % 2, 0], start=True, stop=False)
                    pe.matmul(out, mat("c_im", 512)[:, 32 * s:32 * s + 32], xs[:, q % 2, 1], start=False, stop=True)\
                        .then_inc(y_full, 1)

                for s in range(NST + 2):
                    if s < 8:
                        project((("ua", "gb")[s // 4], l, s % 4))
                    elif s < NST:
                        step(l, 0, s - 8, ug, lambda: pe.wait_ge(ya_ready, l + 1))
                    if s == 3:
                        pe.wait_ge(xc_ready, l + 1)
                        for g in range(8):
                            w = mat(("wa", "wx")[g // 4], 512)[:, P * (g % 4):P * (g % 4) + P]
                            product(a_take(("ri", l, g))[:, 0:T], [w], [xc[:, g % 4]], a_full)
                    if s == 4:
                        pe.wait_ge(v_ready, l + 1)
                        pe.wait_ge(layer_prepared, 3 * (l + 1))
                        for h in range(H_A):
                            out = v_take(("mixed", l, h))
                            c = slice(P * h, P * h + P)
                            pe.matmul(out[:, 0:P], v_tok[:, 0, c], mat("ws", 512)[:, c], start=True, stop=True)
                            pe.matmul(out[:, P:SEQ], v_tok[:, 1, c], mat("ws", 512)[:, c], start=True, stop=True)
                            pe.matmul(out[:, SEQ:T], v_tok[64:P, 2, c], mat("ws_s", 256)[64:P, 64 * h:64 * h + 64],
                                      start=True, stop=True).then_inc(v_full, 1)
                    if s < NST:
                        s5_in(s)
                    if s >= 2:
                        s5_out_(s - 2)
                for m in range(KD):
                    step(l, 1, m, gbg, lambda: pe.wait_ge(yb_ready, l + 1))
                pe.wait_ge(z_ready, KB * (l + 1))
                for m in range(KB):
                    w = whole(("glu", l, m // 2))[:, :].rearrange("p (k n) -> p k n", k=KB)
                    c = P * (m % 2)
                    product(a_take(("glu", l, m))[:, 0:T], [w[:, k, c:c + P] for k in range(KB)],
                            [zc[:, k] for k in range(KB)], a_full)
                for m in range(KD):
                    step(l, 2, m, zc, lambda: pe.wait_ge(yc_ready, KB * (l + 1)))
                pe.wait_ge(acc_ready, KD * (l + 1))
                for m in range(KD):
                    product(v_take(("wo", l, m))[:, 0:T], cols(whole(("wo", l, m))), [acc[:, k] for k in range(KD)], v_full)
                norm(("norm2", l), 2 * l + 1)
                if l == 1:
                    pe.wait_ge(router_hi_ready, 2)
                    w_h, w_l = ([router_w[:, NEXP * (i * KD + k):NEXP * (i * KD + k) + P] for k in range(KD)]
                                for i in range(2))
                    product3(a_take(("logits_t",))[:, 0:T], w_h, w_l, hh, hl, a_full,
                             ready=lambda k: pe.wait_ge(hn_ready, 8 * (2 * l + 1) + k + 1))
                    pe.wait_ge(a_free, A.of[("logits_t",)][1] + 1)
                    out = a_take(("logits",))
                    for b, t0 in enumerate(TOKS):
                        mm = pe.matmul(out[:, NEXP * b:NEXP * b + NEXP], tmp[:, t0:t0 + P], ident[:, 0:NEXP],
                                       start=True, stop=True)
                    mm.then_inc(a_full, 1)

                    pe.wait_ge(ident_r_ready, 1)
                    for i in range(12):
                        b, h = i % 6 // 2, i % 2
                        out = a_take(("tok", i))
                        for j in range(4):
                            mm = pe.matmul(out[:, P * j:P * j + P],
                                           (hn_hi, hn_lo)[i // 6][:, 4 * h + j, TOKS[b]:TOKS[b] + P], ident_r[:, :],
                                           start=True, stop=True)
                        mm.then_inc(a_full, 1)
                    pe.wait_ge(chosen_ready, 1)
                    pe.wait_ge(before_ready, 1)
                    out = small_bank[0]
                    for b in range(3):
                        o = out[:, NEXP * b:NEXP * b + NEXP]
                        for i in range(b):
                            pe.matmul(o, ones[:, :], rt[:, 4, i], start=i == 0, stop=False)
                        pe.matmul(o, before[:, :], rt[:, 4, b], start=b == 0, stop=True)
                    for b in range(3):
                        pe.matmul(out[:, 3 * NEXP:4 * NEXP], ones[:, :], rt[:, 4, b], start=b == 0, stop=b == 2)
                    pe.matmul(out[:, 4 * NEXP:4 * NEXP + SLOTS], ones[:, :], before[:, :], start=True, stop=True)\
                        .then_inc(small_full, 1)
                    continue
                ab, vb, s0 = A.of[("unit", l)], V.of[("unit", l)], plan.split[("unit", l)]
                hb = 0
                with pe.Fori(0, N_UNITS) as u:
                    for g in range(UNIT_G):
                        w_h, w_l = uw_hi[g % SPLIT], uw_lo[g % SPLIT]
                        pe.wait_ge(lo_ready, s0 + g + 1 + UNIT_G * u)
                        if g < 2 * FT:
                            f = g // 2
                            if g % 2 == 0:
                                pe.wait_ge(a_free, ab + (f - 2 if f >= 3 else 0) + UNIT_A * u)
                                product3(a_bank[f % 3][:, 0:T], cols(w_h), cols(w_l), hh, hl, a_full,
                                         ready=None if g else lambda k: pe.wait_ge(hn_ready, 8 * (2 * l + 1) + k + 1))
                            else:
                                pe.wait_ge(v_free, vb + (f - 1 if f >= 2 else 0) + UNIT_V * u)
                                product3(v_bank[f % 2][:, 0:T], cols(w_h), cols(w_l), hh, hl, v_full)
                            continue
                        q = g - FT
                        pe.wait_ge(v_free, vb + q - 1 + UNIT_V * u)
                        if g == 2 * FT:
                            pe.wait_ge(hid_lo_ready, hb + FT + FT * u)
                        product3(v_bank[q % 2][:, 0:T], cols(w_h, FT), cols(w_l, FT), [hid_hi[:, k] for k in range(FT)],
                                 [hid_lo[:, k] for k in range(FT)], v_full)

            def gather(no, out, h):
                pe.wait_ge(small_free, no - 3)
                for j in range(4):
                    c = slice(P * (4 * h + j), P * (4 * h + j) + P)
                    for i, t in enumerate((tok_hi, tok_lo)):
                        for b in range(3):
                            mm = pe.matmul(out[:, SLOTS * j:SLOTS * j + SLOTS], t[:, b, c], disp[:, b],
                                           start=i == 0 and b == 0, stop=i == 1 and b == 2)
                mm.then_inc(small_full, 1)

            def round_(r):
                pe.wait_ge(disp_ready, 1 + NEXP * r)
                if isinstance(r, int):
                    pe.wait_ge(a_free, A.of[("tok", 11)][1] + 1)
                    pe.wait_ge(small_free, 1)
                gather(4 if isinstance(r, int) else of_round(r, 0), small_bank[1], 0)
                pe.wait_ge(small_free, of_round(r, 1))
                gather(4 if isinstance(r, int) else of_round(r, 1), small_bank[2], 1)
                pe.wait_ge(small_free, of_round(r, 2))
                pe.sem_inc(round_begun, 1)

                def item(u, it, last):
                    def small_take(name):
                        no, out = small_no(r, u, name, last)
                        pe.wait_ge(small_free, no - 2 if name == "PS" else no - 3)
                        return out

                    def projected(c):
                        b, out = c // 2, wide_bank[c % 4][:, 0:BLK]
                        pe.wait_ge(lo_ready, parted(it, c))
                        pe.wait_ge(v_free, up_done(it, b - 2) if b >= 2 else down_done(it - 1, c))
                        w_h, w_l = (w[c % MSPLIT][:, :].rearrange("p (k n) -> p k n", k=KD) for w in (mw_hi, mw_lo))
                        for k0 in (0, 4):
                            ks = range(k0, k0 + 4)
                            product3(out, [x_hi[:, k] for k in ks], [x_lo[:, k] for k in ks], [w_h[:, k] for k in ks],
                                     [w_l[:, k] for k in ks], v_full if k0 else None, start=not k0, stop=bool(k0))

                    def transposed(b):
                        out = small_take(f"T{b}")
                        pe.wait_ge(v_free, up_done(it, b))
                        for j, k in enumerate(BLK_TILES[b]):
                            mm = pe.transpose(out[:, SLOTS * j:SLOTS * j + SLOTS], hid[:, P * k:P * k + P], ident[:, :])
                        mm.then_inc(small_full, 1)

                    def down(q):
                        pe.wait_ge(lo_ready, parted(it, 8 + q))
                        pe.wait_ge(v_free, up_done(it, 2 + q // 2))
                        w_h, w_l = (w[(8 + q) % MSPLIT][:, :].rearrange("p (k n) -> p k n", k=FT) for w in (mw_hi, mw_lo))
                        last_tiles = BLK_TILES[3][0]
                        for k0, k1 in ((0, last_tiles), (last_tiles, FT)):
                            if q == 0:
                                pe.wait_ge(small_free, small_no(r, u, "T3" if k0 else "T2", last)[0] + 1)
                            ks = range(k0, k1)
                            product3(wide_bank[q][:, 0:QTR], [ht_hi[:, k] for k in ks], [ht_lo[:, k] for k in ks],
                                     [w_h[:, k] for k in ks], [w_l[:, k] for k in ks], v_full if k0 else None,
                                     start=not k0, stop=bool(k0))

                    def scatter(q):
                        pe.wait_ge(v_free, down_done(it, q))
                        for m in (2 * q, 2 * q + 1):
                            out = small_take(f"Sc{m}")[:, 0:T]
                            pe.matmul(out, ym_hi[:, P * m:P * m + P], scat[:, :], start=True, stop=False)
                            pe.matmul(out, ym_lo[:, P * m:P * m + P], scat[:, :], start=False, stop=True)\
                                .then_inc(small_full, 1)

                    for b in range(4):
                        projected(2 * b)
                        projected(2 * b + 1)
                        if b:
                            transposed(b - 1)
                            continue
                        out = small_take("PS")
                        for i, t in enumerate((comb_hi, comb_lo)):
                            for b in range(3):
                                mm = pe.matmul(out[:, 0:NEXP], disp[:, b], t[:, b], start=i == 0 and b == 0,
                                               stop=i == 1 and b == 2)
                        mm.then_inc(small_full, 1)
                        out = small_take("S")
                        for b, p0 in enumerate((0, 0, 64)):
                            mm = pe.matmul(out[:, TOKS[b] + p0:TOKS[b] + P], disp[:, b], ident_r[:, p0:P],
                                           start=True, stop=True)
                        mm.then_inc(small_full, 1)
                    if not last:
                        pe.wait_ge(disp_ready, it + 2)
                        gather(*small_no(r, u, "G0"), 0)
                    transposed(3)
                    down(0)
                    down(1)
                    scatter(0)
                    down(2)
                    scatter(1)
                    if not last:
                        gather(*small_no(r, u, "G1"), 1)
                    down(3)
                    scatter(2)
                    scatter(3)

                items(pe, r, item)

            rounds(pe, round_)
            norm("norm_f", 2 * DEPTH)


def kernel(x_prompt, x_sample, state_conv_b, state_lru_b, state_s5_re, state_s5_im, norm_mix_g, w_in, b_gate,
           a_ln_g, a_ln_b, a_ws, a_bs, b_conv_w, b_conv_b, b_wa, b_ba, b_wx, b_bx, b_lam, c_lam_re, c_lam_im,
           c_log_dt, c_b_re, c_b_im, c_c_re, c_c_im, c_d, c_glu_w, c_glu_b, w_branch, w_out, norm_ffn_g,
           ffn_w_gate, ffn_w_up, ffn_w_down, moe_router_w, moe_router_b, moe_w_gate, moe_w_up, moe_w_down,
           final_norm_g):
    import numpy as np
    import concourse.bacc as bacc
    from concourse.bass_utils import run_bass_kernel_spmd

    def host(a):
        return np.ascontiguousarray(a)

    L = DEPTH

    def vec(a):
        return host(a).reshape(L, -1, P).transpose(2, 0, 1)

    def state(a):
        a = host(a)
        a = a.reshape((L, NST, P) + a.shape[3:])
        return a.transpose((2, 0, 1) + tuple(range(3, a.ndim)))

    x = np.concatenate([host(x_prompt)[0], host(x_sample).reshape(-1, D)])
    arrays = {"x": x.T.reshape(KD, P, T).transpose(1, 0, 2)}
    log_dt = np.broadcast_to(host(c_log_dt)[:, :, None], (L, 32, 64))
    parts = {
        "g_mix": vec(norm_mix_g), "g_ffn": vec(norm_ffn_g), "b_gate": vec(b_gate),
        "conv_w": vec(host(b_conv_w).reshape(L, -1)), "conv_b": vec(b_conv_b), "ba": vec(b_ba), "bx": vec(b_bx),
        "lam": vec(b_lam), "c_d": vec(c_d), "glu_b": vec(c_glu_b), "lam_re": state(c_lam_re),
        "lam_im": state(c_lam_im), "log_dt": state(log_dt),
        "lru_h0": host(state_lru_b).reshape(L, NSEQ, KB, P).transpose(3, 0, 2, 1).reshape(P, L, -1)}
    arrays["small"] = np.concatenate([parts[k] for k in SM], axis=2)
    arrays["final"] = host(final_norm_g).reshape(KD, P).T
    arrays["router"] = host(moe_router_w)[0].reshape(KD, P, NEXP).transpose(1, 0, 2)
    arrays["rb"] = host(moe_router_b)

    f = np.float32
    cblk = {k: np.zeros((P, L, NST, 2, HG), f) for k in ("c_re", "c_im")}
    for k, a in (("c_re", c_c_re), ("c_im", c_c_im)):
        a = host(a).reshape(L, NST, 2, HG, 64)
        for g in range(2):
            cblk[k][64 * g:64 * g + 64, :, :, g] = a[:, :, g].transpose(3, 0, 1, 2)
    wblk = {k: np.zeros((P, L, KB, P), f) for k in ("wa", "wx")}
    for k, a in (("wa", b_wa), ("wx", b_wx)):
        a = host(a).reshape(L, KB, 2, 64, 64)
        for g in range(2):
            wblk[k][64 * g:64 * g + 64, :, :, 64 * g:64 * g + 64] = a[:, :, g].transpose(2, 0, 1, 3)
    wst = host(a_ws).transpose(3, 0, 1, 2)
    wss = np.zeros((P, L, H_A, NSEQ, TS), f)
    for b in range(NSEQ):
        wss[64 + TS * b:64 + TS * b + TS, :, :, b] = wst[0:TS, :, :, 0:TS]
    mats = {
        "b_re": state(c_b_re), "b_im": state(c_b_im), **cblk, "ws": wst, "ws_s": wss, **wblk,
        "h0_re": state(host(state_s5_re).transpose(0, 2, 3, 1)), "h0_im": state(host(state_s5_im).transpose(0, 2, 3, 1)),
        "conv": host(state_conv_b).reshape(L, NSEQ, 3, KB, P).transpose(4, 0, 3, 1, 2)}
    arrays["pl"] = np.concatenate([host(mats[k]).reshape(P, L, -1) for k in PL], axis=2).transpose(1, 0, 2)
    arrays["rows"] = np.stack([host(a_ln_g), host(a_ln_b), host(a_bs).reshape(L, -1)], axis=1)

    def chunks(w, width):
        w = host(w)
        return w.reshape(w.shape[0], -1, P, w.shape[2] // width, width).transpose(0, 3, 2, 1, 4)

    win, wva = chunks(w_in, P), chunks(host(w_in)[:, :, DB:D], 256)
    order = list(range(16, 20)) + [0, 1, 2, 3] + list(range(8, 12)) + list(range(0, 4)) + list(range(12, 16)) \
        + list(range(20, 44))
    arrays["w_in"] = win[:, order].reshape(L, 44, P, CHUNK)
    arrays["w_in"][:, 4:8] = wva.reshape(L, 2, P, 2, CHUNK).transpose(0, 1, 3, 2, 4).reshape(L, 4, P, CHUNK)
    br = host(w_branch)
    arrays["w_br"] = br.reshape(L, 3, KB, P, 4, 256).transpose(0, 1, 4, 3, 2, 5)
    arrays["w_glu"] = chunks(c_glu_w, 256)
    arrays["w_wo"] = chunks(w_out, P)

    def cols(w):
        return w.reshape(-1, KD, P, FT, P).transpose(3, 0, 2, 1, 4)[:, None]

    def dense(w):
        return host(w)[0].reshape(D, 2, FT * P).transpose(1, 0, 2)

    arrays["w_gu"] = np.concatenate([cols(dense(ffn_w_gate)), cols(dense(ffn_w_up))], axis=1)
    arrays["w_dn"] = host(ffn_w_down).reshape(2, FT, P, KD, P).transpose(3, 0, 2, 1, 4)

    def blocks(w, width):
        w = host(w)[0]
        return w.reshape(NEXP, -1, P, 4, width).transpose(3, 0, 2, 1, 4).reshape(4, NEXP, P, MCHUNK)

    gate_up = np.stack([blocks(moe_w_gate, BLK), blocks(moe_w_up, BLK)], axis=1)
    arrays["w_moe"] = np.concatenate([gate_up.reshape(8, NEXP, P, MCHUNK), blocks(moe_w_down, QTR)])

    shapes = {"x": (P, KD, T), "small": (P, L, NSM), "final": (P, KD), "router": (P, KD, NEXP), "rb": (1, NEXP),
              "pl": (L, P, NPL), "rows": (L, 3, DB), "w_in": (L, 44, P, CHUNK), "w_br": (L, 12, P, CHUNK),
              "w_glu": (L, 2, P, CHUNK), "w_wo": (L, KD, P, CHUNK), "w_gu": (2 * FT, N_UNITS, P, KD * P),
              "w_dn": (KD, N_UNITS, P, UCHUNK), "w_moe": (N_CHUNK, NEXP, P, MCHUNK)}
    outs = {"y": (P, KD * T), "va": (L, 64, DB), "conv": (L, P, KB * NLAST * 3), "lru": (L, P, KB * NLAST),
            "s5": (L, P, 2 * NST * NLAST)}
    nc = bacc.Bacc("TRN2", target_bir_lowering=False, num_devices=1)
    feed, args = {}, []
    for name, shape in shapes.items():
        feed[f"{name}_in"] = host(arrays[name]).reshape(shape)
        args.append(nc.dram_tensor(f"{name}_in", shape, F32, kind="ExternalInput").ap())
    for name, shape in outs.items():
        args.append(nc.dram_tensor(f"{name}_out", shape, F32, kind="ExternalOutput").ap())
    build(nc, *args)
    got = run_bass_kernel_spmd(nc, [feed], core_ids=[0]).results[0]

    y = got["y_out"].reshape(P, KD, T).transpose(2, 1, 0).reshape(T, D)
    va = got["va_out"].reshape(L, NSEQ, TS, DB)
    conv = got["conv_out"].reshape(L, P, KB, NLAST, 3).transpose(0, 3, 4, 2, 1).reshape(L, NLAST, 3, DB)
    lru = got["lru_out"].reshape(L, P, KB, NLAST).transpose(0, 3, 2, 1).reshape(L, NLAST, DB)
    s5 = got["s5_out"].reshape(L, P, 2, NST, NLAST).transpose(2, 0, 4, 3, 1).reshape(2, L, NLAST, 32, 64)
    return (host(y[None, 0:SEQ]), host(y[SEQ:].reshape(NSEQ, TS, D)), host(conv[:, 0:1]), host(lru[:, 0:1]),
            host(s5[0][:, 0:1]), host(s5[1][:, 0:1]), host(va), host(conv[:, 1:]), host(lru[:, 1:]),
            host(s5[0][:, 1:]), host(s5[1][:, 1:]))
```

```python
from contextlib import ExitStack

import concourse.bass as bass
from concourse import mybir

ALU = mybir.AluOpType
ACT = mybir.ActivationFunctionType
F32 = mybir.dt.float32
F32R = mybir.dt.float32r
AX_X = mybir.AxisListType.X

P = 128
D, DEPTH, SEQ, NSEQ, TS = 1024, 2, 256, 8, 8
T = SEQ + NSEQ * TS
KD = D // P
DB = D // 2
KB = DB // P
CONVW = 4
SEG = CONVW - 1 + TS
XB = CONVW - 1 + SEQ + NSEQ * SEG
H_A = 4
NST = 16
SLOT_N, S5_AT = 24, 3
HG = 16
NEXP = 8
FT = 11
EPS = 1e-6
TOKS = (0, 128, 192)
E_DVE = 6
NLAST = 1 + NSEQ
RAW, WHOLE, CHUNK = 3, 2, 1024
SPLIT = 3
URAW, UCHUNK = 5, FT * P
N_UNITS = 2
UNIT_G, UNIT_A, UNIT_V = 2 * FT + KD, FT, FT + KD

SLOTS = 128
BLK = FT * P // 4
QTR = D // 4
MCHUNK = KD * BLK
assert MCHUNK == FT * QTR
N_CHUNK = 12
MRAW, MSPLIT = 4, 3
BLK_TILES = [[k for k in range(FT) if b * BLK < P * (k + 1) <= (b + 1) * BLK] for b in range(4)]
SMALLS = ["PS", "S", "T0", "T1", "T2", "G0", "T3", "Sc0", "Sc1", "Sc2", "Sc3", "G1", "Sc4", "Sc5", "Sc6", "Sc7"]
SMALLS_LAST = [k for k in SMALLS if k[0] != "G"]
ITEM_S = len(SMALLS)
ROUND_S = 2 + ITEM_S * (NEXP - 1) + len(SMALLS_LAST)
ROUNDS = -(-T // SLOTS)

SM = {}
_n = 0
for _name, _w in (("g_mix", 8), ("g_ffn", 8), ("b_gate", 24), ("conv_w", 16), ("conv_b", 4), ("ba", 4), ("bx", 4),
                  ("lam", 4), ("c_d", 4), ("glu_b", 4), ("lam_re", 16), ("lam_im", 16), ("log_dt", 16), ("lru_h0", 32)):
    SM[_name] = _n
    _n += _w
NSM = _n
N_HALF = SM["lam_re"]
PL = {}
_n = 0
for _name, _w in (("b_re", 256), ("b_im", 256), ("c_re", 512), ("c_im", 512), ("ws", 512), ("ws_s", 256), ("wa", 512),
                  ("wx", 512), ("h0_re", 128), ("h0_im", 128), ("conv", 96)):
    PL[_name] = _n
    _n += _w
NPL = _n


def upto(k, m):
    return 20 + 12 * k + 3 * (m // 2) + (3 if m % 2 else 2)


WO = upto(2, 7)


class Ring:

    def __init__(self, banks):
        self.banks, self.n, self.drained, self.of = banks, 0, {}, {}

    def take(self, key):
        b = self.n % self.banks
        self.of[key] = (b, self.n, self.drained.get(b, 0))
        self.n += 1
        self.drained[b] = self.n

    def loop(self, key, per, times):
        self.of[key] = self.n
        self.n += per * times
        self.drained = {b: self.n for b in range(self.banks)}


class Plan:

    def __init__(self):
        self.a, self.v = Ring(3), Ring(2)
        self.chunks, self.order = {}, []
        self.loads = {"split": [], "whole": []}
        self.split, self.reader = {}, {}
        self.n_split = self.n_half = 0
        for l in range(DEPTH):
            self.layer(l)
        self.a.take("norm_f")
        for c, key in enumerate(self.loads["split"]):
            self.chunks[key] = (c % RAW, 16 * (c // RAW + 1), ("lo", self.split[self.loads["split"][c - RAW]] + 1) if c >= RAW else None)
        whole = self.loads["whole"]
        for c, (key, last) in enumerate(whole):
            freed = None
            if c >= WHOLE:
                freed = ("a", self.count(whole[c - WHOLE][1]))
            self.chunks[key] = (RAW + c % WHOLE, 16 * (c // WHOLE + 1), freed)
        for l in range(DEPTH):
            self.merge(l)

    def merge(self, l):
        for key in self.loads["split"]:
            if key[1] == l:
                self.order.append(key)
                if key == ("gate", l, 1, 2):
                    self.order += [k for k, _ in self.loads["whole"] if k[1] == l]

    def count(self, key):
        return (self.a if key in self.a.of else self.v).of[key][1] + 1

    def split_chunk(self, key, reader):
        self.loads["split"].append(key)
        self.split[key] = self.n_split
        self.reader[self.n_split] = reader
        self.n_split += 1

    def layer(self, l):
        a, v = self.a, self.v
        self.first = self.n_split
        a.take(("norm1", l))
        for m in range(KB):
            a.take(("uc", l, m))
            self.split_chunk(("uc", l, m), ("a", a.n))
        for c in range(2):
            a.take(("bt", l, c))
        for j in range(2):
            for b in range(3):
                a.take(("va", l, j, b))
            self.n_half += 1
            self.split_chunk(("va", l, j, 0), ("half", self.n_half))
            self.split_chunk(("va", l, j, 1), ("a", a.n))
        for m in range(KB):
            a.take(("xb", l, m))
            self.split_chunk(("xb", l, m), ("a", a.n))
        for s in range(NST):
            if s < 8:
                key = (("ua", "gb")[s // 4], l, s % 4)
                a.take(key)
                self.split_chunk(key, ("a", a.n))
            else:
                self.step(l, 0, s - 8)
            if s == 3:
                for g in range(8):
                    a.take(("ri", l, g))
            if s == 4:
                for h in range(H_A):
                    v.take(("mixed", l, h))
        for m in range(KD):
            self.step(l, 1, m)
        for m in range(KB):
            a.take(("glu", l, m))
            if m % 2:
                self.loads["whole"].append((("glu", l, m // 2), ("glu", l, m)))
        for m in range(KD):
            self.step(l, 2, m)
        for m in range(KD):
            v.take(("wo", l, m))
            self.split_chunk(("wo", l, m), ("v", v.n))
        a.take(("norm2", l))
        if l == 1:
            a.take(("logits_t",))
            a.take(("logits",))
            for i in range(12):
                a.take(("tok", i))
            self.moe_v, self.moe_split = v.n, self.n_split
            return
        a.loop(("unit", l), UNIT_A, N_UNITS)
        v.loop(("unit", l), UNIT_V, N_UNITS)
        self.split[("unit", l)] = self.n_split
        self.n_split += UNIT_G * N_UNITS
        for k in range(SPLIT):
            self.reader[self.n_split - SPLIT + k] = ("v", v.n - (SPLIT - 1 - k))

    def step(self, l, k, m):
        self.a.take(("gate", l, k, m))
        self.split_chunk(("gate", l, k, m), ("a", self.a.n))
        self.v.take(("branch", l, k, m))
        if m % 2 == 0:
            self.split_chunk(("branch", l, k, m // 2), ("v", self.v.n + 1))


def build(nc, x_in, small_in, final_in, router_in, rb_in, pl_in, rows_in, w_in, w_br, w_glu, w_wo, w_gu, w_dn, w_moe,
          y_out, va_out, conv_out, lru_out, s5_out):
    plan = Plan()
    A, V = plan.a, plan.v

    with ExitStack() as ctx:
        at = [-(-nc.sbuf_base // 32) * 32]

        def sb(name, shape, dt=F32, where=None):
            size = 4
            for w in shape[1:]:
                size *= w
            t = nc.alloc_sbuf_tensor_at(name, shape, dt, offset=at[0] if where is None else where)
            if where is None:
                at[0] += -(-size // 32) * 32
            return t

        def sem(name):
            return ctx.enter_context(nc.semaphore(name))

        x = sb("x", [P, KD, T])
        hn_at = at[0]
        hn_hi, hn_lo = sb("hn_hi", [P, KD, T], F32R), sb("hn_lo", [P, KD, T], F32R)
        small = sb("small", [P, DEPTH, NSM])
        half = sb("half", [P, DEPTH, N_HALF])
        final = sb("final", [P, KD])
        router = sb("router", [P, KD, NEXP])
        router_w = sb("router_w", [P, 2 * KD * NEXP + P - NEXP], F32R)
        router_hi, router_lo = (router_w[:, i * KD * NEXP:(i + 1) * KD * NEXP].rearrange("p (k e) -> p k e", e=NEXP)
                                for i in range(2))
        rb = sb("rb", [P, NEXP])
        ones = sb("ones", [P, P])
        ident = sb("ident", [P, P])
        mask = sb("mask", [P, T])
        eps = sb("eps", [P, 1])
        rs = sb("rs", [P, T])
        tmp = sb("tmp", [P, T])
        sp = sb("sp", [P, 21, DEPTH * NST])
        lg = sb("lg", [P, 3, NEXP])
        rt = sb("rt", [P, 6, 3, NEXP])
        rm = sb("rm", [P, 8, 3])
        revidx = sb("revidx", [P, NEXP])
        pl_at = at[0]
        pl = sb("pl", [P, NPL])
        bs_row = sb("bs_row", [P, DB])
        raw = [sb(f"raw{i}", [P, CHUNK]) for i in range(RAW + WHOLE)]
        w_hi = [sb(f"w_hi{i}", [P, CHUNK], F32R) for i in range(SPLIT)]
        w_lo = [sb(f"w_lo{i}", [P, CHUNK], F32R) for i in range(SPLIT)]
        th_at = at[0]
        th = sb("th", [P, 2, T])
        ah0 = sb("ah0", [P, 2, NST, NSEQ])
        ah_t = sb("ah_t", [P, NST, NSEQ])
        bnst = sb("bnst", [P, 3, 6])
        mv = sb("mv", [P, 3, 2])
        lnr = sb("lnr", [P, 3])
        s5_last = sb("s5_last", [P, 2, NST, NLAST])
        lru_last = sb("lru_last", [P, KB, NLAST])
        conv_last = sb("conv_last", [P, KB, NLAST * (CONVW - 1)])
        e_at = at[0]
        E = sb("E", [P, 2, NST, SEQ])
        mix_at = at[0]
        mix = sb("mix", [P, 7936])
        bbar = sb("bbar", [P, 2, NST, 2 * HG], where=mix_at + 4 * 2560)
        ln_rows = sb("ln_rows", [P, 2, DB], where=mix_at + 4 * 3840)
        squares = [sb("squares0", [P, KD, T], where=mix_at), sb("squares1", [P, KD, T], where=mix_at + 4 * 12 * T)]
        y_fin = sb("y_fin", [P, KD, T], where=mix_at + 4 * 2560)
        acc_at = at[0]
        acc = sb("acc", [P, KD, T])
        xbuf = sb("xbuf", [P, KB, XB])
        z = sb("z", [P, 2, 2, T])
        xs = sb("xs", [P, 2, 2, T])
        rot_v = sb("rot_v", [P, 2, T])
        rot_p = sb("rot_p", [P, 2, T])
        decay = sb("decay", [P, 2, T])
        bt = sb("bt", [P, 2, 4, P])
        def part(name, tile, k=KB):
            return sb(name, [P, k, T], F32R, where=mix_at + 4 * T * tile)

        ya_hi, ya_lo = part("ya_hi", 4), part("ya_lo", 8)
        yb_hi, yb_lo = sb("yb_hi", [P, KB, T], F32R, where=mix_at + 4 * 6656), part("yb_lo", 12)
        yc_hi, yc_lo = part("yc_hi", 0), part("yc_lo", 16)
        acc_hi, acc_lo = part("acc_hi", 4, KD), sb("acc_lo", [P, KD, T], F32R, where=acc_at)
        def over(name, shape, dt, where):
            size = 4 * shape[1] * (shape[2] if len(shape) > 2 else 1)
            return sb(name, shape, dt, where), where + -(-size // 32) * 32

        uraw, cur = [], e_at
        for i in range(URAW):
            t, cur = over(f"uraw{i}", [P, UCHUNK], F32, cur)
            uraw.append(t)
        silu, cur = over("silu", [P, 3, T], F32, cur)
        assert cur <= mix_at
        hid_hi, cur = over("hid_hi", [P, FT, T], F32R, mix_at)
        hid_lo, cur = over("hid_lo", [P, FT, T], F32R, cur)
        assert cur <= acc_at
        cur, uw_hi, uw_lo = acc_at, [], []
        for i in range(SPLIT):
            t, cur = over(f"uw_hi{i}", [P, UCHUNK], F32R, cur)
            uw_hi.append(t)
            t, cur = over(f"uw_lo{i}", [P, UCHUNK], F32R, cur)
            uw_lo.append(t)
        assert cur <= at[0] <= nc.sbuf_usable_end, (cur, at[0], nc.sbuf_usable_end)
        cur, mraw, mw_hi, mw_lo = e_at, [None] * MRAW, [None] * MSPLIT, [None] * MSPLIT
        mraw[0], cur = over("mraw0", [P, MCHUNK], F32, cur)
        mraw[1], cur = over("mraw1", [P, MCHUNK], F32, cur)
        x_hi, cur = over("x_hi", [P, KD, SLOTS], F32R, cur)
        x_lo, cur = over("x_lo", [P, KD, SLOTS], F32R, cur)
        scat, cur = over("scat", [P, T], F32R, cur)
        assert cur <= mix_at
        mraw[3], cur = over("mraw3", [P, MCHUNK], F32, mix_at)
        disp, cur = over("disp", [P, 3, SLOTS], F32R, cur)
        hid, cur = over("hid", [P, FT * P], F32, cur)
        ht_hi, cur = over("ht_hi", [P, FT, SLOTS], F32R, cur)
        ht_lo, cur = over("ht_lo", [P, FT, SLOTS], F32R, cur)
        assert cur <= acc_at
        mraw[2], cur = over("mraw2", [P, MCHUNK], F32, acc_at)
        mw_hi[0], cur = over("mw_hi0", [P, MCHUNK], F32R, cur)
        mw_hi[1], cur = over("mw_hi1", [P, MCHUNK], F32R, cur)
        assert cur <= at[0]
        mw_hi[2], cur = over("mw_hi2", [P, MCHUNK], F32R, hn_at)
        ym_hi, cur = over("ym_hi", [P, D], F32R, cur)
        ym_lo, cur = over("ym_lo", [P, D], F32R, cur)
        assert cur <= hn_at + 8 * KD * T
        cur = pl_at
        for i in range(MSPLIT):
            mw_lo[i], cur = over(f"mw_lo{i}", [P, MCHUNK], F32R, cur)
        tok_hi, cur = over("tok_hi", [P, 3, D], F32R, cur)
        tok_lo, cur = over("tok_lo", [P, 3, D], F32R, cur)
        tok_hi, tok_lo = (t[:, :, :] for t in (tok_hi, tok_lo))
        before, cur = over("before", [P, P], F32, cur)
        slot_no, cur = over("slot_no", [P, SLOTS], F32, cur)
        ident_r, cur = over("ident_r", [P, P], F32R, cur)
        comb_hi, cur = over("comb_hi", [P, 3, NEXP], F32R, cur)
        comb_lo, cur = over("comb_lo", [P, 3, NEXP], F32R, cur)
        slot_w, cur = over("slot_w", [P, 1], F32, cur)
        busiest, cur = over("busiest", [P, 1], mybir.dt.int32, cur)
        assert cur <= th_at

        bank = [ctx.enter_context(nc.psum_tensor(f"bank{i}", [P, 512], F32)) for i in range(5)]
        s5_bank = ctx.enter_context(nc.psum_tensor("s5_bank", [P, 2, 512], F32))
        bank += [s5_bank[:, 0], s5_bank[:, 1], ctx.enter_context(nc.psum_tensor("bank7", [P, 512], F32))]
        a_bank, v_bank, y_bank = bank[0:3], bank[3:5], bank[7]

        def tiles(t, off, n=KB):
            return t[:, off:off + n * T].rearrange("p (k t) -> p k t", k=n)

        uc, xc, ug, gbg = (tiles(mix[:, :], i * KB * T) for i in range(4))
        v_tok = mix[:, 5120:6656].rearrange("p (b c) -> p b c", b=3)
        zc = tiles(mix[:, :], 5120)
        lru_i = tiles(mix[:, :], 6656)
        accf = acc[:, :, :].rearrange("p k t -> p (k t)")
        lru_a, lru_d = tiles(accf, 0), tiles(accf, KB * T)

        def sm(name, l, i=0, n=1, t=None):
            return (small if t is None else t)[:, l, SM[name] + i:SM[name] + i + n]

        def mat(name, n, **kw):
            return pl[:, PL[name]:PL[name] + n]

        def cst(row, l, i=0, n=NST):
            return sp[:, row, l * NST + i:l * NST + i + n]

        def with_e(t, c, s):
            e = E[:, c, s]
            return ((t[:, :, 0:SEQ], e.unsqueeze(1).to_broadcast([P, 2, SEQ])),
                    (t[:, :, SEQ:T].rearrange("p c (b t) -> p c b t", t=TS),
                     e[:, 0:TS].unsqueeze(1).unsqueeze(1).to_broadcast([P, 2, NSEQ, TS])))

        (R_DT, R_X, R_TH, R_M, R_Y, R_R, R_N, R_SH, R_SN, R_C1, R_CS, R_AR, R_AI, R_NR, R_CR, R_CI, R_T, R_T2,
         R_Q, R_E, R_L) = range(21)

        def powers(engine, chain, l, s0, s1, scratch, between=None):
            def c(v, w):
                return v.unsqueeze(2).to_broadcast([P, s1 - s0, w])

            e = E[:, :, s0:s1]
            chain(engine.memset(e[:, 0, :, 0:1], 1.0))
            chain(engine.memset(e[:, 1, :, 0:1], 0.0))
            chain(engine.tensor_copy(e[:, 0, :, 1:2], cst(R_CS, l, s0, s1 - s0).unsqueeze(2)))
            chain(engine.tensor_copy(e[:, 1, :, 1:2], cst(R_SN, l, s0, s1 - s0).unsqueeze(2)))
            pr, pi, pt = (sp[:, r, s0:s1] for r in (R_X, R_TH, R_Y))
            w = 2
            while w < SEQ:
                er, ei = e[:, 0, :, w // 2], e[:, 1, :, w // 2]
                chain(engine.tensor_tensor(pr, er, er, ALU.mult))
                chain(engine.tensor_tensor(pt, ei, ei, ALU.mult))
                chain(engine.tensor_tensor(pr, pr, pt, ALU.subtract))
                chain(engine.tensor_tensor(pi, er, ei, ALU.mult))
                chain(engine.tensor_tensor(pi, pi, pi, ALU.add))
                tt = scratch[:, 0:(s1 - s0) * w].rearrange("p (s w) -> p s w", w=w)
                lo_r, lo_i, hi_r, hi_i = e[:, 0, :, 0:w], e[:, 1, :, 0:w], e[:, 0, :, w:2 * w], e[:, 1, :, w:2 * w]
                chain(engine.tensor_tensor(hi_r, lo_r, c(pr, w), ALU.mult))
                chain(engine.tensor_tensor(tt, lo_i, c(pi, w), ALU.mult))
                chain(engine.tensor_tensor(hi_r, hi_r, tt, ALU.subtract))
                chain(engine.tensor_tensor(hi_i, lo_r, c(pi, w), ALU.mult))
                chain(engine.tensor_tensor(tt, lo_i, c(pr, w), ALU.mult))
                chain(engine.tensor_tensor(hi_i, hi_i, tt, ALU.add))
                w *= 2
                if between:
                    between(w)

        landed = [sem(f"landed{i}") for i in range(RAW + WHOLE)]
        ulanded = [sem(f"ulanded{i}") for i in range(URAW)]
        hi_ready, lo_ready = sem("hi_ready"), sem("lo_ready")
        half_read = sem("half_read")
        hid_hi_ready, hid_lo_ready = sem("hid_hi_ready"), sem("hid_lo_ready")
        xn_ready, hnh_ready = sem("xn_ready"), sem("hnh_ready")
        router_hi_ready = sem("router_hi_ready")
        x_loaded = [sem(f"x_loaded{i}") for i in range(2)]
        vectors_loaded, small_loaded = sem("vectors_loaded"), sem("small_loaded")
        layer_loaded, ln_loaded = sem("layer_loaded"), sem("ln_loaded")
        const_ready = sem("const_ready")
        layer_prepared = sem("layer_prepared")
        a_full, a_free = sem("a_full"), sem("a_free")
        v_full, v_free = sem("v_full"), sem("v_free")
        dve_done = sem("dve_done")
        act_done = sem("act_done")
        pool_done = sem("pool_done")
        consts_in = sem("consts_in")
        consts_act = sem("consts_act")
        angles_ready = sem("angles_ready")
        powers_ready = sem("powers_ready")
        decays_done = sem("decays_done")
        consts_done = sem("consts_done")
        x_ready = sem("x_ready")
        sq_ready = sem("sq_ready")
        hn_ready = sem("hn_ready")
        bbar_ready = sem("bbar_ready")
        var_ready, std_ready, v_ready = sem("var_ready"), sem("std_ready"), sem("v_ready")
        pads_ready, tap_ready = sem("pads_ready"), sem("tap_ready")
        xc_ready, xc_used = sem("xc_ready"), sem("xc_used")
        tanh_ready = sem("tanh_ready")
        dec_root = sem("dec_root")
        lru_ready = sem("lru_ready")
        ya_ready, yb_ready, yc_ready = sem("ya_ready"), sem("yb_ready"), sem("yc_ready")
        s5_full, s5_free = sem("s5_full"), sem("s5_free")
        decay_ready = sem("decay_ready")
        scan_ready, rot_ready = sem("scan_ready"), sem("rot_ready")
        y_full, ys_ready, z_ready = sem("y_full"), sem("ys_ready"), sem("z_ready")
        acc_ready = sem("acc_ready")
        y_hi_ready, y_lo_ready = sem("y_hi_ready"), sem("y_lo_ready")
        acc_hi_ready, acc_lo_ready = sem("acc_hi_ready"), sem("acc_lo_ready")
        diff_ready, ediff_ready, comb_ready = sem("diff_ready"), sem("ediff_ready"), sem("comb_ready")
        mlanded = [sem(f"mlanded{i}") for i in range(MRAW)]
        before_ready, ident_r_ready = sem("before_ready"), sem("ident_r_ready")
        chosen_ready, comb_hi_ready = sem("chosen_ready"), sem("comb_hi_ready")
        small_full, small_free = sem("small_full"), sem("small_free")
        key_ready, disp_ready, busiest_ready = sem("key_ready"), sem("disp_ready"), sem("busiest_ready")
        silu_ready = sem("silu_ready")
        round_begun = sem("round_begun")
        x_hi_ready, ht_hi_ready, ym_hi_ready = sem("x_hi_ready"), sem("ht_hi_ready"), sem("ym_hi_ready")
        stored, va_stored, y_stored = sem("stored"), sem("va_stored"), sem("y_stored")

        block = ctx.enter_context(nc.Block())

        first = [min(plan.split[k] for k in plan.chunks if k in plan.split and k[1] == l) for l in range(DEPTH)]
        count_of = {"a": a_full, "v": v_full, "lo": lo_ready, "half": half_read}

        def uloads(g):
            return 16 * (g // URAW + 1)

        def u_reader(l, g, u):
            ab, vb = A.of[("unit", l)], V.of[("unit", l)]
            if g < 0:
                return v_full, vb + g + 1 + UNIT_V * u
            if g >= 2 * FT:
                return v_full, vb + g - FT + 1 + UNIT_V * u
            return (v_full, vb + g // 2 + 1 + UNIT_V * u) if g % 2 else (a_full, ab + g // 2 + 1 + UNIT_A * u)

        wide_bank, small_bank = bank[0:4], bank[4:8]

        def of_round(r, c):
            return 1 + c + ROUND_S * r

        def small_no(r, u, name, last=False):
            i = (SMALLS_LAST if last else SMALLS).index(name)
            return of_round(r, 2 + i + ITEM_S * u), small_bank[(3 + i) % 4]

        def parted(it, c):
            return plan.moe_split + c + 1 + N_CHUNK * it

        def wide(it, c):
            return plan.moe_v + c + 1 + N_CHUNK * it

        def up_done(it, b):
            return plan.moe_v + b + 1 + 8 * it

        def down_done(it, q):
            return plan.moe_v + 4 + q + 1 + 8 * it

        def items(engine, r, item):
            with engine.Fori(0, NEXP - 1) as u:
                item(u, u if isinstance(r, int) and r == 0 else u + NEXP * r, False)
            item(NEXP - 1, (NEXP - 1) + NEXP * r, True)

        def rounds(engine, round_):
            round_(0)
            engine.wait_ge(busiest_ready, 1)
            most = engine.value_load(busiest[0:1, 0:1], min_val=0, max_val=T)
            with engine.If(most > SLOTS):
                with engine.Fori(1, ROUNDS) as r:
                    round_(r)

        @block.sync
        def _(sync):
            for l in range(DEPTH):
                for key in plan.order:
                    if key[1] != l:
                        continue
                    slot, _, freed = plan.chunks[key]
                    if freed:
                        sync.wait_ge(count_of[freed[0]], freed[1])
                    name, m = key[0], key[2]
                    tile = {"uc": 0, "xb": 8, "ua": 12, "gb": 16}
                    if name in tile:
                        src = w_in[l, tile[name] + m]
                    elif name == "va":
                        src = w_in[l, 4 + 2 * m + key[3]]
                    elif name == "gate":
                        src = w_in[l, 20 + 8 * m + key[3]]
                    elif name == "branch":
                        src = w_br[l, 4 * m + key[3]]
                    else:
                        src = (w_glu if name == "glu" else w_wo)[l, m]
                    sync.dma_start(raw[slot][:, :], src).then_inc(landed[slot], 16)
                sync.wait_ge(rot_ready, NST * (l + 1))
                if l == 0:
                    s0 = plan.split[("unit", l)]
                    with sync.Fori(0, N_UNITS) as u:
                        for g in range(UNIT_G):
                            sync.wait_ge(lo_ready, s0 + g + 1 - URAW + UNIT_G * u)
                            if g < 2 * FT:
                                dst, src = uraw[g % URAW][:, 0:KD * P], w_gu[g, bass.ds(u, 1)]
                            else:
                                dst, src = uraw[g % URAW][:, :], w_dn[g - 2 * FT, bass.ds(u, 1)]
                            sync.dma_start(dst, src.rearrange("u p n -> p (u n)")).then_inc(ulanded[g % URAW], 16)

            def item(u, it, last):
                for c in range(N_CHUNK):
                    sync.wait_ge(lo_ready, parted(it, c - MRAW))
                    if c in (2, 3):
                        sync.wait_ge(v_full, V.of[("wo", 1, KD - 1)][1] + 1)
                    src = w_moe[c, u] if isinstance(u, int) else w_moe[c, bass.ds(u, 1)].rearrange("u p n -> p (u n)")
                    sync.dma_start(mraw[c % MRAW][:, :], src).then_inc(mlanded[c % MRAW], 16)

            rounds(sync, lambda r: items(sync, r, item))
            for k in range(0, KD, 2):
                sync.wait_ge(hn_ready, 8 * 2 * DEPTH + k + 2)
                sync.dma_start(y_out[:, k * T:(k + 2) * T], y_fin[:, k:k + 2].rearrange("p k t -> p (k t)"))\
                    .then_inc(y_stored, 16)
            sync.wait_ge(y_stored, 16 * (KD // 2))
            sync.wait_ge(stored, 48 * DEPTH)
            sync.wait_ge(va_stored, 16 * DEPTH)

        @block.gpsimd
        def _(pool):
            n = [0]

            def chain(ins):
                n[0] += 1
                ins.then_inc(pool_done, 1)
                pool.wait_ge(pool_done, n[0])

            def load_layer(l):
                pool.dma_start(pl[:, :], pl_in[l]).then_inc(layer_loaded, 16)
                pool.dma_start(bs_row[:, :], rows_in[l, 2:3].to_broadcast([P, DB])).then_inc(layer_loaded, 16)

            def load_ln(l):
                for r in range(2):
                    pool.dma_start(ln_rows[:, r, :], rows_in[l, r:r + 1].to_broadcast([P, DB])).then_inc(ln_loaded, 16)

            pool.dma_start(small[:, :, :], small_in).then_inc(vectors_loaded, 16)
            pool.memset(ones[:, :], 1.0).then_inc(const_ready, 1)
            pool.memset(eps[:, :], EPS).then_inc(const_ready, 1)
            chain(pool.memset(ident[:, :], 0.0))
            pool.affine_select(out=ident[:, :], in_=ident[:, :], compare_op=ALU.not_equal, fill=1.0, base=0,
                               pattern=[[-1, P]], channel_multiplier=1).then_inc(const_ready, 1)
            chain(pool.memset(mask[:, :], 1.0))
            pool.memset(mask[:, SEQ::TS], 0.0).then_inc(const_ready, 1)
            pool.memset(mv[:, :, :], 1.0).then_inc(const_ready, 1)
            pool.memset(lg[:, :, :], 0.0).then_inc(const_ready, 1)
            for e in range(NEXP):
                pool.memset(revidx[:, e:e + 1], float(NEXP - e)).then_inc(const_ready, 1)
            pool.wait_ge(x_loaded[1], 16)
            load_layer(0)
            load_ln(0)
            pool.dma_start(final[:, :], final_in).then_inc(small_loaded, 16)
            pool.dma_start(router[:, :, :], router_in).then_inc(small_loaded, 16)
            pool.dma_start(rb[:, :], rb_in.to_broadcast([P, NEXP])).then_inc(small_loaded, 16)

            for l in range(DEPTH):
                if l:
                    pool.wait_ge(x_ready, 16 * (l - 1) + 8)
                    load_layer(l)
                pool.wait_ge(layer_loaded, 32 * (l + 1))
                ws = mat("ws", 512).rearrange("p (h t) -> p h t", h=H_A)
                pool.affine_select(out=ws, in_=ws, compare_op=ALU.is_ge, fill=0.0, base=0,
                                   pattern=[[0, H_A], [1, P]], channel_multiplier=-1).then_inc(layer_prepared, 1)
                wss = mat("ws_s", 256).rearrange("p (h t) -> p h t", h=H_A)
                pool.affine_select(out=wss, in_=wss, compare_op=ALU.is_ge, fill=0.0, base=64,
                                   pattern=[[0, H_A], [1, 64]], channel_multiplier=-1).then_inc(layer_prepared, 1)
                ci = mat("c_im", 512)
                pool.tensor_scalar(ci, ci, -1.0, 0.0, ALU.mult, ALU.add).then_inc(layer_prepared, 1)

                if l:
                    pool.wait_ge(x_ready, 16 * l)
                    load_ln(l)
                else:
                    pool.wait_ge(angles_ready, 1)
                powers(pool, chain, l, E_DVE, NST, xs[:, :, :, :].rearrange("p b c t -> p (b c t)"))
                pool.sem_inc(powers_ready, 1)
                pool.wait_ge(v_ready, l + 1)
                pool.dma_start(va_out[l], v_tok[64:128, 2, :]).then_inc(va_stored, 16)

                pool.wait_ge(a_free, A.of[("xb", l, KB - 1)][1] + 1)
                pool.wait_ge(pads_ready, l + 1)
                if l:
                    pool.wait_ge(stored, 48 * l)
                chain(pool.tensor_copy(conv_last[:, :, 0:3], xbuf[:, :, SEQ:SEQ + 3]))
                seg = xbuf[:, :, 3 + SEQ:].rearrange("p k (b s) -> p k b s", s=SEG)
                for k in range(KB):
                    chain(pool.tensor_copy(conv_last[:, k, 3:].rearrange("p (b s) -> p b s", s=3), seg[:, k, :, TS:SEG]))
                pool.dma_start(conv_out[l], conv_last[:, :, :].rearrange("p k n -> p (k n)")).then_inc(stored, 16)

                for s in range(NST):
                    q = l * NST + s
                    zq, xq = z[:, q % 2], xs[:, q % 2]
                    pool.wait_ge(scan_ready, 2 * q + 2)
                    if q >= 2:
                        pool.wait_ge(y_full, q - 1)
                    for out, c in ((xq, 0), (rot_p[:, :, :], 1)):
                        for (o, e), (i, _) in zip(with_e(out, c, s), with_e(zq, c, s)):
                            pool.tensor_tensor(o, i, e, ALU.mult).then_inc(pool_done, 1)
                            n[0] += 1
                    pool.wait_ge(pool_done, n[0])
                    pool.tensor_tensor(xq[:, 0], xq[:, 0], rot_p[:, 1], ALU.subtract).then_inc(pool_done, 1)
                    n[0] += 1
                    chain(pool.tensor_tensor(xq[:, 1], xq[:, 1], rot_p[:, 0], ALU.add))
                    pool.tensor_copy(s5_last[:, :, s, :], xq[:, :, SEQ - 1::TS]).then_inc(rot_ready, 1)
                pool.wait_ge(pool_done, n[0])
                pool.wait_ge(rot_ready, NST * (l + 1))
                pool.dma_start(s5_out[l], s5_last[:, :, :, :].rearrange("p c s n -> p (c s n)")).then_inc(stored, 16)
                pool.wait_ge(lru_ready, l + 1)
                pool.dma_start(lru_out[l], lru_last[:, :, :].rearrange("p k n -> p (k n)")).then_inc(stored, 16)
                pool.wait_ge(stored, 48 * (l + 1))
            pool.wait_ge(x_ready, 24)
            chain(pool.memset(before[:, :], 1.0))
            pool.affine_select(out=before[:, :], in_=before[:, :], compare_op=ALU.is_ge, fill=0.0, base=-1,
                               pattern=[[1, P]], channel_multiplier=-1).then_inc(before_ready, 1)

        @block.scalar
        def _(act):
            n = [0]

            def chain(ins):
                n[0] += 1
                ins.then_inc(act_done, 1)
                act.wait_ge(act_done, n[0])

            def evac(key, rows_, cols):
                b, q, _ = A.of[key]
                act.wait_ge(a_full, q + 1)
                return a_bank[b][0:rows_, 0:cols]

            def split(l, upto):
                while todo and plan.split[todo[0]] <= first[l] + upto and todo[0][1] == l:
                    key = todo.pop(0)
                    g = plan.split[key]
                    slot, loads, _ = plan.chunks[key]
                    act.wait_ge(landed[slot], loads)
                    reader = plan.reader.get(g - SPLIT)
                    if reader:
                        act.wait_ge(count_of[reader[0]], reader[1])
                    act.activation(w_hi[g % SPLIT][:, :], raw[slot][:, :], ACT.Copy).then_inc(hi_ready, 1)

            def high(it, c):
                slot, loads = c % MRAW, 16 * (c // MRAW + 1) + 16 * (N_CHUNK // MRAW) * it
                act.wait_ge(mlanded[slot], loads)
                act.wait_ge(v_full, wide(it, c - MSPLIT))
                act.activation(mw_hi[c % MSPLIT][:, :], mraw[slot][:, :], ACT.Copy).then_inc(hi_ready, 1)

            def unit_high(u, g):
                if u == N_UNITS:
                    return
                w = KD * P if g < 2 * FT else UCHUNK
                act.wait_ge(ulanded[g % URAW], uloads(g) + 16 * (UNIT_G // URAW) * u)
                act.wait_ge(*u_reader(0, g - SPLIT, u))
                act.activation(uw_hi[g % SPLIT][:, 0:w], uraw[g % URAW][:, 0:w], ACT.Copy).then_inc(hi_ready, 1)

            def norm(key, r, between=None, each=None):
                for k in range(KD):
                    if each:
                        each(k)
                    if r:
                        act.wait_ge(x_ready, 8 * (r - 1) + k + 1)
                    elif k % 4 == 0:
                        act.wait_ge(x_loaded[k // 4], 16)
                    act.activation(squares[r % 2][:, k], x[:, k], ACT.Square).then_inc(sq_ready, 1)
                act.wait_ge(const_ready, 2)
                if r:
                    act.wait_ge(hn_ready, 8 * r)
                act.activation(rs[:, :], evac(key, P, T), ACT.Sqrt, bias=eps[:, :], scale=1.0 / D).then_inc(a_free, 1)
                if between:
                    between()
                if r < 2 * DEPTH:
                    for k in range(KD):
                        act.wait_ge(xn_ready, 8 * r + k + 1)
                        act.activation(hn_hi[:, k], squares[r % 2][:, k], ACT.Copy).then_inc(hnh_ready, 1)

            todo = [k for k in plan.chunks if k in plan.split]
            todo.sort(key=plan.split.get)
            for i in range(2):
                act.dma_start(x[:, 4 * i:4 * i + 4], x_in[:, 4 * i:4 * i + 4]).then_inc(x_loaded[i], 16)
            act.wait_ge(vectors_loaded, 16)
            act.activation(sp[:, R_DT].rearrange("p (l n) -> p l n", l=DEPTH), small[:, :, SM["log_dt"]:SM["log_dt"] + NST],
                           ACT.Exp).then_inc(consts_act, 1)
            act.wait_ge(consts_in, 1)
            act.activation(sp[:, R_E, 0:8], sp[:, R_L, 0:8], ACT.Exp, scale=-1.0).then_inc(consts_act, 1)
            for l in range(DEPTH):
                split(l, 2)
                norm(("norm1", l), 2 * l)
                if l == 0:
                    act.wait_ge(consts_in, 2)
                    act.activation(sp[:, R_SH], sp[:, R_N], ACT.Sin, scale=0.5).then_inc(consts_act, 1)
                    act.activation(sp[:, R_SN], sp[:, R_N], ACT.Sin).then_inc(consts_act, 1)
                    act.wait_ge(const_ready, 3)
                    act.wait_ge(small_loaded, 48)
                    act.activation(router_hi, router[:, :, :], ACT.Copy).then_inc(router_hi_ready, 1)
                    act.activation(router_w[:, 2 * KD * NEXP:], ident[:, 0:P - NEXP], ACT.Copy).then_inc(router_hi_ready, 1)
                for m in range(KB):
                    split(l, m + 2)
                    act.activation(uc[:, m], evac(("uc", l, m), P, T), ACT.Copy).then_inc(a_free, 1)
                for c in range(2):
                    act.activation(bt[:, c].rearrange("p k n -> p (k n)"), evac(("bt", l, c), P, 512), ACT.Copy)\
                        .then_inc(a_free, 1)
                for j in range(2):
                    split(l, 7 + 2 * j)
                    for b in range(3):
                        act.activation(v_tok[:, b, 256 * j:256 * j + 256], evac(("va", l, j, b), P, 256),
                                       ACT.Gelu_apprx_tanh).then_inc(a_free, 1)
                def tap(m):
                    if m == 0:
                        act.wait_ge(pads_ready, l + 1)
                    act.wait_ge(a_free, A.of[("xb", l, m)][1] + 1)
                    w0, b0 = sm("conv_w", l, m), sm("conv_b", l, m)
                    act.activation(xc[:, m, 0:SEQ], xbuf[:, m, 0:SEQ], ACT.Identity, scale=w0, bias=b0).then_inc(act_done, 1)
                    n[0] += 1
                    segs = xbuf[:, m, 3 + SEQ:].rearrange("p (b s) -> p b s", s=SEG)
                    act.activation(xc[:, m, SEQ:T].rearrange("p (b s) -> p b s", s=TS), segs[:, :, 0:TS], ACT.Identity,
                                   scale=w0, bias=b0).then_inc(tap_ready, 1)

                for m in range(KB):
                    split(l, 10 + m)
                    if m == 2:
                        act.wait_ge(var_ready, l + 1)
                        act.activation(lnr[:, :], mv[:, :, 1], ACT.Sqrt, bias=eps[:, :]).then_inc(std_ready, 1)
                    if m:
                        tap(m - 1)
                    src = evac(("xb", l, m), P, T)
                    chain(act.activation(xbuf[:, m, 3:3 + SEQ], src[:, 0:SEQ], ACT.Copy))
                    act.activation(xbuf[:, m, 3 + SEQ:].rearrange("p (b s) -> p b s", s=SEG)[:, :, 3:SEG],
                                   src[:, SEQ:T].rearrange("p (b s) -> p b s", s=TS), ACT.Copy).then_inc(a_free, 1)
                tap(KB - 1)

                def gate(k, m):
                    b, vq, _ = V.of[("branch", l, k, m)]
                    src = evac(("gate", l, k, m), P, T)
                    q = (l * 3 + k) * 8 + m
                    if q >= 2:
                        prev = (l * 3 + k) * 8 + m - 2
                        pk = ("branch", prev // 24, prev // 8 % 3, prev % 8)
                        act.wait_ge(v_free, V.of[pk][1] + 1)
                    act.activation(th[:, q % 2], src, ACT.Tanh, scale=0.5, bias=sm("b_gate", l, 8 * k + m, t=half))\
                        .then_inc(a_free, 1)

                def z_gelu(ct):
                    act.wait_ge(ys_ready, KB * l + ct + 1)
                    act.activation(zc[:, ct], zc[:, ct], ACT.Gelu_apprx_tanh).then_inc(z_ready, 1)

                def decay_of(s):
                    q = l * NST + s
                    if q >= 2:
                        act.wait_ge(scan_ready, 2 * q - 2)
                    act.activation(decay[:, q % 2], mask[:, :], ACT.Copy, scale=cst(R_R, l, s, 1)).then_inc(decay_ready, 1)

                if l == 0:
                    act.wait_ge(decays_done, 1)
                decay_of(0)
                decay_of(1)
                for s in range(SLOT_N):
                    split(l, 14 + s if s < 8 else upto((s - 8) // 8, s % 8))
                    if s < 8:
                        name, dst = (("ua", ug), ("gb", gbg))[s // 4]
                        act.activation(dst[:, s % 4], evac((name, l, s % 4), P, T), ACT.Gelu_apprx_tanh).then_inc(a_free, 1)
                    else:
                        gate((s - 8) // 8, s % 8)
                    if s == 3:
                        for g in range(8):
                            dst, bias = ((lru_a, "ba"), (lru_i, "bx"))[g // 4]
                            act.activation(dst[:, g % 4], evac(("ri", l, g), P, T), ACT.Tanh, scale=0.5,
                                           bias=sm(bias, l, g % 4, t=half)).then_inc(a_free, 1)
                        split(l, 15 + s)
                        act.wait_ge(a_free, A.of[("ri", l, 7)][1] + 1)
                        if l == 0:
                            act.wait_ge(consts_done, 1)
                        for g in range(4):
                            q = sp[:, R_Q, 4 * l + g:4 * l + g + 1]
                            act.activation(lru_d[:, g], lru_a[:, g], ACT.Tanh, scale=q, bias=q).then_inc(act_done, 1)
                            n[0] += 1
                        for g in range(4):
                            q = sp[:, R_Q, 8 + 4 * l + g:8 + 4 * l + g + 1]
                            act.activation(lru_a[:, g], lru_a[:, g], ACT.Exp, scale=q, bias=q).then_inc(tanh_ready, 1)
                        act.wait_ge(act_done, n[0])
                        act.activation(lru_d, lru_d, ACT.Sqrt).then_inc(dec_root, 1)
                    if s > 8 and s % 2 and s < SLOT_N - 1:
                        split(l, upto((s - 8) // 8, s % 8) + 1)
                    if 1 <= s - S5_AT < NST - 1:
                        decay_of(s - S5_AT + 1)
                    if s == 7:
                        act.wait_ge(xc_used, l + 1)
                        act.activation(ya_hi[:, :, :], ug, ACT.Copy).then_inc(y_hi_ready, 1)
                    if s == 9:
                        act.wait_ge(yb_ready, l + 1)
                        act.activation(yb_hi[:, :, :], gbg, ACT.Copy).then_inc(y_hi_ready, 1)
                    if s - S5_AT >= 7 and (s - S5_AT - 7) % 4 == 0:
                        z_gelu((s - S5_AT - 7) // 4)
                for m in range(KB):
                    act.activation(lru_i[:, m], evac(("glu", l, m), P, T), ACT.Tanh, scale=0.5,
                                   bias=sm("glu_b", l, m, t=half)).then_inc(a_free, 1)
                for m in range(KB):
                    act.wait_ge(yc_ready, KB * l + m + 1)
                    act.activation(yc_hi[:, m], zc[:, m], ACT.Copy).then_inc(y_hi_ready, 1)

                def acc_high(m):
                    act.wait_ge(acc_ready, KD * l + m + 1)
                    act.activation(acc_hi[:, m], acc[:, m], ACT.Copy).then_inc(acc_hi_ready, 1)

                for m in range(KD):
                    split(l, upto(2, m))
                    gate(2, m)
                    if m:
                        acc_high(m - 1)
                acc_high(KD - 1)
                split(l, WO + 1)
                if l == 0:
                    norm(("norm2", l), 2 * l + 1, lambda: (unit_high(0, 0), unit_high(0, 1)), lambda k: split(0, WO + 2 + k))
                else:
                    norm(("norm2", l), 2 * l + 1, None, lambda k: split(1, WO + 2 + k))
                    act.activation(ident_r[:, :], ident[:, :], ACT.Copy).then_inc(ident_r_ready, 1)
                    high(0, 0)
                    act.activation(tmp[:, :], evac(("logits_t",), P, T), ACT.Copy).then_inc(a_free, 1)
                    act.activation(lg[:, :, :].rearrange("p b e -> p (b e)"), evac(("logits",), P, 3 * NEXP), ACT.Copy)\
                        .then_inc(a_free, 1)
                    for i in range(12):
                        h, b = i // 6, i % 3
                        act.activation((tok_hi, tok_lo)[i % 6 // 3][:, b, 512 * h:512 * h + 512], evac(("tok", i), P, 512),
                                       ACT.Copy).then_inc(a_free, 1)
                        if i == 5:
                            act.wait_ge(diff_ready, 1)
                            act.activation(rm[:, 4, :], rm[:, 3, :], ACT.Exp).then_inc(ediff_ready, 1)
                    high(0, 1)
                    act.wait_ge(comb_ready, 1)
                    act.activation(comb_hi[:, :, :], rt[:, 0], ACT.Copy).then_inc(comb_hi_ready, 1)
                    continue
                ab, vb, s0 = A.of[("unit", l)], V.of[("unit", l)], plan.split[("unit", l)]
                hb = 0
                for u in range(N_UNITS):
                    def usplit(g):
                        unit_high(u + g // UNIT_G, g % UNIT_G)

                    def hid_high(f):
                        act.wait_ge(v_free, vb + f + 1 + UNIT_V * u)
                        act.activation(hid_hi[:, f], silu[:, f % 3], ACT.Copy).then_inc(hid_hi_ready, 1)

                    for g in range(UNIT_G):
                        usplit(g + 2)
                        if g < 2 * FT and g % 2 == 0:
                            f = g // 2
                            act.wait_ge(a_full, ab + f + 1 + UNIT_A * u)
                            if f >= 3:
                                act.wait_ge(hid_lo_ready, hb + f - 2 + FT * u)
                            act.activation(silu[:, f % 3], a_bank[f % 3][:, 0:T], ACT.Silu).then_inc(a_free, 1)
                            if f:
                                hid_high(f - 1)
                        if g == 2 * FT - 1:
                            hid_high(FT - 1)

            def tokens_high(no, src, h):
                act.wait_ge(small_full, no + 1)
                act.activation(x_hi[:, 4 * h:4 * h + 4].rearrange("p k n -> p (k n)"), src[:, 0:4 * SLOTS], ACT.Copy)\
                    .then_inc(x_hi_ready, 1)

            def round_(r):
                if not isinstance(r, int):
                    high(NEXP * r, 0)
                    high(NEXP * r, 1)
                for h in range(2):
                    tokens_high(of_round(r, h), small_bank[1 + h], h)

                def item(u, it, last):
                    def silu_(b):
                        act.wait_ge(v_full, wide(it, 2 * b))
                        act.activation(hid[:, BLK * b:BLK * b + BLK], wide_bank[2 * b % 4][:, 0:BLK], ACT.Silu)\
                            .then_inc(silu_ready, 1)

                    def hidden_high(b):
                        no, src = small_no(r, u, f"T{b}", last)
                        act.wait_ge(small_full, no + 1)
                        k0, n = BLK_TILES[b][0], len(BLK_TILES[b])
                        act.activation(ht_hi[:, k0:k0 + n].rearrange("p k n -> p (k n)"), src[:, 0:n * SLOTS], ACT.Copy)\
                            .then_inc(ht_hi_ready, 1)

                    def result_high(q):
                        if q == 0:
                            act.wait_ge(small_free, small_no(r, u, "PS", last)[0] + 1)
                        act.wait_ge(v_full, wide(it, 8 + q))
                        act.activation(ym_hi[:, QTR * q:QTR * q + QTR], wide_bank[q][:, 0:QTR], ACT.Copy,
                                       scale=slot_w[:, 0:1]).then_inc(ym_hi_ready, 1)

                    for c in range(N_CHUNK):
                        if c in (1, 3, 5, 7):
                            silu_(c // 2)
                        if c in (4, 6, 8):
                            hidden_high(c // 2 - 2)
                        if c > 8:
                            result_high(c - 9)
                        if c + 2 < N_CHUNK:
                            high(it, c + 2)
                        elif not last:
                            high(it + 1, c + 2 - N_CHUNK)
                        if c == 8:
                            if not last:
                                tokens_high(*small_no(r, u, "G0"), 0)
                            hidden_high(3)
                    if not last:
                        tokens_high(*small_no(r, u, "G1"), 1)
                    result_high(3)

                items(act, r, item)

            rounds(act, round_)
            norm("norm_f", 2 * DEPTH)

        @block.vector
        def _(dve):
            n = [0]

            def chain(ins):
                n[0] += 1
                ins.then_inc(dve_done, 1)
                dve.wait_ge(dve_done, n[0])

            todo = [k for k in plan.chunks if k in plan.split]
            todo.sort(key=plan.split.get)

            def split(l, upto):
                while todo and plan.split[todo[0]] <= first[l] + upto and todo[0][1] == l:
                    key = todo.pop(0)
                    g = plan.split[key]
                    slot = plan.chunks[key][0]
                    dve.wait_ge(hi_ready, g + 1)
                    dve.tensor_tensor(w_lo[g % SPLIT][:, :], raw[slot][:, :], w_hi[g % SPLIT][:, :].bitcast(F32),
                                      ALU.subtract).then_inc(lo_ready, 1)

            def low(it, c):
                dve.wait_ge(hi_ready, parted(it, c))
                dve.tensor_tensor(mw_lo[c % MSPLIT][:, :], mraw[c % MRAW][:, :], mw_hi[c % MSPLIT][:, :].bitcast(F32),
                                  ALU.subtract).then_inc(lo_ready, 1)

            def unit_low(u, g):
                if u == N_UNITS:
                    return
                w = KD * P if g < 2 * FT else UCHUNK
                dve.wait_ge(hi_ready, plan.split[("unit", 0)] + g + 1 + UNIT_G * u)
                dve.tensor_tensor(uw_lo[g % SPLIT][:, 0:w], uraw[g % URAW][:, 0:w],
                                  uw_hi[g % SPLIT][:, 0:w].bitcast(F32), ALU.subtract).then_inc(lo_ready, 1)

            def norm(key, r, gain, between=None):
                b, q, _ = A.of[key]
                dve.wait_ge(a_free, q + 1)
                chain(dve.reciprocal(rs[:, :], rs[:, :]))
                def low(k):
                    dve.wait_ge(xn_ready, 8 * r + k + 1)
                    dve.wait_ge(hnh_ready, 8 * r + k + 1)
                    dve.tensor_tensor(hn_lo[:, k], squares[r % 2][:, k], hn_hi[:, k].bitcast(F32), ALU.subtract).then_inc(hn_ready, 1)

                for k in range(KD):
                    if r == 2 * DEPTH:
                        dve.scalar_tensor_tensor(y_fin[:, k], x[:, k], gain(k), rs[:, :], ALU.mult, ALU.mult).then_inc(hn_ready, 1)
                        continue
                    dve.scalar_tensor_tensor(squares[r % 2][:, k], x[:, k], gain(k), rs[:, :], ALU.mult, ALU.mult).then_inc(xn_ready, 1)
                    if k == 1 and between:
                        between()
                    if k > 1:
                        low(k - 2)
                if r < 2 * DEPTH:
                    low(KD - 2)
                    low(KD - 1)

            def bc(ap, shape):
                return ap.unsqueeze(len(shape) - 1).to_broadcast(shape)

            row = lambda r: sp[:, r]

            dve.wait_ge(vectors_loaded, 16)
            chain(dve.tensor_scalar(half[:, :, :], small[:, :, 0:N_HALF], 0.5, None, ALU.mult))
            two = lambda r, w: sp[:, r, 0:DEPTH * w].rearrange("p (l n) -> p l n", l=DEPTH)
            lam = small[:, :, SM["lam"]:SM["lam"] + 4]
            l1, l2, l3, l4 = (sp[:, R_L, 8 * i:8 * i + 8] for i in range(4))
            ee = sp[:, R_E, 0:8]
            two4 = lambda v: v.rearrange("p (l n) -> p l n", l=DEPTH)
            chain(dve.tensor_scalar(two4(l2), lam, -1.0, None, ALU.mult))
            dve.tensor_tensor(two4(l1), two4(l2), lam, ALU.max).then_inc(consts_in, 1)
            dve.wait_ge(consts_act, 2)
            chain(dve.tensor_scalar(l3, ee, 2.0, None, ALU.add))
            chain(dve.reciprocal(l3, l3))
            chain(dve.tensor_tensor(l3, l3, ee, ALU.mult))
            chain(dve.tensor_tensor(l4, l3, l3, ALU.mult))
            chain(dve.tensor_scalar(ee, l4, 1.0 / 15, None, ALU.mult))
            for d in (13, 11, 9, 7, 5, 3):
                chain(dve.scalar_tensor_tensor(ee, ee, 1.0 / d, l4, ALU.add, ALU.mult))
            chain(dve.scalar_tensor_tensor(ee, ee, 1.0, l3, ALU.add, ALU.mult))
            chain(dve.tensor_scalar(l2, l2, 0.0, None, ALU.max))
            chain(dve.scalar_tensor_tensor(l1, ee, 2.0, l2, ALU.mult, ALU.add))
            chain(dve.tensor_scalar(sp[:, R_Q, 8:16], l1, -4.0, None, ALU.mult))
            dve.tensor_scalar(sp[:, R_Q, 0:8], l1, 2.0, None, ALU.mult).then_inc(consts_done, 1)

            lre, lim = (small[:, :, SM[k]:SM[k] + NST] for k in ("lam_re", "lam_im"))
            chain(dve.tensor_tensor(two(R_X, NST), lre, two(R_DT, NST), ALU.mult))
            chain(dve.tensor_tensor(two(R_TH, NST), lim, two(R_DT, NST), ALU.mult))
            chain(dve.tensor_scalar(row(R_N), row(R_TH), 0.15915494309189535, 12582912.0, ALU.mult, ALU.add))
            chain(dve.tensor_scalar(row(R_N), row(R_N), -12582912.0, None, ALU.add))
            chain(dve.scalar_tensor_tensor(row(R_TH), row(R_N), -6.28125, row(R_TH), ALU.mult, ALU.add))
            chain(dve.scalar_tensor_tensor(row(R_TH), row(R_N), -0.0019353071795864769, row(R_TH), ALU.mult, ALU.add))
            dve.tensor_scalar(row(R_N), row(R_TH), 3.1415925, -3.1415925, ALU.min, ALU.max).then_inc(consts_in, 1)
            chain(dve.tensor_scalar(row(R_Y), row(R_X), 1.0 / 64, None, ALU.mult))
            chain(dve.tensor_scalar(row(R_M), row(R_Y), 1.0 / 5040, None, ALU.mult))
            for c in (720, 120, 24, 6, 2, 1):
                chain(dve.scalar_tensor_tensor(row(R_M), row(R_M), 1.0 / c, row(R_Y), ALU.add, ALU.mult))
            for _ in range(6):
                chain(dve.scalar_tensor_tensor(row(R_M), row(R_M), 2.0, row(R_M), ALU.add, ALU.mult))
            dve.tensor_scalar(row(R_R), row(R_M), 1.0, None, ALU.add).then_inc(decays_done, 1)
            dve.wait_ge(decays_done, 1)
            def more_constants():
                dve.wait_ge(consts_act, 4)
                chain(dve.tensor_tensor(row(R_C1), row(R_SH), row(R_SH), ALU.mult))
                chain(dve.tensor_scalar(row(R_C1), row(R_C1), -2.0, None, ALU.mult))
                chain(dve.tensor_scalar(row(R_CS), row(R_C1), 1.0, None, ALU.add))
                chain(dve.tensor_tensor(row(R_AR), row(R_R), row(R_CS), ALU.mult))
                chain(dve.tensor_tensor(row(R_AI), row(R_R), row(R_SN), ALU.mult))
                dve.sem_inc(angles_ready, 1)
                chain(dve.tensor_tensor(row(R_NR), row(R_M), row(R_CS), ALU.mult))
                chain(dve.tensor_tensor(row(R_NR), row(R_NR), row(R_C1), ALU.add))
                chain(dve.tensor_tensor(two(R_T, NST), lre, lre, ALU.mult))
                chain(dve.tensor_tensor(two(R_T2, NST), lim, lim, ALU.mult))
                chain(dve.tensor_tensor(row(R_T), row(R_T), row(R_T2), ALU.add))
                chain(dve.reciprocal(row(R_T), row(R_T)))
                chain(dve.tensor_tensor(two(R_CR, NST), two(R_NR, NST), lre, ALU.mult))
                chain(dve.tensor_tensor(two(R_T2, NST), two(R_AI, NST), lim, ALU.mult))
                chain(dve.tensor_tensor(row(R_CR), row(R_CR), row(R_T2), ALU.add))
                chain(dve.tensor_tensor(row(R_CR), row(R_CR), row(R_T), ALU.mult))
                chain(dve.tensor_tensor(two(R_CI, NST), two(R_AI, NST), lre, ALU.mult))
                chain(dve.tensor_tensor(two(R_T2, NST), two(R_NR, NST), lim, ALU.mult))
                chain(dve.tensor_tensor(row(R_CI), row(R_CI), row(R_T2), ALU.subtract))
                chain(dve.tensor_tensor(row(R_CI), row(R_CI), row(R_T), ALU.mult))
                dve.wait_ge(const_ready, 14)
                dve.wait_ge(small_loaded, 48)
                dve.wait_ge(router_hi_ready, 1)
                chain(dve.tensor_tensor(router_lo, router[:, :, :], router_hi.bitcast(F32), ALU.subtract))

            for l in range(DEPTH):
                split(l, 2)
                if l == 0:
                    for t in x_loaded:
                        dve.wait_ge(t, 16)
                norm(("norm1", l), 2 * l, lambda k: sm("g_mix", l, k))
                if l == 0:
                    more_constants()

                dve.wait_ge(layer_loaded, 32 * (l + 1))
                br, bi = (mat(k, 256).rearrange("p (s h) -> p s h", h=HG) for k in ("b_re", "b_im"))
                cr, ci = (bc(cst(r, l), [P, NST, HG]) for r in (R_CR, R_CI))
                chain(dve.memset(bbar[:, :, :, :], 0.0))
                t = [accf[:, 256 * i:256 * i + 256].rearrange("p (s h) -> p s h", h=HG) for i in range(4)]
                chain(dve.tensor_tensor(t[0], br, cr, ALU.mult))
                chain(dve.tensor_tensor(t[1], bi, ci, ALU.mult))
                chain(dve.tensor_tensor(t[2], br, ci, ALU.mult))
                chain(dve.tensor_tensor(t[3], bi, cr, ALU.mult))
                for c, op in ((0, ALU.subtract), (1, ALU.add)):
                    for g in range(2):
                        rng = slice(64 * g, 64 * g + 64)
                        dve.tensor_tensor(bbar[rng, c, :, HG * g:HG * g + HG], t[2 * c][rng], t[2 * c + 1][rng], op)\
                            .then_inc(bbar_ready, 1)
                dve.wait_ge(bbar_ready, 4 * (l + 1))

                split(l, 4)
                h0r, h0i = (mat(k, 128).rearrange("p (s b) -> p s b", b=NSEQ) for k in ("h0_re", "h0_im"))
                ar, ai = (bc(cst(r, l), [P, NST, NSEQ]) for r in (R_AR, R_AI))
                chain(dve.tensor_tensor(ah0[:, 0], h0r, ar, ALU.mult))
                chain(dve.tensor_tensor(ah_t[:, :, :], h0i, ai, ALU.mult))
                chain(dve.tensor_tensor(ah0[:, 0], ah0[:, 0], ah_t[:, :, :], ALU.subtract))
                chain(dve.tensor_tensor(ah0[:, 1], h0r, ai, ALU.mult))
                chain(dve.tensor_tensor(ah_t[:, :, :], h0i, ar, ALU.mult))
                chain(dve.tensor_tensor(ah0[:, 1], ah0[:, 1], ah_t[:, :, :], ALU.add))

                split(l, 5)
                powers(dve, chain, l, 0, E_DVE, accf, lambda w: split(l, {4: 5, 8: 5, 16: 6, 32: 6, 64: 7, 128: 8, 256: 9}[w]))

                seg = xbuf[:, :, 3 + SEQ:].rearrange("p k (b s) -> p k b s", s=SEG)
                cv = mat("conv", 96).rearrange("p (k b w) -> p k b w", k=KB, w=3)
                if l:
                    dve.wait_ge(stored, 48 * l)
                chain(dve.memset(xbuf[:, :, 0:CONVW - 1], 0.0))
                for k in range(KB):
                    chain(dve.tensor_copy(seg[:, k, :, 0:3], cv[:, k]))
                dve.sem_inc(pads_ready, 1)

                split(l, 10)
                dve.wait_ge(a_free, A.of[("va", l, 1, 2)][1] + 1)
                for b, w in enumerate((P, P, P)):
                    chain(dve.bn_stats(bnst[0:w, b], v_tok[0:w, b]))
                    if b < 2:
                        chain(dve.bn_aggr(mv[0:w, b], bnst[0:w, b]))
                    else:
                        dve.bn_aggr(mv[0:w, b], bnst[0:w, b]).then_inc(var_ready, 1)
                split(l, 12)
                dve.wait_ge(std_ready, l + 1)
                dve.wait_ge(ln_loaded, 32 * (l + 1))
                chain(dve.reciprocal(lnr[:, :], lnr[:, :]))
                for b, w in enumerate((P, P, P)):
                    vt = v_tok[0:w, b]
                    chain(dve.tensor_scalar(vt, vt, mv[0:w, b, 0:1], lnr[0:w, b:b + 1], ALU.subtract, ALU.mult))
                    chain(dve.tensor_tensor(vt, vt, ln_rows[0:w, 0], ALU.mult))
                    if b < 2:
                        chain(dve.tensor_tensor(vt, vt, ln_rows[0:w, 1], ALU.add))
                    else:
                        dve.tensor_tensor(vt, vt, ln_rows[0:w, 1], ALU.add).then_inc(v_ready, 1)
                dve.wait_ge(v_ready, l + 1)

                def s5(s, between=None):
                    q = l * NST + s
                    v, d = s5_bank[:, :, 0:T], z[:, q % 2]

                    if q >= 2:
                        dve.wait_ge(rot_ready, q - 1)
                    if s == E_DVE:
                        dve.wait_ge(powers_ready, l + 1)
                    dve.wait_ge(s5_full, q + 1)
                    for c, out in enumerate((d, rot_v[:, :, :])):
                        for i, ((o, e), (a, _)) in enumerate(zip(with_e(out, c, s), with_e(v, c, s))):
                            mult = dve.tensor_tensor(o, a, e, ALU.mult)
                            if c and i:
                                mult.then_inc(s5_free, 1)
                            else:
                                mult.then_inc(dve_done, 1)
                                n[0] += 1
                    if between:
                        between()
                    dve.wait_ge(dve_done, n[0])
                    dve.wait_ge(s5_free, q + 1)
                    dve.tensor_tensor(d[:, 0], d[:, 0], rot_v[:, 1], ALU.add).then_inc(dve_done, 1)
                    n[0] += 1
                    chain(dve.tensor_tensor(d[:, 1], d[:, 1], rot_v[:, 0], ALU.subtract))
                    chain(dve.tensor_tensor(d[:, :, SEQ::TS], d[:, :, SEQ::TS], ah0[:, :, s], ALU.add))
                    dve.wait_ge(decay_ready, q + 1)
                    for c in range(2):
                        dve.tensor_tensor_scan(d[:, c], decay[:, q % 2], d[:, c], 0.0, ALU.mult, ALU.add)\
                            .then_inc(scan_ready, 1)

                def conv():
                    for k in range(KB):
                        w = lambda i: sm("conv_w", l, 4 * i + k)
                        p_out = xc[:, k, 0:SEQ]
                        s_out = xc[:, k, SEQ:T].rearrange("p (b s) -> p b s", s=TS)
                        dve.wait_ge(tap_ready, KB * l + k + 1)
                        for i in range(1, CONVW):
                            dve.scalar_tensor_tensor(p_out, xbuf[:, k, i:i + SEQ], w(i), p_out, ALU.mult, ALU.add)\
                                .then_inc(dve_done, 1)
                            n[0] += 1
                            chain(dve.scalar_tensor_tensor(s_out, seg[:, k, :, i:i + TS], w(i), s_out, ALU.mult, ALU.add))
                        if k == 1:
                            split(l, 15)
                    dve.sem_inc(xc_ready, 1)

                def mixed():
                    for h in range(H_A):
                        b, q, _ = V.of[("mixed", l, h)]
                        src = v_bank[b]
                        dve.wait_ge(v_full, q + 1)
                        bs = bs_row[:, P * h:P * h + P]
                        chain(dve.tensor_tensor(tmp[:, 0:SEQ].rearrange("p (c t) -> p c t", c=2),
                                                src[:, 0:SEQ].rearrange("p (c t) -> p c t", c=2),
                                                bs.unsqueeze(1).to_broadcast([P, 2, P]), ALU.add))
                        dve.tensor_tensor(tmp[:, SEQ:T].rearrange("p (b t) -> p b t", t=TS),
                                          src[:, SEQ:T].rearrange("p (b t) -> p b t", t=TS),
                                          bs[:, 0:TS].unsqueeze(1).to_broadcast([P, NSEQ, TS]), ALU.add).then_inc(v_free, 1)
                        dve.wait_ge(v_free, q + 1)
                        dve.wait_ge(a_free, A.of[("ua", l, h)][1] + 1)
                        chain(dve.tensor_tensor(ug[:, h], tmp[:, :], ug[:, h], ALU.mult))
                    dve.sem_inc(ya_ready, 1)

                def lru():
                    dve.scalar_tensor_tensor(lru_i, lru_i, 1.0, xc, ALU.add, ALU.mult).then_inc(xc_used, 1)
                    dve.wait_ge(xc_used, l + 1)
                    dve.wait_ge(tanh_ready, 4 * (l + 1))
                    dve.wait_ge(dec_root, l + 1)
                    chain(dve.scalar_tensor_tensor(lru_d, lru_a, 1.0, lru_d, ALU.add, ALU.mult))
                    chain(dve.scalar_tensor_tensor(lru_i, lru_i, 0.5, lru_d, ALU.mult, ALU.mult))
                    a0, d0 = lru_a[:, :, SEQ::TS], lru_i[:, :, SEQ::TS]
                    t = ah_t[:, 0:KB, :]
                    chain(dve.tensor_tensor(t, a0, sm("lru_h0", l, 0, 32).rearrange("p (k b) -> p k b", b=NSEQ), ALU.mult))
                    chain(dve.tensor_tensor(d0, d0, t, ALU.add))
                    chain(dve.memset(a0, 0.0))
                    for k in range(KB):
                        chain(dve.tensor_tensor_scan(lru_d[:, k], lru_a[:, k], lru_i[:, k], 0.0, ALU.mult, ALU.add))
                    dve.tensor_copy(lru_last[:, :, :], lru_d[:, :, SEQ - 1::TS]).then_inc(lru_ready, 1)

                def branch(k, m):
                    b, q, _ = V.of[("branch", l, k, m)]
                    src = v_bank[b][:, 0:T]
                    g = th[:, ((l * 3 + k) * 8 + m) % 2]
                    dve.wait_ge(v_full, q + 1)
                    dve.wait_ge(a_free, A.of[("gate", l, k, m)][1] + 1)
                    dst = acc[:, m] if k == 0 else tmp[:, :]
                    dve.scalar_tensor_tensor(dst, g, 1.0, src, ALU.add, ALU.mult).then_inc(v_free, 1)
                    dve.wait_ge(v_free, q + 1)
                    if k == 1:
                        chain(dve.tensor_tensor(acc[:, m], acc[:, m], tmp[:, :], ALU.add))
                    if k == 2:
                        dve.scalar_tensor_tensor(acc[:, m], tmp[:, :], 0.5, acc[:, m], ALU.mult, ALU.add).then_inc(acc_ready, 1)
                        dve.wait_ge(acc_ready, KD * l + m + 1)

                def y_low(y, hi, lo, n):
                    dve.wait_ge(y_hi_ready, 6 * l + n)
                    dve.tensor_tensor(lo, y, hi.bitcast(F32), ALU.subtract).then_inc(y_lo_ready, 1)

                def acc_low(m):
                    dve.wait_ge(acc_hi_ready, KD * l + m + 1)
                    dve.tensor_tensor(acc_lo[:, m], acc[:, m], acc_hi[:, m].bitcast(F32), ALU.subtract).then_inc(acc_lo_ready, 1)

                def ys(ct):
                    dve.wait_ge(y_full, l * NST + 4 * ct + 4)
                    dve.scalar_tensor_tensor(zc[:, ct], uc[:, ct], sm("c_d", l, ct), y_bank[:, 0:T], ALU.mult, ALU.add)\
                        .then_inc(ys_ready, 1)

                for s in range(SLOT_N):
                    split(l, 14 + s if s < 8 else upto((s - 8) // 8, s % 8))
                    tile = s - S5_AT
                    if tile >= 6 and (tile - 6) % 4 == 0:
                        if tile == 6:
                            dve.wait_ge(va_stored, 16 * (l + 1))
                        ys((tile - 6) // 4)
                    if s == 4:
                        mixed()
                    if s == 8:
                        dve.wait_ge(lru_ready, l + 1)
                        dve.wait_ge(a_free, A.of[("gb", l, 3)][1] + 1)
                        dve.tensor_tensor(gbg, gbg, lru_d, ALU.mult).then_inc(yb_ready, 1)
                        dve.wait_ge(yb_ready, l + 1)
                    if s == 10:
                        y_low(gbg, yb_hi[:, :, :], yb_lo[:, :, :], 2)
                    if s >= 8:
                        branch((s - 8) // 8, s % 8)
                    if s == 7:
                        y_low(ug, ya_hi[:, :, :], ya_lo[:, :, :], 1)
                    if 0 <= tile < NST:
                        ahead = s > 8 and s % 2 and s < SLOT_N - 1
                        s5(tile, (lambda: split(l, upto((s - 8) // 8, s % 8) + 1)) if ahead else None)
                    if s == 0:
                        dve.wait_ge(a_free, A.of[("xb", l, 3)][1] + 1)
                        conv()
                    if s == 5:
                        lru()
                dve.wait_ge(a_free, A.of[("glu", l, 3)][1] + 1)
                for m in range(KB):
                    dve.scalar_tensor_tensor(zc[:, m], lru_i[:, m], 1.0, zc[:, m], ALU.add, ALU.mult).then_inc(yc_ready, 1)
                for m in range(KB):
                    y_low(zc[:, m], yc_hi[:, m], yc_lo[:, m], 3 + m)
                for m in range(KD):
                    split(l, upto(2, m))
                    branch(2, m)
                    if m:
                        acc_low(m - 1)
                acc_low(KD - 1)
                split(l, WO + 1)
                for m in range(KD):
                    split(l, WO + 2 + m)
                    b, q, _ = V.of[("wo", l, m)]
                    dve.wait_ge(v_full, q + 1)
                    dve.scalar_tensor_tensor(x[:, m], v_bank[b][:, 0:T], 0.5, x[:, m], ALU.mult, ALU.add).then_inc(v_free, 1)
                    dve.wait_ge(v_free, q + 1)
                    dve.sem_inc(x_ready, 1)
                norm(("norm2", l), 2 * l + 1, lambda k: sm("g_ffn", l, k), None if l else lambda: unit_low(0, 0))
                if l == 0:
                    unit_low(0, 1)
                if l == 1:
                    dve.wait_ge(a_free, A.of[("logits",)][1] + 1)
                    full = [P, 3, NEXP]
                    rix = revidx[:, :].unsqueeze(1).to_broadcast(full)
                    for b in range(3):
                        chain(dve.tensor_tensor(lg[:, b], lg[:, b], rb[:, :], ALU.add))
                    k1, k2, t0, lg2 = rt[:, 0], rt[:, 1], rt[:, 2], rt[:, 3]
                    m1, m2, mx, df, ex, p1, p2 = (rm[:, i] for i in range(7))

                    def best(src, top, pick):
                        chain(dve.tensor_reduce(top, src, AX_X, ALU.max))
                        chain(dve.tensor_tensor(t0, src, bc(top, full), ALU.is_equal))
                        chain(dve.tensor_tensor(t0, t0, rix, ALU.mult))
                        chain(dve.tensor_reduce(mx, t0, AX_X, ALU.max))
                        chain(dve.tensor_tensor(pick, t0, bc(mx, full), ALU.is_equal))

                    best(lg[:, :, :], m1, k1)
                    chain(dve.scalar_tensor_tensor(lg2, k1, -3.0e38, lg[:, :, :], ALU.mult, ALU.add))
                    best(lg2, m2, k2)
                    chosen, key = rt[:, 4], rt[:, 5]
                    chain(dve.tensor_tensor(chosen, k1, k2, ALU.add))
                    dve.memset(chosen[0:64, 2], 0.0).then_inc(chosen_ready, 1)
                    dve.tensor_tensor(df, m2, m1, ALU.subtract).then_inc(diff_ready, 1)
                    low(0, 0)
                    dve.wait_ge(ediff_ready, 1)
                    chain(dve.tensor_scalar(p1, ex, 1.0, None, ALU.add))
                    chain(dve.reciprocal(p1, p1))
                    chain(dve.tensor_tensor(p2, ex, p1, ALU.mult))
                    chain(dve.tensor_tensor(k1, k1, bc(p1, full), ALU.mult))
                    chain(dve.tensor_tensor(k2, k2, bc(p2, full), ALU.mult))
                    dve.tensor_tensor(k1, k1, k2, ALU.add).then_inc(comb_ready, 1)
                    dve.wait_ge(small_full, 1)
                    places = small_bank[0][:, 0:3 * NEXP].rearrange("p (b e) -> p b e", e=NEXP)
                    dve.wait_ge(chosen_ready, 1)
                    chain(dve.scalar_tensor_tensor(key, places, 1.0, chosen, ALU.add, ALU.mult))
                    chain(dve.tensor_scalar(key, key, -1.0, None, ALU.add))
                    chain(dve.tensor_reduce(rm[:, 7, 0:1], small_bank[0][:, 3 * NEXP:4 * NEXP], AX_X, ALU.max))
                    dve.tensor_copy(busiest[:, :], rm[:, 7, 0:1]).then_inc(busiest_ready, 1)
                    dve.tensor_copy(slot_no[:, :], small_bank[0][:, 4 * NEXP:4 * NEXP + SLOTS]).then_inc(small_free, 1)
                    dve.wait_ge(small_free, 1)
                    dve.wait_ge(comb_hi_ready, 1)
                    low(0, 1)
                    chain(dve.tensor_tensor(comb_lo[:, :, :], k1, comb_hi[:, :, :].bitcast(F32), ALU.subtract))
                    continue
                ab, vb, s0 = A.of[("unit", l)], V.of[("unit", l)], plan.split[("unit", l)]
                hb = 0
                for u in range(N_UNITS):
                    def usplit(g):
                        unit_low(u + g // UNIT_G, g % UNIT_G)

                    def hid_low(f):
                        dve.wait_ge(hid_hi_ready, hb + f + 1 + FT * u)
                        dve.wait_ge(v_free, vb + f + 1 + UNIT_V * u)
                        dve.tensor_tensor(hid_lo[:, f], silu[:, f % 3], hid_hi[:, f].bitcast(F32), ALU.subtract)\
                            .then_inc(hid_lo_ready, 1)

                    for g in range(UNIT_G):
                        usplit(g + 2)
                        if g < 2 * FT and g % 2:
                            f = g // 2
                            dve.wait_ge(a_free, ab + f + 1 + UNIT_A * u)
                            dve.wait_ge(v_full, vb + f + 1 + UNIT_V * u)
                            dve.tensor_tensor(silu[:, f % 3], silu[:, f % 3], v_bank[f % 2][:, 0:T], ALU.mult).then_inc(v_free, 1)
                            if f:
                                hid_low(f - 1)
                            if f == FT - 1:
                                hid_low(f)
                        if g >= 2 * FT:
                            m = g - 2 * FT
                            q = FT + m
                            dve.wait_ge(v_full, vb + q + 1 + UNIT_V * u)
                            dve.tensor_tensor(x[:, m], v_bank[q % 2][:, 0:T], x[:, m], ALU.add).then_inc(v_free, 1)
                            dve.wait_ge(v_free, vb + q + 1 + UNIT_V * u)
                for m in range(KD):
                    dve.sem_inc(x_ready, 1)

            def tokens_low(no, src, r, i, h):
                dve.wait_ge(x_hi_ready, 1 + i + 2 * NEXP * r)
                dve.wait_ge(small_full, no + 1)
                k = slice(4 * h, 4 * h + 4)
                dve.tensor_tensor(x_lo[:, k].rearrange("p k n -> p (k n)"), src[:, 0:4 * SLOTS],
                                  x_hi[:, k].rearrange("p k n -> p (k n)").bitcast(F32), ALU.subtract)\
                    .then_inc(small_free, 1)

            def dispatch(key):
                full = [P, 3, SLOTS]
                dve.tensor_tensor(disp[:, :, :], slot_no[:, :].unsqueeze(1).to_broadcast(full), key.to_broadcast(full),
                                  ALU.is_equal).then_inc(disp_ready, 1)

            def round_(r):
                if not isinstance(r, int):
                    dve.tensor_scalar(rt[:, 5], rt[:, 5], float(-SLOTS), None, ALU.add).then_inc(key_ready, 1)
                    dve.wait_ge(key_ready, r)
                dispatch(rt[:, 5, :, 0:1])
                if not isinstance(r, int):
                    low(NEXP * r, 0)
                    low(NEXP * r, 1)
                for h in range(2):
                    tokens_low(of_round(r, h), small_bank[1 + h], r, h, h)

                def item(u, it, last):
                    def product(b):
                        dve.wait_ge(silu_ready, b + 1 + 4 * it)
                        dve.wait_ge(v_full, wide(it, 2 * b + 1))
                        h = hid[:, BLK * b:BLK * b + BLK]
                        dve.tensor_tensor(h, wide_bank[(2 * b + 1) % 4][:, 0:BLK], h, ALU.mult).then_inc(v_free, 1)

                    def small(name):
                        no, src = small_no(r, u, name, last)
                        dve.wait_ge(small_full, no + 1)
                        return no, src

                    def hidden_low(b):
                        _, src = small(f"T{b}")
                        dve.wait_ge(ht_hi_ready, b + 1 + 4 * it)
                        k = slice(BLK_TILES[b][0], BLK_TILES[b][-1] + 1)
                        dve.tensor_tensor(ht_lo[:, k].rearrange("p k n -> p (k n)"), src[:, 0:len(BLK_TILES[b]) * SLOTS],
                                          ht_hi[:, k].rearrange("p k n -> p (k n)").bitcast(F32), ALU.subtract)\
                            .then_inc(small_free, 1)

                    def result_low(q):
                        dve.wait_ge(ym_hi_ready, q + 1 + 4 * it)
                        c = slice(QTR * q, QTR * q + QTR)
                        dve.scalar_tensor_tensor(ym_lo[:, c], wide_bank[q][:, 0:QTR], slot_w[:, 0:1],
                                                 ym_hi[:, c].bitcast(F32), ALU.mult, ALU.subtract).then_inc(v_free, 1)

                    def scattered(m):
                        no, src = small(f"Sc{m}")
                        dve.wait_ge(small_free, no)
                        dve.tensor_tensor(x[:, m], x[:, m], src[:, 0:T], ALU.add).then_inc(small_free, 1)

                    for c in range(N_CHUNK):
                        if c in (2, 4, 6, 8):
                            product(c // 2 - 1)
                        if c == 2:
                            no, src = small("PS")
                            w = src[:, u:u + 1] if last else src[:, bass.ds(u, 1)]
                            dve.tensor_copy(slot_w[:, 0:1], w).then_inc(small_free, 1)
                            dve.wait_ge(small_free, no + 1)
                            _, src = small("S")
                            dve.tensor_copy(scat[:, :], src[:, 0:T]).then_inc(small_free, 1)
                            if not last:
                                dispatch(rt[:, 5, :, bass.ds(u + 1, 1)])
                        if c in (4, 6, 8):
                            hidden_low(c // 2 - 2)
                        if c > 8:
                            result_low(c - 9)
                        if c > 9:
                            scattered(2 * (c - 10))
                            scattered(2 * (c - 10) + 1)
                        if c + 2 < N_CHUNK:
                            low(it, c + 2)
                        elif not last:
                            low(it + 1, c + 2 - N_CHUNK)
                        if c == 8:
                            if not last:
                                tokens_low(*small_no(r, u, "G0"), r, 2 + 2 * u, 0)
                            hidden_low(3)
                    if not last:
                        tokens_low(*small_no(r, u, "G1"), r, 3 + 2 * u, 1)
                    result_low(3)
                    scattered(4)
                    scattered(5)
                    scattered(6)
                    scattered(7)

                items(dve, r, item)
                dve.wait_ge(small_free, of_round(r, ROUND_S))

            rounds(dve, round_)
            for m in range(KD):
                dve.sem_inc(x_ready, 1)
            norm("norm_f", 2 * DEPTH, lambda k: final[:, k:k + 1])

        @block.tensor
        def _(pe):
            def whole(key):
                slot, n, _ = plan.chunks[key]
                pe.wait_ge(landed[slot], n)
                return raw[slot]

            def parts(key):
                g = plan.split[key]
                pe.wait_ge(lo_ready, g + 1)
                return w_hi[g % SPLIT], w_lo[g % SPLIT]

            def a_take(key):
                b, _, need = A.of[key]
                if need:
                    pe.wait_ge(a_free, need)
                return a_bank[b]

            def v_take(key):
                b, _, need = V.of[key]
                if need:
                    pe.wait_ge(v_free, need)
                return v_bank[b]

            def product(out, w, rhs, full):
                for k, (a, b) in enumerate(zip(w, rhs)):
                    mm = pe.matmul(out, a, b, start=(k == 0), stop=(k == len(w) - 1))
                mm.then_inc(full, 1)

            def product3(out, w_h, w_l, x_h, x_l, full=None, start=True, stop=True, ready=None):
                n = len(w_h)
                for k in range(n):
                    if ready:
                        ready(k)
                    pe.matmul(out, w_h[k], x_h[k], start=start and k == 0, stop=False)
                    pe.matmul(out, w_h[k], x_l[k], start=False, stop=False)
                    mm = pe.matmul(out, w_l[k], x_h[k], start=False, stop=stop and k == n - 1)
                if full is not None:
                    mm.then_inc(full, 1)

            hh, hl = [hn_hi[:, k] for k in range(KD)], [hn_lo[:, k] for k in range(KD)]

            def norm(key, r):
                out = a_take(key)[:, 0:T]
                for k in range(KD):
                    pe.wait_ge(sq_ready, 8 * r + k + 1)
                    mm = pe.matmul(out, ones[:, :], squares[r % 2][:, k], start=(k == 0), stop=(k == KD - 1))
                mm.then_inc(a_full, 1)

            def cols(t, k=KD):
                t = t[:, 0:k * P].rearrange("p (k n) -> p k n", k=k)
                return [t[:, i] for i in range(k)]

            def project(key, ready=None):
                w_h, w_l = parts(key)
                product3(a_take(key)[:, 0:T], cols(w_h), cols(w_l), hh, hl, a_full, ready=ready)

            def tiles_of(t, n=KB):
                return [t[:, i] for i in range(n)]

            def step(l, k, m, y_hi, y_lo):
                project(("gate", l, k, m))
                w_h, w_l = (w[:, :].rearrange("p (k n) -> p k n", k=KB) for w in parts(("branch", l, k, m // 2)))
                c = P * (m % 2)
                out = v_take(("branch", l, k, m))[:, 0:T]
                if m == 0:
                    pe.wait_ge(y_lo_ready, 6 * l + (1, 2, 6)[k])
                product3(out, [w_h[:, i, c:c + P] for i in range(KB)], [w_l[:, i, c:c + P] for i in range(KB)],
                         tiles_of(y_hi), tiles_of(y_lo), v_full)

            pe.wait_ge(const_ready, 3)
            for l in range(DEPTH):
                norm(("norm1", l), 2 * l)
                for m in range(KB):
                    project(("uc", l, m), None if m else lambda k: pe.wait_ge(hn_ready, 8 * 2 * l + k + 1))
                pe.wait_ge(bbar_ready, 4 * (l + 1))
                for c in range(2):
                    out = a_take(("bt", l, c))
                    for ct in range(4):
                        mm = pe.transpose(out[:, P * ct:P * ct + P],
                                          bbar[:, c, 4 * ct:4 * ct + 4, :].rearrange("p s h -> p (s h)"), ident[:, :])
                    mm.then_inc(a_full, 1)
                for j in range(2):
                    for i in range(2):
                        w_h, w_l = (w[:, :].rearrange("p (k n) -> p k n", k=4) for w in parts(("va", l, j, i)))
                        for b, t0 in enumerate(TOKS):
                            if i == 0:
                                a_take(("va", l, j, b))
                            out = a_bank[A.of[("va", l, j, b)][0]][:, 0:256]
                            product3(out, [hn_hi[:, 4 * i + k, t0:t0 + P] for k in range(4)],
                                     [hn_lo[:, 4 * i + k, t0:t0 + P] for k in range(4)],
                                     [w_h[:, k] for k in range(4)], [w_l[:, k] for k in range(4)],
                                     a_full if i else half_read if b == 2 else None, start=i == 0, stop=i == 1)
                for m in range(KB):
                    project(("xb", l, m))

                def s5_in(s):
                    q = l * NST + s
                    if q:
                        pe.wait_ge(s5_free, q)
                    if s == 0:
                        pe.wait_ge(a_free, A.of[("bt", l, 1)][1] + 1)
                    j, ct = 32 * (s % 4), s // 4
                    pe.matmul(s5_bank[:, 0, 0:T], bt[j:j + 32, 0, ct], uc[j:j + 32, ct], start=True, stop=True)
                    pe.matmul(s5_bank[:, 1, 0:T], bt[j:j + 32, 1, ct], uc[j:j + 32, ct], start=True, stop=True)\
                        .then_inc(s5_full, 1)

                def s5_out_(s):
                    q = l * NST + s
                    pe.wait_ge(rot_ready, q + 1)
                    j = 32 * (s % 4)
                    if s % 4 == 0 and q:
                        pe.wait_ge(ys_ready, q // 4)
                    if s == 0:
                        pe.wait_ge(layer_prepared, 3 * (l + 1))
                    out = y_bank[j:j + 32, 0:T]
                    pe.matmul(out, mat("c_re", 512)[:, 32 * s:32 * s + 32], xs[:, q % 2, 0], start=True, stop=False)
                    pe.matmul(out, mat("c_im", 512)[:, 32 * s:32 * s + 32], xs[:, q % 2, 1], start=False, stop=True)\
                        .then_inc(y_full, 1)

                for s in range(SLOT_N):
                    if s < 8:
                        project((("ua", "gb")[s // 4], l, s % 4))
                    else:
                        step(l, (s - 8) // 8, s % 8, *((ya_hi, ya_lo) if s < 16 else (yb_hi, yb_lo)))
                    if s == 3:
                        pe.wait_ge(xc_ready, l + 1)
                        for g in range(8):
                            w = mat(("wa", "wx")[g // 4], 512)[:, P * (g % 4):P * (g % 4) + P]
                            product(a_take(("ri", l, g))[:, 0:T], [w], [xc[:, g % 4]], a_full)
                    if s == 4:
                        pe.wait_ge(v_ready, l + 1)
                        pe.wait_ge(layer_prepared, 3 * (l + 1))
                        for h in range(H_A):
                            out = v_take(("mixed", l, h))
                            c = slice(P * h, P * h + P)
                            pe.matmul(out[:, 0:P], v_tok[:, 0, c], mat("ws", 512)[:, c], start=True, stop=True)
                            pe.matmul(out[:, P:SEQ], v_tok[:, 1, c], mat("ws", 512)[:, c], start=True, stop=True)
                            pe.matmul(out[:, SEQ:T], v_tok[64:P, 2, c], mat("ws_s", 256)[64:P, 64 * h:64 * h + 64],
                                      start=True, stop=True).then_inc(v_full, 1)
                    if 0 <= s - S5_AT < NST:
                        s5_in(s - S5_AT)
                    if 0 <= s - S5_AT - 2 < NST:
                        s5_out_(s - S5_AT - 2)
                pe.wait_ge(z_ready, KB * (l + 1))
                for m in range(KB):
                    w = whole(("glu", l, m // 2))[:, :].rearrange("p (k n) -> p k n", k=KB)
                    c = P * (m % 2)
                    product(a_take(("glu", l, m))[:, 0:T], [w[:, k, c:c + P] for k in range(KB)],
                            [zc[:, k] for k in range(KB)], a_full)
                for m in range(KD):
                    step(l, 2, m, yc_hi, yc_lo)
                for m in range(KD):
                    w_h, w_l = parts(("wo", l, m))
                    product3(v_take(("wo", l, m))[:, 0:T], cols(w_h), cols(w_l), tiles_of(acc_hi, KD), tiles_of(acc_lo, KD),
                             v_full, ready=None if m else lambda k: pe.wait_ge(acc_lo_ready, KD * l + k + 1))
                norm(("norm2", l), 2 * l + 1)
                if l == 1:
                    pe.wait_ge(router_hi_ready, 2)
                    w_h, w_l = ([router_w[:, NEXP * (i * KD + k):NEXP * (i * KD + k) + P] for k in range(KD)]
                                for i in range(2))
                    product3(a_take(("logits_t",))[:, 0:T], w_h, w_l, hh, hl, a_full,
                             ready=lambda k: pe.wait_ge(hn_ready, 8 * (2 * l + 1) + k + 1))
                    pe.wait_ge(a_free, A.of[("logits_t",)][1] + 1)
                    out = a_take(("logits",))
                    for b, t0 in enumerate(TOKS):
                        mm = pe.matmul(out[:, NEXP * b:NEXP * b + NEXP], tmp[:, t0:t0 + P], ident[:, 0:NEXP],
                                       start=True, stop=True)
                    mm.then_inc(a_full, 1)

                    def places():
                        pe.wait_ge(chosen_ready, 1)
                        pe.wait_ge(before_ready, 1)
                        out = small_bank[0]
                        for b in range(3):
                            o = out[:, NEXP * b:NEXP * b + NEXP]
                            for i in range(b):
                                pe.matmul(o, ones[:, :], rt[:, 4, i], start=i == 0, stop=False)
                            pe.matmul(o, before[:, :], rt[:, 4, b], start=b == 0, stop=True)
                        for b in range(3):
                            pe.matmul(out[:, 3 * NEXP:4 * NEXP], ones[:, :], rt[:, 4, b], start=b == 0, stop=b == 2)
                        pe.matmul(out[:, 4 * NEXP:4 * NEXP + SLOTS], ones[:, :], before[:, :], start=True, stop=True)\
                            .then_inc(small_full, 1)

                    pe.wait_ge(ident_r_ready, 1)
                    for i in range(12):
                        if i == 6:
                            places()
                        h, b = i // 6, i % 3
                        out = a_take(("tok", i))
                        for j in range(4):
                            mm = pe.matmul(out[:, P * j:P * j + P],
                                           (hn_hi, hn_lo)[i % 6 // 3][:, 4 * h + j, TOKS[b]:TOKS[b] + P], ident_r[:, :],
                                           start=True, stop=True)
                        mm.then_inc(a_full, 1)
                    continue
                ab, vb, s0 = A.of[("unit", l)], V.of[("unit", l)], plan.split[("unit", l)]
                hb = 0
                for u in range(N_UNITS):
                    for g in range(UNIT_G):
                        w_h, w_l = uw_hi[g % SPLIT], uw_lo[g % SPLIT]
                        pe.wait_ge(lo_ready, s0 + g + 1 + UNIT_G * u)
                        if g < 2 * FT:
                            f = g // 2
                            if g % 2 == 0:
                                pe.wait_ge(a_free, ab + (f - 2 if f >= 3 else 0) + UNIT_A * u)
                                product3(a_bank[f % 3][:, 0:T], cols(w_h), cols(w_l), hh, hl, a_full,
                                         ready=None if g or u else lambda k: pe.wait_ge(hn_ready, 8 * (2 * l + 1) + k + 1))
                            else:
                                pe.wait_ge(v_free, vb + (f - 1 if f >= 2 else 0) + UNIT_V * u)
                                product3(v_bank[f % 2][:, 0:T], cols(w_h), cols(w_l), hh, hl, v_full)
                            continue
                        q = g - FT
                        pe.wait_ge(v_free, vb + q - 1 + UNIT_V * u)
                        if g == 2 * FT:
                            pe.wait_ge(hid_lo_ready, hb + FT + FT * u)
                        product3(v_bank[q % 2][:, 0:T], cols(w_h, FT), cols(w_l, FT), [hid_hi[:, k] for k in range(FT)],
                                 [hid_lo[:, k] for k in range(FT)], v_full)

            def gather(no, out, h):
                pe.wait_ge(small_free, no - 3)
                for j in range(4):
                    c = slice(P * (4 * h + j), P * (4 * h + j) + P)
                    for i, t in enumerate((tok_hi, tok_lo)):
                        for b in range(3):
                            mm = pe.matmul(out[:, SLOTS * j:SLOTS * j + SLOTS], t[:, b, c], disp[:, b],
                                           start=i == 0 and b == 0, stop=i == 1 and b == 2)
                mm.then_inc(small_full, 1)

            def round_(r):
                pe.wait_ge(disp_ready, 1 + NEXP * r)
                if isinstance(r, int):
                    pe.wait_ge(a_free, A.of[("tok", 11)][1] + 1)
                    pe.wait_ge(small_free, 1)
                gather(4 if isinstance(r, int) else of_round(r, 0), small_bank[1], 0)
                gather(4 if isinstance(r, int) else of_round(r, 1), small_bank[2], 1)
                pe.wait_ge(small_free, of_round(r, 2))
                pe.sem_inc(round_begun, 1)

                def item(u, it, last):
                    def small_take(name):
                        no, out = small_no(r, u, name, last)
                        pe.wait_ge(small_free, no - 2 if name == "PS" else no - 3)
                        return out

                    def projected(c):
                        b, out = c // 2, wide_bank[c % 4][:, 0:BLK]
                        pe.wait_ge(lo_ready, parted(it, c))
                        pe.wait_ge(v_free, up_done(it, b - 2) if b >= 2 else down_done(it - 1, c))
                        w_h, w_l = (w[c % MSPLIT][:, :].rearrange("p (k n) -> p k n", k=KD) for w in (mw_hi, mw_lo))
                        for k0 in (0, 4):
                            ks = range(k0, k0 + 4)
                            product3(out, [x_hi[:, k] for k in ks], [x_lo[:, k] for k in ks], [w_h[:, k] for k in ks],
                                     [w_l[:, k] for k in ks], v_full if k0 else None, start=not k0, stop=bool(k0))

                    def transposed(b):
                        out = small_take(f"T{b}")
                        pe.wait_ge(v_free, up_done(it, b))
                        for j, k in enumerate(BLK_TILES[b]):
                            mm = pe.transpose(out[:, SLOTS * j:SLOTS * j + SLOTS], hid[:, P * k:P * k + P], ident[:, :])
                        mm.then_inc(small_full, 1)

                    def down(q):
                        pe.wait_ge(lo_ready, parted(it, 8 + q))
                        pe.wait_ge(v_free, up_done(it, 2 + q // 2))
                        w_h, w_l = (w[(8 + q) % MSPLIT][:, :].rearrange("p (k n) -> p k n", k=FT) for w in (mw_hi, mw_lo))
                        last_tiles = BLK_TILES[3][0]
                        for k0, k1 in ((0, last_tiles), (last_tiles, FT)):
                            if q == 0:
                                pe.wait_ge(small_free, small_no(r, u, "T3" if k0 else "T2", last)[0] + 1)
                            ks = range(k0, k1)
                            product3(wide_bank[q][:, 0:QTR], [ht_hi[:, k] for k in ks], [ht_lo[:, k] for k in ks],
                                     [w_h[:, k] for k in ks], [w_l[:, k] for k in ks], v_full if k0 else None,
                                     start=not k0, stop=bool(k0))

                    def scatter(q):
                        pe.wait_ge(v_free, down_done(it, q))
                        for m in (2 * q, 2 * q + 1):
                            out = small_take(f"Sc{m}")[:, 0:T]
                            pe.matmul(out, ym_hi[:, P * m:P * m + P], scat[:, :], start=True, stop=False)
                            pe.matmul(out, ym_lo[:, P * m:P * m + P], scat[:, :], start=False, stop=True)\
                                .then_inc(small_full, 1)

                    for b in range(4):
                        projected(2 * b)
                        projected(2 * b + 1)
                        if b:
                            transposed(b - 1)
                            continue
                        out = small_take("PS")
                        for i, t in enumerate((comb_hi, comb_lo)):
                            for b in range(3):
                                mm = pe.matmul(out[:, 0:NEXP], disp[:, b], t[:, b], start=i == 0 and b == 0,
                                               stop=i == 1 and b == 2)
                        mm.then_inc(small_full, 1)
                        out = small_take("S")
                        for b, p0 in enumerate((0, 0, 64)):
                            mm = pe.matmul(out[:, TOKS[b] + p0:TOKS[b] + P], disp[:, b], ident_r[:, p0:P],
                                           start=True, stop=True)
                        mm.then_inc(small_full, 1)
                    if not last:
                        pe.wait_ge(disp_ready, it + 2)
                        gather(*small_no(r, u, "G0"), 0)
                    transposed(3)
                    down(0)
                    down(1)
                    scatter(0)
                    down(2)
                    scatter(1)
                    if not last:
                        gather(*small_no(r, u, "G1"), 1)
                    down(3)
                    scatter(2)
                    scatter(3)

                items(pe, r, item)

            rounds(pe, round_)
            norm("norm_f", 2 * DEPTH)


def kernel(x_prompt, x_sample, state_conv_b, state_lru_b, state_s5_re, state_s5_im, norm_mix_g, w_in, b_gate,
           a_ln_g, a_ln_b, a_ws, a_bs, b_conv_w, b_conv_b, b_wa, b_ba, b_wx, b_bx, b_lam, c_lam_re, c_lam_im,
           c_log_dt, c_b_re, c_b_im, c_c_re, c_c_im, c_d, c_glu_w, c_glu_b, w_branch, w_out, norm_ffn_g,
           ffn_w_gate, ffn_w_up, ffn_w_down, moe_router_w, moe_router_b, moe_w_gate, moe_w_up, moe_w_down,
           final_norm_g):
    import numpy as np
    import concourse.bacc as bacc
    from concourse.bass_utils import run_bass_kernel_spmd

    def host(a):
        return np.ascontiguousarray(a)

    L = DEPTH

    def vec(a):
        return host(a).reshape(L, -1, P).transpose(2, 0, 1)

    def state(a):
        a = host(a)
        a = a.reshape((L, NST, P) + a.shape[3:])
        return a.transpose((2, 0, 1) + tuple(range(3, a.ndim)))

    x = np.concatenate([host(x_prompt)[0], host(x_sample).reshape(-1, D)])
    arrays = {"x": x.T.reshape(KD, P, T).transpose(1, 0, 2)}
    log_dt = np.broadcast_to(host(c_log_dt)[:, :, None], (L, 32, 64))
    parts = {
        "g_mix": vec(norm_mix_g), "g_ffn": vec(norm_ffn_g), "b_gate": vec(b_gate),
        "conv_w": vec(host(b_conv_w).reshape(L, -1)), "conv_b": vec(b_conv_b), "ba": vec(b_ba), "bx": vec(b_bx),
        "lam": vec(b_lam), "c_d": vec(c_d), "glu_b": vec(c_glu_b), "lam_re": state(c_lam_re),
        "lam_im": state(c_lam_im), "log_dt": state(log_dt),
        "lru_h0": host(state_lru_b).reshape(L, NSEQ, KB, P).transpose(3, 0, 2, 1).reshape(P, L, -1)}
    arrays["small"] = np.concatenate([parts[k] for k in SM], axis=2)
    arrays["final"] = host(final_norm_g).reshape(KD, P).T
    arrays["router"] = host(moe_router_w)[0].reshape(KD, P, NEXP).transpose(1, 0, 2)
    arrays["rb"] = host(moe_router_b)

    f = np.float32
    cblk = {k: np.zeros((P, L, NST, 2, HG), f) for k in ("c_re", "c_im")}
    for k, a in (("c_re", c_c_re), ("c_im", c_c_im)):
        a = host(a).reshape(L, NST, 2, HG, 64)
        for g in range(2):
            cblk[k][64 * g:64 * g + 64, :, :, g] = a[:, :, g].transpose(3, 0, 1, 2)
    wblk = {k: np.zeros((P, L, KB, P), f) for k in ("wa", "wx")}
    for k, a in (("wa", b_wa), ("wx", b_wx)):
        a = host(a).reshape(L, KB, 2, 64, 64)
        for g in range(2):
            wblk[k][64 * g:64 * g + 64, :, :, 64 * g:64 * g + 64] = a[:, :, g].transpose(2, 0, 1, 3)
    wst = host(a_ws).transpose(3, 0, 1, 2)
    wss = np.zeros((P, L, H_A, NSEQ, TS), f)
    for b in range(NSEQ):
        wss[64 + TS * b:64 + TS * b + TS, :, :, b] = wst[0:TS, :, :, 0:TS]
    mats = {
        "b_re": state(c_b_re), "b_im": state(c_b_im), **cblk, "ws": wst, "ws_s": wss, **wblk,
        "h0_re": state(host(state_s5_re).transpose(0, 2, 3, 1)), "h0_im": state(host(state_s5_im).transpose(0, 2, 3, 1)),
        "conv": host(state_conv_b).reshape(L, NSEQ, 3, KB, P).transpose(4, 0, 3, 1, 2)}
    arrays["pl"] = np.concatenate([host(mats[k]).reshape(P, L, -1) for k in PL], axis=2).transpose(1, 0, 2)
    arrays["rows"] = np.stack([host(a_ln_g), host(a_ln_b), host(a_bs).reshape(L, -1)], axis=1)

    def chunks(w, width):
        w = host(w)
        return w.reshape(w.shape[0], -1, P, w.shape[2] // width, width).transpose(0, 3, 2, 1, 4)

    win, wva = chunks(w_in, P), chunks(host(w_in)[:, :, DB:D], 256)
    order = list(range(16, 20)) + [0, 1, 2, 3] + list(range(8, 12)) + list(range(0, 4)) + list(range(12, 16)) \
        + list(range(20, 44))
    arrays["w_in"] = win[:, order].reshape(L, 44, P, CHUNK)
    arrays["w_in"][:, 4:8] = wva.reshape(L, 2, P, 2, CHUNK).transpose(0, 1, 3, 2, 4).reshape(L, 4, P, CHUNK)
    br = host(w_branch)
    arrays["w_br"] = br.reshape(L, 3, KB, P, 4, 256).transpose(0, 1, 4, 3, 2, 5)
    arrays["w_glu"] = chunks(c_glu_w, 256)
    arrays["w_wo"] = chunks(w_out, P)

    def cols(w):
        return w.reshape(-1, KD, P, FT, P).transpose(3, 0, 2, 1, 4)[:, None]

    def dense(w):
        return host(w)[0].reshape(D, 2, FT * P).transpose(1, 0, 2)

    arrays["w_gu"] = np.concatenate([cols(dense(ffn_w_gate)), cols(dense(ffn_w_up))], axis=1)
    arrays["w_dn"] = host(ffn_w_down).reshape(2, FT, P, KD, P).transpose(3, 0, 2, 1, 4)

    def blocks(w, width):
        w = host(w)[0]
        return w.reshape(NEXP, -1, P, 4, width).transpose(3, 0, 2, 1, 4).reshape(4, NEXP, P, MCHUNK)

    gate_up = np.stack([blocks(moe_w_gate, BLK), blocks(moe_w_up, BLK)], axis=1)
    arrays["w_moe"] = np.concatenate([gate_up.reshape(8, NEXP, P, MCHUNK), blocks(moe_w_down, QTR)])

    shapes = {"x": (P, KD, T), "small": (P, L, NSM), "final": (P, KD), "router": (P, KD, NEXP), "rb": (1, NEXP),
              "pl": (L, P, NPL), "rows": (L, 3, DB), "w_in": (L, 44, P, CHUNK), "w_br": (L, 12, P, CHUNK),
              "w_glu": (L, 2, P, CHUNK), "w_wo": (L, KD, P, CHUNK), "w_gu": (2 * FT, N_UNITS, P, KD * P),
              "w_dn": (KD, N_UNITS, P, UCHUNK), "w_moe": (N_CHUNK, NEXP, P, MCHUNK)}
    outs = {"y": (P, KD * T), "va": (L, 64, DB), "conv": (L, P, KB * NLAST * 3), "lru": (L, P, KB * NLAST),
            "s5": (L, P, 2 * NST * NLAST)}
    nc = bacc.Bacc("TRN2", target_bir_lowering=False, num_devices=1)
    feed, args = {}, []
    for name, shape in shapes.items():
        feed[f"{name}_in"] = host(arrays[name]).reshape(shape)
        args.append(nc.dram_tensor(f"{name}_in", shape, F32, kind="ExternalInput").ap())
    for name, shape in outs.items():
        args.append(nc.dram_tensor(f"{name}_out", shape, F32, kind="ExternalOutput").ap())
    build(nc, *args)
    got = run_bass_kernel_spmd(nc, [feed], core_ids=[0]).results[0]

    y = got["y_out"].reshape(P, KD, T).transpose(2, 1, 0).reshape(T, D)
    va = got["va_out"].reshape(L, NSEQ, TS, DB)
    conv = got["conv_out"].reshape(L, P, KB, NLAST, 3).transpose(0, 3, 4, 2, 1).reshape(L, NLAST, 3, DB)
    lru = got["lru_out"].reshape(L, P, KB, NLAST).transpose(0, 3, 2, 1).reshape(L, NLAST, DB)
    s5 = got["s5_out"].reshape(L, P, 2, NST, NLAST).transpose(2, 0, 4, 3, 1).reshape(2, L, NLAST, 32, 64)
    return (host(y[None, 0:SEQ]), host(y[SEQ:].reshape(NSEQ, TS, D)), host(conv[:, 0:1]), host(lru[:, 0:1]),
            host(s5[0][:, 0:1]), host(s5[1][:, 0:1]), host(va), host(conv[:, 1:]), host(lru[:, 1:]),
            host(s5[0][:, 1:]), host(s5[1][:, 1:]))
```
